# Optimizing a Trainium2 kernel written in Bass

```python
import math
import jax, jax.numpy as jnp
from jax import lax
import numpy as np

D_MODEL = 1024
BATCH = 1
SEQ = 256
DEPTH = 2

N_META = 16
BLOCK_Q = 128
ROPE_THETA = 10000.0
RMS_EPS = 1e-6
DA_HEADS = 8
DA_HEAD_DIM = 64
DSA_HEADS = 16
DSA_HEAD_DIM = 64
IDX_HEADS = 8
IDX_DIM = 64
TOPK_MAX = 256
DSA_QKV = DSA_HEADS * DSA_HEAD_DIM
DSA_SPLITS = [DSA_QKV, 2 * DSA_QKV, 3 * DSA_QKV,
              3 * DSA_QKV + IDX_HEADS * IDX_DIM,
              3 * DSA_QKV + IDX_HEADS * IDX_DIM + IDX_DIM]
DSA_IN_WIDTH = DSA_SPLITS[-1] + IDX_HEADS
ROPE_DIM = 64
BIG_SCORE = 1e30
FFN_HIDDEN = 2816
CONV_WIDTH = 3


def rms_norm(x, g):
    xf = x.astype(jnp.float32)
    y = xf * lax.rsqrt(jnp.mean(xf * xf, axis=-1, keepdims=True) + RMS_EPS)
    return (y * g.astype(jnp.float32)).astype(x.dtype)

def rope_tables(T, dim):
    inv = ROPE_THETA ** (-jnp.arange(0, dim, 2, dtype=jnp.float32) / dim)
    ang = jnp.arange(T, dtype=jnp.float32)[:, None] * inv[None, :]
    return jnp.cos(ang), jnp.sin(ang)

def apply_rope(x, cos, sin):
    shape = (1, cos.shape[0]) + (1,) * (x.ndim - 3) + (cos.shape[1],)
    c = cos.reshape(shape)
    s = sin.reshape(shape)
    x1, x2 = jnp.split(x.astype(jnp.float32), 2, axis=-1)
    return jnp.concatenate([x1 * c - x2 * s, x2 * c + x1 * s], axis=-1).astype(x.dtype)

def sweep_blocks(fn, T):
    out = lax.map(fn, jnp.arange(T // BLOCK_Q) * BLOCK_Q)
    out = jnp.moveaxis(out, 0, 1)
    return out.reshape((out.shape[0], T) + out.shape[3:])

def diff_attention(h, w_qkv, lq1, lk1, lq2, lk2, subln, w_o, cos, sin, lambda_init):
    B, T, _ = h.shape
    q, k, v = jnp.split(h @ w_qkv, 3, axis=-1)
    q = apply_rope(q.reshape(B, T, DA_HEADS, 2, DA_HEAD_DIM), cos, sin) * (DA_HEAD_DIM ** -0.5)
    k = apply_rope(k.reshape(B, T, DA_HEADS, 2, DA_HEAD_DIM), cos, sin)
    v = v.reshape(B, T, DA_HEADS, 2 * DA_HEAD_DIM)
    f32 = jnp.float32
    lam = (jnp.exp(jnp.sum(lq1.astype(f32) * lk1.astype(f32)))
           - jnp.exp(jnp.sum(lq2.astype(f32) * lk2.astype(f32))) + lambda_init)
    k_pos = jnp.arange(T)

    def block(start):
        q_pos = start + jnp.arange(BLOCK_Q)
        qb = lax.dynamic_slice_in_dim(q, start, BLOCK_Q, axis=1)
        s = jnp.einsum('bqhcd,bkhcd->bhcqk', qb, k).astype(f32)
        s = jnp.where(k_pos[None, :] <= q_pos[:, None], s, -jnp.inf)
        p = jax.nn.softmax(s, axis=-1)
        a = p[:, :, 0] - lam * p[:, :, 1]
        return jnp.einsum('bhqk,bkhe->bqhe', a.astype(v.dtype), v)

    o = sweep_blocks(block, T)
    o = rms_norm(o, subln) * (1.0 - lambda_init)
    return o.reshape(B, T, DA_HEADS * 2 * DA_HEAD_DIM) @ w_o

def dsa_attention(h, w_in, idx_k_norm, w_o, cos, sin, n_keys):
    B, T, _ = h.shape
    q, k, v, qi, ki, wi = jnp.split(h @ w_in, DSA_SPLITS, axis=-1)
    q = apply_rope(q.reshape(B, T, DSA_HEADS, DSA_HEAD_DIM), cos, sin) * (DSA_HEAD_DIM ** -0.5)
    k = apply_rope(k.reshape(B, T, DSA_HEADS, DSA_HEAD_DIM), cos, sin)
    v = v.reshape(B, T, DSA_HEADS, DSA_HEAD_DIM)
    qi = apply_rope(qi.reshape(B, T, IDX_HEADS, IDX_DIM), cos, sin)
    ki = apply_rope(rms_norm(ki, idx_k_norm), cos, sin)
    wi = wi * (IDX_HEADS ** -0.5)
    topk = min(TOPK_MAX, n_keys // 4)
    k_pos = jnp.arange(T)
    f32 = jnp.float32
    gather = jax.vmap(lambda arr, idx: arr[idx])

    def block(start):
        q_pos = start + jnp.arange(BLOCK_Q)
        qb = lax.dynamic_slice_in_dim(q, start, BLOCK_Q, axis=1)
        qib = lax.dynamic_slice_in_dim(qi, start, BLOCK_Q, axis=1)
        wb = lax.dynamic_slice_in_dim(wi, start, BLOCK_Q, axis=1)
        raw = jnp.einsum('bqhd,bkd->bqhk', qib, ki).astype(f32) * (IDX_DIM ** -0.5)
        score = jnp.einsum('bqhk,bqh->bqk', jax.nn.relu(raw), wb.astype(f32))
        causal = k_pos[None, :] <= q_pos[:, None]
        score = jnp.where(causal & (k_pos < N_META)[None, :], BIG_SCORE, score)
        score = jnp.where(causal, score, -jnp.inf)
        top_val, top_idx = lax.top_k(score, topk)
        valid = top_val > -jnp.inf
        ks = gather(k, top_idx)
        vs = gather(v, top_idx)
        s = jnp.einsum('bqhd,bqjhd->bhqj', qb, ks).astype(f32)
        s = jnp.where(valid[:, None], s, -jnp.inf)
        p = jax.nn.softmax(s, axis=-1)
        return jnp.einsum('bhqj,bqjhd->bqhd', p.astype(vs.dtype), vs)

    o = sweep_blocks(block, T)
    return o.reshape(B, T, DSA_QKV) @ w_o

def conv_ffn(h, w_up, conv_w, conv_b, w_down):
    u = h @ w_up
    T = u.shape[1]
    up = jnp.pad(u, ((0, 0), (CONV_WIDTH - 1, 0), (0, 0)))
    c = conv_b + sum(conv_w[j] * up[:, j:j + T] for j in range(CONV_WIDTH))
    g, val = jnp.split(c, 2, axis=-1)
    return (jax.nn.silu(g) * val) @ w_down

def first_inputs(seed: int = 0) -> dict:
    key = jax.random.key(seed)
    ks = iter(jax.random.split(key, 32))
    n_a = (DEPTH + 1) // 2
    n_b = DEPTH // 2
    D, F = D_MODEL, FFN_HIDDEN

    def nrm(shape, scale):
        return jax.random.normal(next(ks), shape, jnp.float32) * scale

    def gain(shape):
        return 1.0 + nrm(shape, 0.02)

    return {
        "x": nrm((BATCH, SEQ, D), 1.0),
        "meta_tokens": nrm((N_META, D), 1.0),
        "da_norm": gain((n_a, D)),
        "da_w_qkv": nrm((n_a, D, 3 * D), D ** -0.5),
        "da_lambda_q1": nrm((n_a, DA_HEAD_DIM), 0.1),
        "da_lambda_k1": nrm((n_a, DA_HEAD_DIM), 0.1),
        "da_lambda_q2": nrm((n_a, DA_HEAD_DIM), 0.1),
        "da_lambda_k2": nrm((n_a, DA_HEAD_DIM), 0.1),
        "da_subln": gain((n_a, 2 * DA_HEAD_DIM)),
        "da_w_o": nrm((n_a, DA_HEADS * 2 * DA_HEAD_DIM, D), D ** -0.5),
        "dsa_norm": gain((n_b, D)),
        "dsa_w_in": nrm((n_b, D, DSA_IN_WIDTH), D ** -0.5),
        "dsa_idx_k_norm": gain((n_b, IDX_DIM)),
        "dsa_w_o": nrm((n_b, DSA_QKV, D), DSA_QKV ** -0.5),
        "ffn_norm": gain((DEPTH, D)),
        "ffn_w_up": nrm((DEPTH, D, 2 * F), D ** -0.5),
        "ffn_conv_w": nrm((DEPTH, CONV_WIDTH, 2 * F), CONV_WIDTH ** -0.5),
        "ffn_conv_b": nrm((DEPTH, 2 * F), 0.02),
        "ffn_w_down": nrm((DEPTH, F, D), F ** -0.5),
        "final_norm": gain((D,)),
    }

def first_block(x, meta_tokens, da_norm, da_w_qkv, da_lambda_q1, da_lambda_k1,
              da_lambda_q2, da_lambda_k2, da_subln, da_w_o, dsa_norm, dsa_w_in,
              dsa_idx_k_norm, dsa_w_o, ffn_norm, ffn_w_up, ffn_conv_w, ffn_conv_b,
              ffn_w_down, final_norm):
    B, L, D = x.shape
    T = L + N_META
    T_pad = ((T + BLOCK_Q - 1) // BLOCK_Q) * BLOCK_Q
    meta = jnp.broadcast_to(meta_tokens[None].astype(x.dtype), (B, N_META, D))
    h = jnp.concatenate([meta, x], axis=1)
    h = jnp.pad(h, ((0, 0), (0, T_pad - T), (0, 0)))
    cos, sin = rope_tables(T_pad, ROPE_DIM)
    for i in range(DEPTH):
        j = i // 2
        if i % 2 == 0:
            lambda_init = 0.8 - 0.6 * math.exp(-0.3 * i)
            h = h + diff_attention(rms_norm(h, da_norm[j]), da_w_qkv[j],
                                   da_lambda_q1[j], da_lambda_k1[j],
                                   da_lambda_q2[j], da_lambda_k2[j],
                                   da_subln[j], da_w_o[j], cos, sin, lambda_init)
        else:
            h = h + dsa_attention(rms_norm(h, dsa_norm[j]), dsa_w_in[j],
                                  dsa_idx_k_norm[j], dsa_w_o[j], cos, sin, L)
        h = h + conv_ffn(rms_norm(h, ffn_norm[i]), ffn_w_up[i], ffn_conv_w[i],
                         ffn_conv_b[i], ffn_w_down[i])
    h = rms_norm(h, final_norm)
    return h[:, N_META:N_META + L]


N_EVEN = (DEPTH + 1) // 2
N_ODD = DEPTH // 2
D_PLE = 256
D_FF = 2816
EPS = 1e-6
N_NORMS = 5
NEG_BIG = -1e30
F_MIN = 1e-6
LB_MAX = 0.999

A_HEADS = 8
A_HEAD_DIM = 64
A_WIDTH = A_HEADS * A_HEAD_DIM
A_CHUNK = 128
B_HEADS = 4
B_KEY_DIM = 128
B_VAL_DIM = 128
B_KW = B_HEADS * B_KEY_DIM
B_VW = B_HEADS * B_VAL_DIM
B_CHUNK = 64
EVEN_IN = 2 * A_WIDTH + 2 * B_KW + 2 * B_VW
EVEN_OUT = A_WIDTH + B_VW
C_HEADS = 8
C_NOPE = 128
C_ROPE = 64
C_V = 128
C_QK = C_NOPE + C_ROPE
Q_LORA = 384
KV_LORA = 256
ODD_IN = Q_LORA + KV_LORA + C_ROPE
ATTN_BLOCK = 128
ATTN_SCALE = C_QK ** -0.5


def rms_norm_2(x, g):
    x32 = x.astype(jnp.float32)
    y = x32 * lax.rsqrt(jnp.mean(x32 * x32, axis=-1, keepdims=True) + EPS)
    return (y * g.astype(jnp.float32)).astype(x.dtype)

def swiglu(h, w_gate, w_up, w_down):
    return (jax.nn.silu(h @ w_gate) * (h @ w_up)) @ w_down

def gmlp_spatial(u, v, v_norm, w_s, b_s):
    bsz, seq = u.shape[:2]
    n_chunks = seq // A_CHUNK
    v = rms_norm_2(v, v_norm)
    vc = v.reshape(bsz, n_chunks, A_CHUNK, A_HEADS, A_HEAD_DIM)
    causal = jnp.tril(jnp.ones((A_CHUNK, A_CHUNK), dtype=bool))
    w = jnp.where(causal[None], w_s, 0.0).astype(vc.dtype)
    mixed = jnp.einsum('hts,bcshd->bcthd', w, vc) + b_s.T[None, None, :, :, None].astype(vc.dtype)
    return u * mixed.reshape(bsz, seq, A_HEADS, A_HEAD_DIM)

def hgrn2_chunkwise(q, log_f, k, v):
    bsz, seq = q.shape[:2]
    n = seq // B_CHUNK

    def to_chunks(t):
        t = t.astype(jnp.float32).reshape(bsz, n, B_CHUNK, B_HEADS, t.shape[-1])
        return jnp.transpose(t, (1, 0, 3, 2, 4))

    qc, kc, vc = to_chunks(q), to_chunks(k), to_chunks(v)
    bc = jnp.cumsum(to_chunks(log_f), axis=3)
    causal = jnp.tril(jnp.ones((B_CHUNK, B_CHUNK), dtype=bool))[:, :, None]

    def step(state, xs):
        q_, k_, v_, b_ = xs
        diff = b_[:, :, :, None, :] - b_[:, :, None, :, :]
        decay = jnp.exp(jnp.where(causal, diff, NEG_BIG))
        scores = jnp.einsum('bhtd,bhtsd->bhts', q_, decay * k_[:, :, None, :, :])
        o = jnp.einsum('bhts,bhse->bhte', scores, v_)
        o = o + jnp.einsum('bhtd,bhde->bhte', q_ * jnp.exp(b_), state)
        b_last = b_[:, :, -1:, :]
        state = jnp.exp(b_last)[:, :, 0, :, None] * state + jnp.einsum(
            'bhsd,bhse->bhde', k_ * jnp.exp(b_last - b_), v_)
        return state, o

    state0 = jnp.zeros((bsz, B_HEADS, B_KEY_DIM, B_VAL_DIM), jnp.float32)
    _, oc = lax.scan(step, state0, (qc, kc, vc, bc))
    return jnp.transpose(oc, (1, 0, 3, 2, 4)).reshape(bsz, seq, B_HEADS, B_VAL_DIM)

def even_mixer(h, w_in, v_norm, w_s, b_s, lb, out_norm, w_out):
    bsz, seq, _ = h.shape
    z = h @ w_in
    a_u, a_v, b_q, b_f, b_i, b_g = jnp.split(
        z, [A_WIDTH, 2 * A_WIDTH, 2 * A_WIDTH + B_KW, 2 * A_WIDTH + 2 * B_KW,
            2 * A_WIDTH + 2 * B_KW + B_VW], axis=-1)
    a_u = jax.nn.gelu(a_u).reshape(bsz, seq, A_HEADS, A_HEAD_DIM)
    a_v = jax.nn.gelu(a_v).reshape(bsz, seq, A_HEADS, A_HEAD_DIM)
    a_out = gmlp_spatial(a_u, a_v, v_norm, w_s, b_s).reshape(bsz, seq, A_WIDTH)
    zf = b_f.astype(jnp.float32)
    f = lb + (1.0 - lb) * jax.nn.sigmoid(zf)
    log_f = jnp.log(jnp.maximum(f, F_MIN))
    k = 1.0 - f
    o = hgrn2_chunkwise(b_q.reshape(bsz, seq, B_HEADS, B_KEY_DIM),
                        log_f.reshape(bsz, seq, B_HEADS, B_KEY_DIM),
                        k.reshape(bsz, seq, B_HEADS, B_KEY_DIM),
                        b_i.reshape(bsz, seq, B_HEADS, B_VAL_DIM))
    o = rms_norm_2(o, out_norm).astype(h.dtype) * jax.nn.silu(b_g.reshape(bsz, seq, B_HEADS, B_VAL_DIM))
    mixed = jnp.concatenate([a_out, o.reshape(bsz, seq, B_VW)], axis=-1)
    return mixed @ w_out

def rotate_half(x, cos, sin):
    x1, x2 = jnp.split(x, 2, axis=-1)
    return jnp.concatenate([x1 * cos - x2 * sin, x2 * cos + x1 * sin], axis=-1).astype(x.dtype)

def mla_mixer(h, positions, w_in, q_a_norm, kv_a_norm, w_q_b, w_kv_b, q_norm, k_norm, w_out):
    bsz, seq, _ = h.shape
    z = h @ w_in
    c_q, c_kv, k_rope = jnp.split(z, [Q_LORA, Q_LORA + KV_LORA], axis=-1)
    q = (rms_norm_2(c_q, q_a_norm) @ w_q_b).reshape(bsz, seq, C_HEADS, C_QK)
    kv = (rms_norm_2(c_kv, kv_a_norm) @ w_kv_b).reshape(bsz, seq, C_HEADS, C_NOPE + C_V)
    k_nope, v = jnp.split(kv, [C_NOPE], axis=-1)
    k_rope = jnp.broadcast_to(k_rope[:, :, None, :], (bsz, seq, C_HEADS, C_ROPE))
    k = jnp.concatenate([k_nope, k_rope], axis=-1)
    q = rms_norm_2(q, q_norm)
    k = rms_norm_2(k, k_norm)
    inv_freq = ROPE_THETA ** (-jnp.arange(0, C_ROPE, 2, dtype=jnp.float32) / C_ROPE)
    ang = positions.astype(jnp.float32)[..., None] * inv_freq
    cos = jnp.cos(ang)[:, :, None, :]
    sin = jnp.sin(ang)[:, :, None, :]
    q = jnp.concatenate([q[..., :C_NOPE], rotate_half(q[..., C_NOPE:], cos, sin)], axis=-1)
    k = jnp.concatenate([k[..., :C_NOPE], rotate_half(k[..., C_NOPE:], cos, sin)], axis=-1)
    q = jnp.transpose(q, (0, 2, 1, 3))
    k = jnp.transpose(k, (0, 2, 1, 3))
    v = jnp.transpose(v, (0, 2, 1, 3))
    n_blocks = seq // ATTN_BLOCK
    q_blocks = jnp.transpose(q.reshape(bsz, C_HEADS, n_blocks, ATTN_BLOCK, C_QK), (2, 0, 1, 3, 4))
    key_pos = jnp.arange(seq)

    def attend(args):
        qb, start = args
        s = jnp.einsum('bhqd,bhkd->bhqk', qb, k).astype(jnp.float32) * ATTN_SCALE
        q_pos = start + jnp.arange(ATTN_BLOCK)
        s = jnp.where(key_pos[None, :] <= q_pos[:, None], s, NEG_BIG)
        pr = jax.nn.softmax(s, axis=-1).astype(v.dtype)
        return jnp.einsum('bhqk,bhkd->bhqd', pr, v)

    out = lax.map(attend, (q_blocks, jnp.arange(n_blocks) * ATTN_BLOCK))
    out = jnp.transpose(out, (1, 0, 3, 2, 4)).reshape(bsz, seq, C_HEADS * C_V)
    return out @ w_out

def per_layer_embedding(h, p_i, w_gate, w_proj, post_norm):
    return rms_norm_2(jax.nn.sigmoid(h @ w_gate) * (p_i @ w_proj), post_norm)

def second_inputs(seed: int = 0) -> dict:
    key = jax.random.key(seed)
    ks = jax.random.split(key, 32)
    f32 = jnp.float32

    def nrm(k, shape, fan_in):
        return jax.random.normal(k, shape, f32) * (fan_in ** -0.5)

    def gain(k, shape):
        return 1.0 + 0.02 * jax.random.normal(k, shape, f32)

    x = jax.random.normal(ks[0], (BATCH, SEQ, D_MODEL), f32)
    p = jax.random.normal(ks[1], (DEPTH, BATCH, SEQ, D_PLE), f32)
    offset = jax.random.randint(ks[2], (BATCH, 1), 0, 1024, dtype=jnp.int32)
    positions = offset + jnp.arange(SEQ, dtype=jnp.int32)[None, :]
    return {
        'x': x,
        'p': p,
        'positions': positions,
        'norm_gains': gain(ks[3], (DEPTH, N_NORMS, D_MODEL)),
        'ffn_w_gate': nrm(ks[4], (DEPTH, 2, D_MODEL, D_FF), D_MODEL),
        'ffn_w_up': nrm(ks[5], (DEPTH, 2, D_MODEL, D_FF), D_MODEL),
        'ffn_w_down': nrm(ks[6], (DEPTH, 2, D_FF, D_MODEL), D_FF),
        'ple_w_gate': nrm(ks[7], (DEPTH, D_MODEL, D_MODEL), D_MODEL),
        'ple_w_proj': nrm(ks[8], (DEPTH, D_PLE, D_MODEL), D_PLE),
        'even_w_in': nrm(ks[9], (N_EVEN, D_MODEL, EVEN_IN), D_MODEL),
        'gmlp_v_norm': gain(ks[10], (N_EVEN, A_HEADS, A_HEAD_DIM)),
        'gmlp_w_s': nrm(ks[11], (N_EVEN, A_HEADS, A_CHUNK, A_CHUNK), A_CHUNK),
        'gmlp_b_s': 1.0 + 0.01 * jax.random.normal(ks[12], (N_EVEN, A_HEADS, A_CHUNK), f32),
        'hgrn_lb_raw': 0.5 * jax.random.normal(ks[13], (N_EVEN, B_KW), f32),
        'hgrn_out_norm': gain(ks[14], (N_EVEN, B_VAL_DIM)),
        'even_w_out': nrm(ks[15], (N_EVEN, EVEN_OUT, D_MODEL), EVEN_OUT),
        'mla_w_in': nrm(ks[16], (N_ODD, D_MODEL, ODD_IN), D_MODEL),
        'mla_q_a_norm': gain(ks[17], (N_ODD, Q_LORA)),
        'mla_kv_a_norm': gain(ks[18], (N_ODD, KV_LORA)),
        'mla_w_q_b': nrm(ks[19], (N_ODD, Q_LORA, C_HEADS * C_QK), Q_LORA),
        'mla_w_kv_b': nrm(ks[20], (N_ODD, KV_LORA, C_HEADS * (C_NOPE + C_V)), KV_LORA),
        'mla_q_norm': gain(ks[21], (N_ODD, C_QK)),
        'mla_k_norm': gain(ks[22], (N_ODD, C_QK)),
        'mla_w_out': nrm(ks[23], (N_ODD, C_HEADS * C_V, D_MODEL), C_HEADS * C_V),
    }

def second_block(x, p, positions, norm_gains, ffn_w_gate, ffn_w_up, ffn_w_down,
              ple_w_gate, ple_w_proj, even_w_in, gmlp_v_norm, gmlp_w_s, gmlp_b_s,
              hgrn_lb_raw, hgrn_out_norm, even_w_out, mla_w_in, mla_q_a_norm,
              mla_kv_a_norm, mla_w_q_b, mla_w_kv_b, mla_q_norm, mla_k_norm, mla_w_out):
    lb_sm = jax.nn.softmax(hgrn_lb_raw.astype(jnp.float32), axis=0)
    lower_bounds = jnp.clip(jnp.cumsum(lb_sm, axis=0) - lb_sm[0], 0.0, LB_MAX)
    for i in range(DEPTH):
        g = norm_gains[i]
        x = x + 0.5 * swiglu(rms_norm_2(x, g[0]), ffn_w_gate[i, 0], ffn_w_up[i, 0], ffn_w_down[i, 0])
        h = rms_norm_2(x, g[1])
        j = i // 2
        if i % 2 == 0:
            m = even_mixer(h, even_w_in[j], gmlp_v_norm[j], gmlp_w_s[j], gmlp_b_s[j],
                           lower_bounds[j], hgrn_out_norm[j], even_w_out[j])
        else:
            m = mla_mixer(h, positions, mla_w_in[j], mla_q_a_norm[j], mla_kv_a_norm[j],
                          mla_w_q_b[j], mla_w_kv_b[j], mla_q_norm[j], mla_k_norm[j], mla_w_out[j])
        x = x + m
        x = x + 0.5 * swiglu(rms_norm_2(x, g[2]), ffn_w_gate[i, 1], ffn_w_up[i, 1], ffn_w_down[i, 1])
        x = x + per_layer_embedding(rms_norm_2(x, g[3]), p[i], ple_w_gate[i], ple_w_proj[i], g[4])
    return x


def setup_inputs(seed=0):
    out = dict(first_inputs(seed))
    for name, value in second_inputs(seed + 1).items():
        if name != "x":
            out[name + "_2"] = value
    return out


def reference(
    x, meta_tokens, da_norm, da_w_qkv, da_lambda_q1, da_lambda_k1, da_lambda_q2, da_lambda_k2,
    da_subln, da_w_o, dsa_norm, dsa_w_in, dsa_idx_k_norm, dsa_w_o, ffn_norm, ffn_w_up,
    ffn_conv_w, ffn_conv_b, ffn_w_down, final_norm, p_2, positions_2, norm_gains_2,
    ffn_w_gate_2, ffn_w_up_2, ffn_w_down_2, ple_w_gate_2, ple_w_proj_2, even_w_in_2,
    gmlp_v_norm_2, gmlp_w_s_2, gmlp_b_s_2, hgrn_lb_raw_2, hgrn_out_norm_2, even_w_out_2,
    mla_w_in_2, mla_q_a_norm_2, mla_kv_a_norm_2, mla_w_q_b_2, mla_w_kv_b_2, mla_q_norm_2,
    mla_k_norm_2, mla_w_out_2,
):
    x = first_block(
        x, meta_tokens, da_norm, da_w_qkv, da_lambda_q1, da_lambda_k1, da_lambda_q2,
        da_lambda_k2, da_subln, da_w_o, dsa_norm, dsa_w_in, dsa_idx_k_norm, dsa_w_o, ffn_norm,
        ffn_w_up, ffn_conv_w, ffn_conv_b, ffn_w_down, final_norm,
    )
    return second_block(
        x, p_2, positions_2, norm_gains_2, ffn_w_gate_2, ffn_w_up_2, ffn_w_down_2, ple_w_gate_2,
        ple_w_proj_2, even_w_in_2, gmlp_v_norm_2, gmlp_w_s_2, gmlp_b_s_2, hgrn_lb_raw_2,
        hgrn_out_norm_2, even_w_out_2, mla_w_in_2, mla_q_a_norm_2, mla_kv_a_norm_2, mla_w_q_b_2,
        mla_w_kv_b_2, mla_q_norm_2, mla_k_norm_2, mla_w_out_2,
    )


_drawn_inputs = setup_inputs


def setup_inputs(seed=0):
    import zlib

    import numpy as np

    out = dict(_drawn_inputs(seed))
    spreads = {}
    factors = {'dsa_norm': 3.073,
     'dsa_idx_k_norm': 4.524,
     'final_norm': 2.771,
     'gmlp_v_norm_2': 8.0,
     'gmlp_b_s_2': 8.0,
     'hgrn_out_norm_2': 8.0,
     'mla_q_a_norm_2': 8.0,
     'mla_kv_a_norm_2': 8.0,
     'mla_q_norm_2': 8.0,
     'mla_k_norm_2': 8.0}
    for name, (base, spread) in spreads.items():
        noise = np.random.default_rng([zlib.crc32(name.encode()), seed]).standard_normal(out[name].shape)
        drawn = base * np.exp(spread * noise) if base else spread * noise
        out[name] = __import__('jax').numpy.asarray(drawn.astype(out[name].dtype))
    for name, factor in factors.items():
        out[name] = (out[name] * factor).astype(out[name].dtype)
    return out
```

```python
from contextlib import ExitStack

import numpy as np
import concourse.bass as bass
from concourse import mybir

F32 = mybir.dt.float32
I32 = mybir.dt.int32
ACT = mybir.ActivationFunctionType
ALU = mybir.AluOpType
AX = mybir.AxisListType

P = 128
D = 1024
KD = D // P
META = 16
T2 = 256
T1 = T2 + META
F = 2816
KF = F // P
EPS = 1e-6
THETA = 10000.0
NEG = -1e30
LAMBDA_INIT = 0.2
TOPK = 64
IDX_HEADS = 8
CHUNK = 64
TILES1 = [(0, 128), (128, 128), (256, 16)]
TILES2 = [(0, 128), (128, 128)]
SLOTS = 4
SLOT = 4096
DENSE_BANKS = 3
B_COL, B_O, B_S, B_PT = 3, 4, 5, 7
SQ_SLOTS = 9
TWO_PI = 2.0 * np.pi


def shape_constants():
    c = {}
    c["ident"] = np.eye(P, dtype=np.float32)
    c["ones"] = np.ones((P, P), np.float32)
    rot = np.zeros((P, P), np.float32)
    for i in range(P):
        if i % 64 < 32:
            rot[i + 32, i] = -1.0
        else:
            rot[i - 32, i] = 1.0
    c["rot"] = rot
    inv = np.float32(THETA) ** (-np.arange(0, 64, 2, dtype=np.float32) / np.float32(64))
    ang = np.arange(T1, dtype=np.float32)[None, :] * inv.astype(np.float32)[:, None]
    c["cos"] = np.tile(np.cos(ang), (4, 1)).astype(np.float32)
    c["sin"] = np.tile(np.sin(ang), (4, 1)).astype(np.float32)
    c["inv"] = np.tile(inv[:, None], (4, 1)).astype(np.float32)
    q = np.arange(P)[:, None, None] + 128 * np.arange(3)[None, :, None]
    k = np.arange(T1)[None, None, :]
    causal = k <= q
    c["causal"] = np.where(causal, 0.0, NEG).astype(np.float32).reshape(P, -1)
    return c


def index_constants():
    q = np.arange(P)[:, None, None] + 128 * np.arange(3)[None, :, None]
    k = np.arange(T1)[None, None, :]
    causal = k <= q
    keep = (causal & (k >= META)).astype(np.float32)
    add = np.where(causal, np.where(k < META, 1e30, 0.0), -1e38).astype(np.float32)
    return np.concatenate([keep.reshape(P, -1), add.reshape(P, -1)], 1)


def level_masks():
    s = np.arange(P)[:, None]
    t = np.arange(P)[None, :]
    out = [(s == t)]
    for m in LEVELS:
        out.append((s // (2 * m) == t // (2 * m)) & (s % (2 * m) < m) & (t % (2 * m) >= m))
    return np.concatenate(out, 1).astype(np.float32)


LEVELS = [32, 16, 8, 4, 2, 1]

CONST_PARTS = [("ident", P), ("ones", P), ("rot", P), ("cos", T1), ("sin", T1), ("inv", 1), ("causal", 3 * T1)]
VEC_PARTS = [("da_norm", 8), ("subln", 1), ("dsa_norm", 8), ("idxk", 1), ("ffn_norm", 16), ("conv_w", 2 * 3 * 44),
             ("conv_b", 2 * 44), ("final", 8), ("gains", 80), ("lb_raw", 4), ("hg_out", 1), ("qa", 3), ("kva", 2),
             ("qn", 1), ("qr", 1), ("kn", 1), ("kr", 1), ("lam", 4)]
EVEN_PARTS = [("lmask", 7 * P), ("wsT", 8 * P), ("bs", 4 * P), ("vnorm", 512)]


def offsets(parts):
    o, at = {}, 0
    for name, n in parts:
        o[name] = (at, n)
        at += n
    return o, at


CONST_AT, CONST_N = offsets(CONST_PARTS)
VEC_AT, VEC_N = offsets(VEC_PARTS)
EVEN_AT, EVEN_N = offsets(EVEN_PARTS)


class Plan:

    def __init__(self):
        self.panels = []
        self.chunks = []
        self.half = 0
        self.stages = {}
        self.owned = {"act": 0, "dve": 0, "hid": 2 * KF}

    def stage(self, name):
        self.stages[name] = {"steps": [], "first": len(self.chunks), "n": 0}
        self.now = self.stages[name]

    def panel(self, loads, k, n):
        self.panels.append({"loads": loads, "k": k, "n": n})
        return len(self.panels) - 1

    def step(self, panel, kind, cols, size, k0, k, owner=None, tile=None, chunk=None, last=True):
        start = chunk is None
        if start:
            chunk = len(self.chunks)
            self.chunks.append({"owner": owner, "nth": self.owned[owner]})
            self.owned[owner] += 1
            self.now["n"] += 1
        self.now["steps"].append(dict(panel=panel, kind=kind, cols=cols, size=size, k0=k0, k=k, tile=tile,
                                      chunk=chunk, start=start, stop=last))
        if last:
            self.panels[panel]["free"] = ("chunk", chunk + 1)
        else:
            self.half += 1
            self.panels[panel]["free"] = ("half", self.half)
        return chunk


def cut(a, n):
    return lambda v, k: v[:, k, a:a + n]


def make_plan(W):
    pl = Plan()

    def rows(w):
        return w.rearrange("(k p) n -> p k n", p=P)

    def feature_panels(w, c0, c1, owner, k=KD, width=512):
        for c in range(c0, c1, width):
            n = min(width, c1 - c)
            p = pl.panel([(0, n, rows(w)[:, :, c:c + n])], k, n)
            for m in range(0, n, P):
                pl.step(p, "fm", cut(m, min(P, n - m)), min(P, n - m), 0, k, owner)

    def token_panels(w, c0, c1, owner, tiles):
        for c in range(c0, c1, 512):
            p = pl.panel([(0, 512, rows(w)[:, :, c:c + 512])], KD, 512)
            for t in range(len(tiles)):
                pl.step(p, "tm", cut(0, 512), 512, 0, KD, owner, tile=tiles[t])

    def up_panels(wg, wu, gate_owner, up_owner):
        for c in range(0, F, 256):
            p = pl.panel([(0, 256, rows(wg)[:, :, c:c + 256]), (256, 512, rows(wu)[:, :, c:c + 256])], KD, 512)
            for m in range(2):
                pl.step(p, "fm", cut(m * P, P), P, 0, KD, gate_owner)
                pl.step(p, "fm", cut(256 + m * P, P), P, 0, KD, up_owner)

    def down_panels(w):
        kh = KF // 2
        for c in range(0, D, 256):
            a = pl.panel([(0, 256, rows(w)[:, 0:kh, c:c + 256])], kh, 256)
            ids = [pl.step(a, "fm", cut(m * P, P), P, 0, kh, "dve", last=False) for m in range(2)]
            b = pl.panel([(0, 256, rows(w)[:, kh:KF, c:c + 256])], kh, 256)
            for m in range(2):
                pl.step(b, "fm", cut(m * P, P), P, kh, kh, chunk=ids[m])

    pl.stage("da_qkv")
    feature_panels(W["da_w_qkv"][0], 0, 2 * D, "act")
    token_panels(W["da_w_qkv"][0], 2 * D, 3 * D, "act", TILES1)
    pl.stage("da_out")
    feature_panels(W["da_w_o"][0], 0, D, "dve")
    for i in range(2):
        if i == 1:
            w = W["dsa_w_in"][0]
            pl.stage("dsa_in")
            feature_panels(w, 3072, 3584, "act")
            p = pl.panel([(0, 72, rows(w)[:, :, 3584:3656])], KD, 72)
            pl.step(p, "fm", cut(0, 64), 64, 0, KD, "act")
            for t in range(3):
                pl.step(p, "tm", cut(64, 8), 8, 0, KD, "act", tile=TILES1[t])
            token_panels(w, 2 * D, 3 * D, "act", TILES1)
            feature_panels(w, 0, 2 * D, "act")
            pl.stage("dsa_out")
            feature_panels(W["dsa_w_o"][0], 0, D, "dve")
        pl.stage(f"conv{i}_up")
        up_panels(W["ffn_w_up"][i][:, 0:F], W["ffn_w_up"][i][:, F:2 * F], "dve", "dve")
        pl.stage(f"conv{i}_down")
        down_panels(W["ffn_w_down"][i])
    for i in range(2):
        for j in range(2):
            if j == 1 and i == 0:
                w = W["even_w_in"][0]
                pl.stage("ev_in")
                feature_panels(w, 1536, 2048, "act")
                feature_panels(w, 1024, 1536, "act")
                token_panels(w, 2048, 2560, "act", TILES2)
                token_panels(w, 512, 1024, "act", TILES2)
                feature_panels(w, 0, 512, "act")
                feature_panels(w, 2560, 3072, "act")
                pl.stage("ev_out")
                feature_panels(W["even_w_out"][0], 0, D, "dve")
            if j == 1 and i == 1:
                pl.stage("mla_in")
                feature_panels(W["mla_w_in"][0], 0, 704, "act")
                pl.stage("mla_q")
                for g in range(2):
                    w = W["mla_w_q_b"][0]
                    loads = []
                    for hh in range(4):
                        c = (4 * g + hh) * 192
                        loads.append((hh * P, (hh + 1) * P, rows(w)[:, :, c:c + P]))
                        loads.append((512 + hh * 64, 512 + hh * 64 + 64, rows(w)[:, :, c + P:c + 192]))
                    p = pl.panel(loads, 3, 768)
                    for m in range(0, 768, P):
                        pl.step(p, "fm", cut(m, P), P, 0, 3, "act")
                pl.stage("mla_kv")
                p = pl.panel([(0, 2048, rows(W["mla_w_kv_b"][0]))], 2, 2048)
                for hh in range(8):
                    pl.step(p, "fm", cut(hh * 256, P), P, 0, 2, "act")
                for g in range(2):
                    for t in range(2):
                        pl.step(p, "tm", lambda v, k, g=g: v.rearrange("p k (h c) -> p k h c", c=256)[
                            :, k, 4 * g:4 * g + 4, 128:256], 512, 0, 2, "act", tile=TILES2[t])
                pl.stage("mla_out")
                feature_panels(W["mla_w_out"][0], 0, D, "dve")
            pl.stage(f"glu{i}{j}_up")
            up_panels(W["ffn_w_gate"][i][j], W["ffn_w_up_2"][i][j], "act", "hid")
            pl.stage(f"glu{i}{j}_down")
            down_panels(W["ffn_w_down_2"][i][j])
        pl.stage(f"ple{i}_gate")
        feature_panels(W["ple_w_gate"][i], 0, D, "act")
        pl.stage(f"ple{i}_proj")
        feature_panels(W["ple_w_proj"][i], 0, D, "dve", k=2, width=1024)
    return pl


def make_norms():
    order = [("da", 8, 8)] + [(f"o{h}", 1, 1) for h in range(8)] + [("conv0", 8, 8), ("dsa", 8, 8), ("ki", 1, 1),
             ("conv1", 8, 8), ("final", 8, 8), ("glu00", 8, 8), ("ev", 8, 8)]
    order += [(f"hg{h}", 1, 1) for h in range(4)] + [("glu01", 8, 8), ("pleh0", 8, 8), ("pleo0", 8, 8),
             ("glu10", 8, 8), ("mla", 8, 8), ("cq", 3, 3), ("ckv", 2, 2)]
    order += [(f"q{h}", 2, 2) for h in range(8)] + [(f"k{h}", 2, 2) for h in range(8)]
    order += [("glu11", 8, 8), ("pleh1", 8, 8), ("pleo1", 8, 8)]
    out, sq, ap = {}, 0, 0
    for i, (name, n, m) in enumerate(order):
        prev = order[i - 1][1] if i else 0
        out[name] = dict(id=i, sq=sq, n=n, ap=ap, m=m, alone=prev + n > SQ_SLOTS)
        sq, ap = sq + n, ap + m
    out["by_id"] = [out[name] for name, _, _ in order]
    return out


def make_attention():
    out, s, u, oc = {}, 0, 0, 0
    for name, heads, tiles, comps, dv in (("da", 8, TILES1, 2, 128), ("dsa", 16, TILES1, 1, 64),
                                          ("mla", 8, TILES2, 1, 128)):
        units = []
        for h in range(heads):
            for t, (q0, qn) in enumerate(tiles):
                per = P // dv
                units.append(dict(h=h, t=t, q0=q0, qn=qn, kn=q0 + qn, u=u, scores=list(range(s, s + comps)),
                                  oc=oc + h // per, first=(h % per == 0 and t == 0),
                                  last=(h % per == per - 1 and t == len(tiles) - 1), part=dv * (h % per), dv=dv,
                                  chunk=h // per, ktiles=[(a, min(n, P)) for a, n in tiles if a < q0 + qn]))
                s += comps
                u += 1
        out[name] = dict(units=units, tiles=tiles, heads=heads)
        oc += heads * dv // P
    unit_of_score = [x["u"] for a in ("da", "dsa", "mla") for x in out[a]["units"] for _ in x["scores"]]
    return out, unit_of_score


ROPE_BASE = {"da": 0, "idx": 16, "dsa": 21, "kr": 37, "mq": 38}


def build(nc, W, hT, consts, idxc, vecs, evenc, pT_in, pos, out):
    plan = make_plan(W)
    norms = make_norms()
    att, unit_of_score = make_attention()
    chunks, stages, panels = plan.chunks, plan.stages, plan.panels

    with ExitStack() as ctx:
        def sb(name, shape, dt=F32):
            return ctx.enter_context(nc.sbuf_tensor(name, shape, dt))

        def sem(name):
            return ctx.enter_context(nc.semaphore(name))

        bank = ctx.enter_context(nc.psum_tensor("bank", [P, 8, 512], F32))
        ring = sb("ring", [P, SLOTS, SLOT])
        h = sb("h", [P, KD, T1])
        hn = sb("hn", [P, KD, T1])
        sq = sb("sq", [P, SQ_SLOTS, T1])
        arena = sb("arena", [P, 22 * T1 + 24 * T1 + 3072 + 8 * T1])
        cst = sb("cst", [P, CONST_N])
        vec = sb("vec", [P, VEC_N])
        cs2 = sb("cs2", [P, 2, T2])
        late = sb("late", [P, max(9 * T1, EVEN_N)])
        sm = sb("sm", [P, 4, T1])
        pr = sb("pr", [P, 4, T1])
        pn = sb("pn", [P, 2, T1])
        pT = sb("pT", [P, 2, 3 * P])
        t1 = sb("t1", [P, 2, T1])
        t2 = sb("t2", [P, 2, T1])
        rinv = sb("rinv", [P, 2, T1])
        rstd = sb("rstd", [P, 2, T1])
        small = sb("small", [P, 128])

        def part(off, n, width=None):
            v = arena[:, off:off + n]
            return v.rearrange("p (c t) -> p c t", t=width) if width else v

        wide = part(0, 22 * T1, T1)
        qT = part(22 * T1, 12 * T1, T1)
        kT = part(34 * T1, 12 * T1, T1)
        v_tok = part(46 * T1, 3072, 1024)
        oT = part(46 * T1 + 3072, 8 * T1, T1)

        def con(name, rows=P):
            a, n = CONST_AT[name]
            return cst[0:rows, a:a + n]

        ident, ones, rot = con("ident"), con("ones"), con("rot")
        cos1, sin1 = con("cos"), con("sin")
        causal = con("causal").rearrange("p (t k) -> p t k", t=3)

        def col(name, i=0, p0=0, pn_=P):
            a, _ = VEC_AT[name]
            return vec[p0:p0 + pn_, a + i:a + i + 1]

        keep = late[:, 0:3 * T1].rearrange("p (t k) -> p t k", t=3)
        addm = late[:, 3 * T1:6 * T1].rearrange("p (t k) -> p t k", t=3)
        amask = late[:, 6 * T1:9 * T1].rearrange("p (t k) -> p t k", t=3)

        def even(name):
            a, n = EVEN_AT[name]
            return late[:, a:a + n]

        mx, nmx, ssum, rs = small[:, 0:8], small[:, 8:16], small[:, 16:24], small[:, 24:32]
        wi_tok = small[:, 32:56].rearrange("p (t h) -> p t h", t=3)
        lam, lam_e, subln8, lam_p = small[:, 56:57], small[:, 57:59], small[:, 59:60], small[:, 60:62]
        max8 = small[:, 62:70]
        lb_t, lb, oml = small[:, 70:74], small[:, 74:78], small[:, 78:82]
        rl = small[:, 82:83]
        vms = small[:, 84:100]
        e_last = small[:, 100:116]

        s_const = sem("constants_loaded")
        s_idxc = sem("index_constants_loaded")
        s_pos = sem("positions_loaded")
        s_even = sem("even_constants_loaded")
        s_slot = [sem(f"slot{i}_loaded") for i in range(SLOTS)]
        s_ple = sem("layer_embedding_loaded")
        s_chunk = sem("chunk_ready")
        s_half = sem("half_chunk_ready")
        s_free = {"act": sem("chunk_emptied_by_act"), "dve": sem("chunk_emptied_by_dve")}
        s_sq = sem("squares_ready")
        s_col = sem("square_sum_ready")
        s_rinv = sem("mean_square_inverse_ready")
        s_rstd = sem("rstd_ready")
        s_app = sem("norm_applied")
        s_rot = sem("rotated_ready")
        s_t1 = sem("cos_part_ready")
        s_rope = sem("rope_ready")
        s_score = sem("scores_ready")
        s_max = sem("row_max_ready")
        s_exp = sem("exp_ready")
        s_prob = sem("probs_ready")
        s_tr = sem("probs_transposed")
        s_ptc = sem("probsT_copied")
        s_pv = sem("pv_done")
        s_oev = sem("attention_out_ready")
        s_idx = sem("index_raw_ready")
        s_relu = sem("index_relu_ready")
        s_idxa = sem("index_sum_ready")
        s_top = sem("topk_mask_ready")
        s_hid = sem("hidden_ready")
        s_conv = sem("conv_first_tap_ready")
        s_free["hid"] = s_hid
        s_silu = sem("silu_ready")
        s_lam = sem("lambda_products_ready")
        s_lams = sem("lambda_sums_ready")
        s_lame = sem("lambda_exp_ready")
        s_final = sem("second_block_input_ready")
        s_ang = sem("angles_ready")
        s_sincos = sem("sincos_ready")
        s_lbd = sem("lb_difference_ready")
        s_lbe = sem("lb_exp_ready")
        s_f = sem("forget_floor_ready")
        s_ln = sem("log_forget_ready")
        s_lvd = sem("level_exponent_ready")
        s_lve = sem("level_decay_ready")
        s_lvq = sem("level_operands_ready")
        s_lvm = sem("level_scores_ready")
        s_lva = sem("level_scores_added")
        s_ws = sem("spatial_weights_masked")
        s_vms = sem("value_mean_square_ready")
        s_vrs = sem("value_rstd_ready")
        s_gv = sem("value_normed")
        s_mixp = sem("spatial_product_ready")
        s_mix = sem("mixed_ready")
        s_kkt = sem("key_transposed")
        s_kkc = sem("key_copied")
        s_upd = sem("state_update_ready")
        s_st = sem("state_ready")
        s_hgo = sem("hgrn_product_ready")
        s_hge = sem("hgrn_out_ready")
        s_gate = sem("hgrn_gated")
        s_kr = sem("shared_rope_key_gained")
        s_out = sem("output_stored")
        s_dve = sem("dve_step")
        s_act = sem("act_step")

        def emptied(eng, c):
            eng.wait_ge(s_free[chunks[c]["owner"]], chunks[c]["nth"] + 1)

        def chunk_of(stage, i):
            return stages[stage]["first"] + i

        def dense_bank(c):
            return bank[:, c % DENSE_BANKS, :]

        def conv_buf(n):
            return sm[:, n % 4, :]

        def silu_buf(n):
            return pn[:, n % 2, :]

        block = ctx.enter_context(nc.Block())

        @block.sync
        def _(sp):
            for n, p in enumerate(panels):
                if n >= SLOTS:
                    kind, v = panels[n - SLOTS]["free"]
                    sp.wait_ge(s_chunk if kind == "chunk" else s_half, v)
                view = ring[:, n % SLOTS, 0:p["k"] * p["n"]].rearrange("p (k n) -> p k n", n=p["n"])
                for a, b, src in p["loads"]:
                    sp.dma_start(view[:, :, a:b], src).then_inc(s_slot[n % SLOTS], 16)
            sp.wait_ge(s_free["dve"], plan.owned["dve"])
            sp.wait_ge(s_final, 8 + 16)
            sp.dma_start(out.rearrange("(c p) t -> p c t", p=P), h[:, :, 0:T2]).then_inc(s_out, 16)
            sp.wait_ge(s_out, 16)

        loaded = []
        seen = [0] * SLOTS
        for n, p in enumerate(panels):
            seen[n % SLOTS] += 16 * len(p["loads"])
            loaded.append(seen[n % SLOTS])

        @block.tensor
        def _(pe):
            def dense(stage, src, T, ready=(), after=None):
                waited, now = set(), -1
                for s in stages[stage]["steps"]:
                    if s["panel"] != now:
                        now = s["panel"]
                        pe.wait_ge(s_slot[now % SLOTS], loaded[now])
                    p = panels[now]
                    view = ring[:, now % SLOTS, 0:p["k"] * p["n"]].rearrange("p (k n) -> p k n", n=p["n"])
                    if s["start"] and s["chunk"] >= DENSE_BANKS:
                        emptied(pe, s["chunk"] - DENSE_BANKS)
                    for k in range(s["k"]):
                        kk = s["k0"] + k
                        if kk not in waited and kk < len(ready):
                            pe.wait_ge(*ready[kk])
                            waited.add(kk)
                        b = dense_bank(s["chunk"])
                        st, sp_ = s["start"] and k == 0, s["stop"] and k == s["k"] - 1
                        if s["kind"] == "fm":
                            mm = nc.tensor.matmul(b[0:s["size"], 0:T], s["cols"](view, k), src(kk)[:, 0:T],
                                                  start=st, stop=sp_)
                        else:
                            q0, qn = s["tile"]
                            mm = nc.tensor.matmul(b[0:qn, 0:s["size"]], src(kk)[:, q0:q0 + qn], s["cols"](view, k),
                                                  start=st, stop=sp_)
                    mm.then_inc(s_chunk if s["stop"] else s_half, 1)
                    if after and s["stop"]:
                        after(s["chunk"] - stages[stage]["first"])

            def norm_sum(name, T, parts=((0, P),) * 8):
                m = norms[name]
                if m["id"]:
                    pe.wait_ge(s_rinv, m["id"])
                for i in range(m["n"]):
                    a, n = parts[i]
                    pe.wait_ge(s_sq, m["sq"] + i + 1)
                    mm = nc.tensor.matmul(bank[:, B_COL, 0:T], ones[a:a + n, :],
                                          sq[a:a + n, (m["sq"] + i) % SQ_SLOTS, 0:T],
                                          start=(i == 0), stop=(i == m["n"] - 1))
                mm.then_inc(s_col, 1)

            def rotate(r, raw, T, ready, rows=P):
                pe.wait_ge(*ready)
                if r >= 2:
                    pe.wait_ge(s_rope, r - 1)
                nc.tensor.matmul(bank[0:rows, B_S + r % 2, 0:T], rot[0:rows, 0:rows], raw,
                                 start=True, stop=True).then_inc(s_rot, 1)

            def attention(name, score_ops):
                A = att[name]
                U = A["units"]
                for i in range(len(U) + 3):
                    if i < len(U):
                        x = U[i]
                        for c, s in enumerate(x["scores"]):
                            if s >= 2:
                                pe.wait_ge(s_max, s - 1)
                            ops = score_ops(x, c)
                            for j, (a, b) in enumerate(ops):
                                mm = nc.tensor.matmul(bank[0:x["qn"], B_S + s % 2, 0:x["kn"]], a, b,
                                                      start=(j == 0), stop=(j == len(ops) - 1))
                            mm.then_inc(s_score, 1)
                    if 2 <= i < len(U) + 2:
                        x = U[i - 2]
                        pe.wait_ge(s_prob, x["u"] + 1)
                        if x["u"]:
                            pe.wait_ge(s_ptc, x["u"])
                        for kt, (a, n) in enumerate(x["ktiles"]):
                            mm = nc.tensor.transpose(bank[0:n, B_PT, kt * P:kt * P + x["qn"]],
                                                     pn[0:x["qn"], x["u"] % 2, a:a + n],
                                                     ident[0:x["qn"], 0:x["qn"]])
                        mm.then_inc(s_tr, 1)
                    if i >= 3:
                        x = U[i - 3]
                        pe.wait_ge(s_ptc, x["u"] + 1)
                        if x["first"] and x["oc"] >= 2:
                            pe.wait_ge(s_oev, x["oc"] - 1)
                        ob = bank[x["part"]:x["part"] + x["dv"], B_O - x["oc"] % 2, x["q0"]:x["q0"] + x["qn"]]
                        for kt, (a, n) in enumerate(x["ktiles"]):
                            mm = nc.tensor.matmul(ob, v_tok[0:n, kt, x["h"] * x["dv"]:(x["h"] + 1) * x["dv"]],
                                                  pT[0:n, x["u"] % 2, kt * P:kt * P + x["qn"]],
                                                  start=(kt == 0), stop=(kt == len(x["ktiles"]) - 1))
                        mm.then_inc(s_pv, 1)

            def normed(name):
                m = norms[name]
                return [(s_app, m["ap"] + i + 1) for i in range(m["m"])]

            def hidden(i):
                return [(s_hid, i * KF + k + 1) for k in range(KF)]

            def act_chunk(c):
                return (s_free["act"], chunks[c]["nth"] + 1)

            hn_k = lambda k: hn[:, k, :]
            wide_k = lambda k: wide[:, k, :]
            oT_k = lambda k: oT[:, k, :]

            pe.wait_ge(s_const, 48)
            pe.wait_ge(s_lam, 1)
            nc.tensor.matmul(bank[:, B_PT, 0:2], ones[0:64, :], lam_p[0:64, :], start=True, stop=True)\
                .then_inc(s_lams, 1)
            norm_sum("da", T1)

            def da_after(j):
                if 2 <= j < 18:
                    rotate(j - 2, wide[:, j - 2, :], T1, act_chunk(chunk_of("da_qkv", j - 2)))
            dense("da_qkv", hn_k, T1, normed("da"), da_after)
            pe.wait_ge(s_rope, 16)

            def da_ops(x, c):
                return [(qT[64 * c:64 * c + 64, x["h"], x["q0"]:x["q0"] + x["qn"]],
                         kT[64 * c:64 * c + 64, x["h"], 0:x["kn"]])]
            attention("da", da_ops)
            for hh in range(8):
                norm_sum(f"o{hh}", T1)
            m = norms["o0"]
            dense("da_out", oT_k, T1, [(s_app, m["ap"] + i + 1) for i in range(8)])
            norm_sum("conv0", T1)
            dense("conv0_up", hn_k, T1, normed("conv0"))
            dense("conv0_down", wide_k, T1, hidden(0))

            norm_sum("dsa", T1)
            rb = ROPE_BASE["idx"]

            def dsa_after(j):
                if 2 <= j < 6:
                    rotate(rb + j - 2, wide[:, j - 2, :], T1, act_chunk(chunk_of("dsa_in", j - 2)))
                if j == 7:
                    norm_sum("ki", T1, ((0, 64),))
                    rotate(rb + 4, wide[0:64, 5, :], T1, (s_app, norms["ki"]["ap"] + 1), rows=64)
                    pe.wait_ge(s_rope, rb + 5)
                    pe.wait_ge(s_top, 1)
                    for x in range(24):
                        t, hh = divmod(x, 8)
                        q0, qn = TILES1[t]
                        a = 64 * (hh % 2)
                        if x >= 2:
                            pe.wait_ge(s_relu, x - 1)
                        nc.tensor.matmul(bank[0:qn, B_S + x % 2, 0:q0 + qn], qT[a:a + 64, 8 + hh // 2, q0:q0 + qn],
                                         kT[a:a + 64, 8, 0:q0 + qn], start=True, stop=True).then_inc(s_idx, 1)
                if j == 14:
                    pe.wait_ge(s_relu, 24)
                if j >= 16:
                    i = j - 16
                    rotate(ROPE_BASE["dsa"] + i, wide[:, 6 + i, :], T1, act_chunk(chunk_of("dsa_in", 14 + i)))
            dense("dsa_in", hn_k, T1, normed("dsa"), dsa_after)
            for i in (14, 15):
                rotate(ROPE_BASE["dsa"] + i, wide[:, 6 + i, :], T1, act_chunk(chunk_of("dsa_in", 14 + i)))
            pe.wait_ge(s_rope, ROPE_BASE["dsa"] + 16)

            def dsa_ops(x, c):
                a = 64 * (x["h"] % 2)
                return [(qT[a:a + 64, x["h"] // 2, x["q0"]:x["q0"] + x["qn"]], kT[a:a + 64, x["h"] // 2, 0:x["kn"]])]
            attention("dsa", dsa_ops)
            oc0 = att["dsa"]["units"][0]["oc"]
            dense("dsa_out", oT_k, T1, [(s_oev, oc0 + i + 1) for i in range(8)])
            norm_sum("conv1", T1)
            dense("conv1_up", hn_k, T1, normed("conv1"))
            dense("conv1_down", wide_k, T1, hidden(1))
            norm_sum("final", T1)

            def glu(i, j):
                norm_sum(f"glu{i}{j}", T2)
                dense(f"glu{i}{j}_up", hn_k, T2, normed(f"glu{i}{j}"))
                dense(f"glu{i}{j}_down", wide_k, T2, hidden(2 + 2 * i + j))

            def ple(i):
                norm_sum(f"pleh{i}", T2)
                dense(f"ple{i}_gate", hn_k, T2, normed(f"pleh{i}"))
                dense(f"ple{i}_proj", lambda k: oT[:, k, :], T2, [(s_ple, 16 * (i + 1))] * 2)
                norm_sum(f"pleo{i}", T2)

            glu(0, 0)
            norm_sum("ev", T2)
            dense("ev_in", hn_k, T2, normed("ev"))
            slot = lambda i: part(i * 1024, 1024)
            hg_v = part(11 * 1024, 1024, 512)
            scT = part(10 * 1024, 1024, 512)
            nq = chunks[chunk_of("ev_in", 4)]["nth"]
            pe.wait_ge(s_free["act"], nq + 6)
            for lv in range(7):
                pe.wait_ge(s_lvq, lv + 1)
                if lv == 0:
                    qe_, ke_ = slot(0), slot(1)
                else:
                    qe_, ke_ = slot(6 + lv % 2), slot(8 + lv % 2)
                for t in range(2):
                    if lv:
                        pe.wait_ge(s_lva, 2 * (lv - 1) + t + 1)
                    for hh in range(4):
                        o = hh * T2 + t * P
                        mm = nc.tensor.matmul(bank[:, B_S + t, hh * P:(hh + 1) * P], ke_[:, o:o + P],
                                              qe_[:, o:o + P], start=True, stop=True)
                    mm.then_inc(s_lvm, 1)
            pe.wait_ge(s_gv, 1)
            pe.wait_ge(s_ws, 1)
            gvn = part(14 * 1024, 1024, 512)
            wsT = even("wsT").rearrange("p (h t) -> p h t", h=8)
            for t in range(2):
                for hh in range(8):
                    a = 64 * (hh % 2)
                    mm = nc.tensor.matmul(bank[a:a + 64, B_COL + t, (hh // 2) * P:(hh // 2 + 1) * P],
                                          gvn[:, t, hh * 64:hh * 64 + 64], wsT[:, hh, :], start=True, stop=True)
                mm.then_inc(s_mixp, 1)
            pe.wait_ge(s_gate, 1)
            kk = slot(7)
            for t in range(2):
                if t == 1:
                    pe.wait_ge(s_kkc, 1)
                for hh in range(4):
                    mm = nc.tensor.transpose(bank[:, B_PT, hh * P:(hh + 1) * P],
                                             kk[:, hh * T2 + t * P:hh * T2 + t * P + P], ident)
                mm.then_inc(s_kkt, 1)
            kk_tok = part(14 * 1024, 1024, 512)
            pe.wait_ge(s_kkc, 2)
            pe.wait_ge(s_lva, 14)
            for n in range(3):
                a, t = 64 * (n % 2), n // 2
                if n >= 2:
                    pe.wait_ge(s_st, n - 1)
                for hh in range(4):
                    mm = nc.tensor.matmul(bank[:, B_S + n % 2, hh * P:(hh + 1) * P],
                                          kk_tok[a:a + 64, t, hh * P:(hh + 1) * P],
                                          hg_v[a:a + 64, t, hh * P:(hh + 1) * P], start=True, stop=True)
                mm.then_inc(s_upd, 1)
            states = part(8 * 1024, 1536, 512)
            qe = slot(6)
            pe.wait_ge(s_mix, 2)
            pe.wait_ge(s_st, 3)
            for hh in range(4):
                b = B_COL + hh // 2
                for t in range(2):
                    o = (hh % 2) * T2 + t * P
                    nc.tensor.matmul(bank[:, b, o:o + P], hg_v[:, t, hh * P:(hh + 1) * P],
                                     scT[:, t, hh * P:(hh + 1) * P], start=True, stop=False)
                    for n in range(max(1, 2 * t), 2 * t + 2):
                        oo = (hh % 2) * T2 + n * CHUNK
                        mm = nc.tensor.matmul(bank[:, b, oo:oo + CHUNK], states[:, n - 1, hh * P:(hh + 1) * P],
                                              qe[:, hh * T2 + n * CHUNK:hh * T2 + (n + 1) * CHUNK],
                                              start=False, stop=(n == 2 * t + 1))
                mm.then_inc(s_hgo, 1)
            pe.wait_ge(s_hge, 4)
            for hh in range(4):
                norm_sum(f"hg{hh}", T2)
            mixr = [(s_mix, 2)] * 4 + [(s_gate, 2 + i) for i in range(4)]
            dense("ev_out", oT_k, T2, mixr)
            glu(0, 1)
            ple(0)
            glu(1, 0)
            norm_sum("mla", T2)
            dense("mla_in", hn_k, T2, normed("mla"))
            norm_sum("cq", T2)
            norm_sum("ckv", T2)
            dense("mla_q", lambda k: hn[:, k, :], T2, normed("cq"))
            dense("mla_kv", lambda k: hn[:, 3 + k, :], T2, normed("ckv"))
            rotate(ROPE_BASE["kr"], oT[:, 6, 0:T2], T2, (s_kr, 1))
            for hh in range(8):
                a = 64 * (hh % 2)
                norm_sum(f"q{hh}", T2, ((0, P), (a, 64)))
            for hh in range(8):
                a = 64 * (hh % 2)
                norm_sum(f"k{hh}", T2, ((0, P), (a, 64)))
            for r in range(4):
                rotate(ROPE_BASE["mq"] + r, wide[:, 6 + 8 + r, 0:T2], T2, (s_app, norms[f"q{2 * r + 1}"]["ap"] + 2))
            pe.wait_ge(s_rope, ROPE_BASE["mq"] + 4)
            pe.wait_ge(s_app, norms["k7"]["ap"] + 2)

            def mla_ops(x, c):
                a = 64 * (x["h"] % 2)
                hh = x["h"]
                q = slice(x["q0"], x["q0"] + x["qn"])
                return [(qT[:, hh, q], kT[:, hh, 0:x["kn"]]),
                        (qT[a:a + 64, 8 + hh // 2, q], kT[a:a + 64, 8 + hh // 2, 0:x["kn"]])]
            attention("mla", mla_ops)
            oc0 = att["mla"]["units"][0]["oc"]
            dense("mla_out", oT_k, T2, [(s_oev, oc0 + i + 1) for i in range(8)])
            glu(1, 1)
            ple(1)

        @block.scalar
        def _(act):
            def step(ins):
                step.n += 1
                ins.then_inc(s_act, 1)
                act.wait_ge(s_act, step.n)
            step.n = 0

            def square(name, srcs, ready, parts=((0, P),) * 8, T=T1):
                m = norms[name]
                need = m["id"] if m["alone"] else m["id"] - 1
                if need > 0:
                    act.wait_ge(s_col, need)
                for i, s in enumerate(srcs):
                    a, n = parts[i]
                    act.wait_ge(*ready[i])
                    nc.scalar.activation(sq[a:a + n, (m["sq"] + i) % SQ_SLOTS, 0:T], s, ACT.Square).then_inc(s_sq, 1)

            def root(name, T):
                m = norms[name]
                act.wait_ge(s_rinv, m["id"] + 1)
                if m["id"] >= 2:
                    act.wait_ge(s_app, norms["by_id"][m["id"] - 1]["ap"])
                nc.scalar.activation(rstd[:, m["id"] % 2, 0:T], rinv[:, m["id"] % 2, 0:T], ACT.Sqrt)\
                    .then_inc(s_rstd, 1)

            def residual(stage):
                c0 = stages[stage]["first"]
                return [(s_free["dve"], chunks[c0 + i]["nth"] + 1) for i in range(8)]

            def norm_h(name, ready, T):
                square(name, [h[:, c, 0:T] for c in range(KD)], ready, T=T)
                root(name, T)

            def evict(c, dst, func=ACT.Copy, src=None, scale=1.0, last=True):
                act.wait_ge(s_chunk, c + 1)
                b = dense_bank(c)
                src = b[0:dst.shape[0], 0:int(np.prod(dst.shape[1:]))] if src is None else src
                ins = nc.scalar.activation(dst, src, func, scale=scale)
                if last:
                    ins.then_inc(s_free["act"], 1)

            def attention(name, scale):
                U = att[name]["units"]
                for i in range(len(U) + 3):
                    if i < len(U):
                        x = U[i]
                        for s in x["scores"]:
                            act.wait_ge(s_max, s + 1)
                            if s >= 4:
                                act.wait_ge(s_prob, unit_of_score[s - 4] + 1)
                            q, k = x["qn"], x["kn"]
                            nc.scalar.activation(pr[0:q, s % 4, 0:k], sm[0:q, s % 4, 0:k], ACT.Exp,
                                                 bias=nmx[0:q, s % 8:s % 8 + 1], scale=scale,
                                                 accum_out=ssum[0:q, s % 8:s % 8 + 1]).then_inc(s_exp, 1)
                    if 2 <= i < len(U) + 2:
                        x = U[i - 2]
                        u, q = x["u"], x["qn"]
                        act.wait_ge(s_tr, u + 1)
                        if u >= 2:
                            act.wait_ge(s_pv, u - 1)
                        full = [kt for kt in x["ktiles"] if kt[1] == P]
                        v = lambda z: z.rearrange("p (k q) -> p k q", q=P)
                        ins = nc.scalar.activation(v(pT[:, u % 2, :])[:, 0:len(full), 0:q],
                                                   v(bank[:, B_PT, 0:3 * P])[:, 0:len(full), 0:q], ACT.Copy)
                        if len(full) < len(x["ktiles"]):
                            kt, n = len(full), x["ktiles"][-1][1]
                            ins = nc.scalar.activation(pT[0:n, u % 2, kt * P:kt * P + q],
                                                       bank[0:n, B_PT, kt * P:kt * P + q], ACT.Copy)
                        ins.then_inc(s_ptc, 1)
                    if i >= 3 and U[i - 3]["last"]:
                        x = U[i - 3]
                        T = T2 if name == "mla" else T1
                        act.wait_ge(s_pv, x["u"] + 1)
                        nc.scalar.activation(oT[:, x["chunk"], 0:T], bank[:, B_O - x["oc"] % 2, 0:T], ACT.Copy)\
                            .then_inc(s_oev, 1)

            act.dma_start(cst[:, :], consts).then_inc(s_const, 16)
            act.dma_start(vec[:, :], vecs).then_inc(s_const, 16)
            act.dma_start(h[:, :, :], hT.rearrange("(c p) t -> p c t", p=P)).then_inc(s_const, 16)
            act.dma_start(late[:, 0:6 * T1], idxc).then_inc(s_idxc, 16)
            act.dma_start(t1[:, 0, 0:T2].bitcast(I32), pos).then_inc(s_pos, 16)

            act.wait_ge(s_ang, 2)
            for i in range(2):
                ins = nc.scalar.activation(cs2[:, i, :], t2[:, i, 0:T2], ACT.Sin)
            ins.then_inc(s_sincos, 1)
            act.wait_ge(s_lbd, 1)
            nc.scalar.activation(lb, lb_t, ACT.Exp).then_inc(s_lbe, 1)
            act.wait_ge(s_lams, 1)
            nc.scalar.activation(lam_e, bank[:, B_PT, 0:2], ACT.Exp).then_inc(s_lame, 1)
            act.wait_ge(s_const, 48)
            norm_h("da", [(s_const, 48)] * 8, T1)
            for j in range(16):
                evict(chunk_of("da_qkv", j), wide[:, j, :])
            for j in range(6):
                g, t = divmod(j, 3)
                evict(chunk_of("da_qkv", 16 + j), v_tok[0:TILES1[t][1], t, g * 512:(g + 1) * 512])
            attention("da", 64 ** -0.5)
            oc0 = att["da"]["units"][0]["oc"]
            for hh in range(9):
                if hh < 8:
                    square(f"o{hh}", [oT[:, hh, :]], [(s_oev, oc0 + hh + 1)])
                if hh >= 1:
                    root(f"o{hh - 1}", T1)
            norm_h("conv0", residual("da_out"), T1)

            def conv_up(i):
                for j in range(KF + 1):
                    if j < KF:
                        for g in range(2):
                            c = chunk_of(f"conv{i}_up", 2 * j + g)
                            n = i * 2 * KF + 2 * j + g
                            ch = j + g * KF
                            act.wait_ge(s_chunk, c + 1)
                            if n >= 4:
                                act.wait_ge(s_hid, (n - 4) // 2 + 1)
                            nc.scalar.activation(conv_buf(n), dense_bank(c)[:, 0:T1], ACT.Identity,
                                                 bias=col("conv_b", i * 44 + ch),
                                                 scale=col("conv_w", (i * 3 + 2) * 44 + ch)).then_inc(s_conv, 1)
                    if j >= 1:
                        n = i * 2 * KF + 2 * (j - 1)
                        c = chunk_of(f"conv{i}_up", 2 * (j - 1))
                        act.wait_ge(s_free["dve"], chunks[c]["nth"] + 1)
                        nc.scalar.activation(silu_buf(n // 2), conv_buf(n), ACT.Silu).then_inc(s_silu, 1)
            conv_up(0)
            norm_h("dsa", residual("conv0_down"), T1)
            for j in range(4):
                evict(chunk_of("dsa_in", j), wide[:, j, :])
            evict(chunk_of("dsa_in", 4), wide[0:64, 4, :])
            square("ki", [wide[0:64, 4, :]], [(s_free["act"], chunks[chunk_of("dsa_in", 4)]["nth"] + 1)], ((0, 64),))
            for t in range(3):
                evict(chunk_of("dsa_in", 5 + t), wi_tok[0:TILES1[t][1], t, :], scale=IDX_HEADS ** -0.5)
            root("ki", T1)
            act.wait_ge(s_rope, ROPE_BASE["idx"] + 5)
            nc.scalar.activation(kT[64:128, 8, :], kT[0:64, 8, :], ACT.Copy).then_inc(s_top, 1)

            def index_relu(x):
                t, hh = divmod(x, 8)
                q0, qn = TILES1[t]
                act.wait_ge(s_idx, x + 1)
                if x >= 2:
                    act.wait_ge(s_idxa, x - 1)
                nc.scalar.activation(pr[0:qn, x % 2, 0:q0 + qn], bank[0:qn, B_S + x % 2, 0:q0 + qn],
                                     ACT.Relu, scale=0.125).then_inc(s_relu, 1)
            for x in range(24):
                index_relu(x)
            for j in range(6):
                g, t = divmod(j, 3)
                evict(chunk_of("dsa_in", 8 + j), v_tok[0:TILES1[t][1], t, g * 512:(g + 1) * 512])
            for j in range(16):
                evict(chunk_of("dsa_in", 14 + j), wide[:, 6 + j, :])
            attention("dsa", 64 ** -0.5)
            act.wait_ge(s_max, att["dsa"]["units"][-1]["scores"][-1] + 1)
            act.dma_start(late[:, 0:EVEN_N], evenc).then_inc(s_even, 16)
            norm_h("conv1", residual("dsa_out"), T1)
            conv_up(1)
            norm_h("final", residual("conv1_down"), T1)
            for c in range(KD):
                act.wait_ge(s_app, norms["final"]["ap"] + c + 1)
                nc.scalar.activation(h[:, c, 0:T2], wide[:, c, 0:T2], ACT.Copy).then_inc(s_final, 1)

            def glu_up(i, j):
                for n in range(KF):
                    c = chunk_of(f"glu{i}{j}_up", 2 * n)
                    g = 2 * KF + (2 * i + j) * KF + n
                    act.wait_ge(s_chunk, c + 1)
                    act.wait_ge(s_hid, g - 1)
                    nc.scalar.activation(silu_buf(g)[:, 0:T2], dense_bank(c)[:, 0:T2], ACT.Silu)\
                        .then_inc(s_free["act"], 1)

            def ple(i, before):
                norm_h(f"pleh{i}", before, T2)
                act.wait_ge(s_free["dve"], before[-1][1])
                act.dma_start(oT[:, 0:2, 0:T2], pT_in[i].rearrange("(c p) t -> p c t", p=P)).then_inc(s_ple, 16)
                for c in range(KD):
                    evict(chunk_of(f"ple{i}_gate", c), wide[:, c, 0:T2], ACT.Sigmoid)
                square(f"pleo{i}", [wide[:, 8 + c, 0:T2] for c in range(KD)], residual(f"ple{i}_proj"), T=T2)
                root(f"pleo{i}", T2)

            norm_h("glu00", [(s_final, c + 1) for c in range(8)], T2)
            glu_up(0, 0)
            norm_h("ev", residual("glu00_down"), T2)
            slot = lambda i: part(i * 1024, 1024)
            for c in range(4):
                evict(chunk_of("ev_in", c), slot(1)[:, c * T2:(c + 1) * T2], ACT.Sigmoid)
            for c in range(4):
                evict(chunk_of("ev_in", 4 + c), slot(0)[:, c * T2:(c + 1) * T2])
            for t in range(2):
                evict(chunk_of("ev_in", 8 + t), slot(11)[:, t * 512:(t + 1) * 512])
            act.wait_ge(s_f, 1)
            nc.scalar.activation(slot(2), slot(3), ACT.Ln).then_inc(s_ln, 1)
            for t in range(2):
                evict(chunk_of("ev_in", 10 + t), slot(14)[:, t * 512:(t + 1) * 512], ACT.Gelu_apprx_tanh)
            for c in range(4):
                evict(chunk_of("ev_in", 12 + c), slot(12)[:, c * T2:(c + 1) * T2], ACT.Gelu_apprx_tanh)
            for c in range(4):
                evict(chunk_of("ev_in", 16 + c), slot(13)[:, c * T2:(c + 1) * T2], ACT.Silu)
            act.wait_ge(s_vms, 1)
            nc.scalar.activation(vms, vms, ACT.Sqrt).then_inc(s_vrs, 1)
            for lv in range(1, 7):
                act.wait_ge(s_lvd, lv)
                e = slot(4 + lv % 2)
                nc.scalar.activation(e, e, ACT.Exp).then_inc(s_lve, 1)
            act.wait_ge(s_lvd, 7)
            nc.scalar.activation(e_last, slot(2).rearrange("p (n c) -> p n c", c=CHUNK)[:, :, CHUNK - 1], ACT.Exp)
            nc.scalar.activation(slot(4), slot(2), ACT.Exp)
            nc.scalar.activation(slot(5), slot(5), ACT.Exp).then_inc(s_lve, 1)
            for t in range(2):
                act.wait_ge(s_kkt, t + 1)
                nc.scalar.activation(slot(14)[:, t * 512:(t + 1) * 512], bank[:, B_PT, :], ACT.Copy)\
                    .then_inc(s_kkc, 1)
            for hh in range(4):
                act.wait_ge(s_hgo, 2 * (hh // 2) + 2)
                o = (hh % 2) * T2
                nc.scalar.activation(slot(3)[:, hh * T2:(hh + 1) * T2], bank[:, B_COL + hh // 2, o:o + T2], ACT.Copy)\
                    .then_inc(s_hge, 1)
            for hh in range(5):
                if hh < 4:
                    square(f"hg{hh}", [slot(3)[:, hh * T2:(hh + 1) * T2]], [(s_hge, hh + 1)], T=T2)
                if hh >= 1:
                    root(f"hg{hh - 1}", T2)
            norm_h("glu01", residual("ev_out"), T2)
            glu_up(0, 1)
            ple(0, residual("glu01_down"))
            norm_h("glu10", [(s_final, 8 + c + 1) for c in range(8)], T2)
            glu_up(1, 0)
            norm_h("mla", residual("glu10_down"), T2)
            for c in range(5):
                evict(chunk_of("mla_in", c), wide[:, c, 0:T2])
            c5 = chunk_of("mla_in", 5)
            evict(c5, wide[0:64, 5, 0:T2], last=False)
            evict(c5, wide[64:128, 5, 0:T2], src=dense_bank(c5)[0:64, 0:T2])
            f0 = chunks[chunk_of("mla_in", 0)]["nth"]
            square("cq", [wide[:, c, 0:T2] for c in range(3)], [(s_free["act"], f0 + 1 + c) for c in range(3)], T=T2)
            square("ckv", [wide[:, 3 + c, 0:T2] for c in range(2)], [(s_free["act"], f0 + 4 + c) for c in range(2)],
                   T=T2)
            root("cq", T2)
            root("ckv", T2)
            for g in range(2):
                for x in range(4):
                    evict(chunk_of("mla_q", 6 * g + x), wide[:, 6 + 4 * g + x, 0:T2])
                for r in range(2):
                    evict(chunk_of("mla_q", 6 * g + 4 + r), wide[:, 14 + 2 * g + r, 0:T2])
            for hh in range(8):
                evict(chunk_of("mla_kv", hh), kT[:, hh, 0:T2])
            for j in range(4):
                g, t = divmod(j, 2)
                evict(chunk_of("mla_kv", 8 + j), v_tok[:, t, g * 512:(g + 1) * 512])
            fq = [chunks[chunk_of("mla_q", j)]["nth"] + 1 for j in range(12)]
            fk = [chunks[chunk_of("mla_kv", j)]["nth"] + 1 for j in range(8)]
            heads = []
            for hh in range(8):
                a = 64 * (hh % 2)
                heads.append((f"q{hh}", [wide[:, 6 + hh, 0:T2], wide[a:a + 64, 14 + hh // 2, 0:T2]],
                              [(s_free["act"], fq[6 * (hh // 4) + hh % 4]), (s_free["act"], fq[11])], a))
            for hh in range(8):
                a = 64 * (hh % 2)
                heads.append((f"k{hh}", [kT[:, hh, 0:T2], wide[a:a + 64, 5, 0:T2]],
                              [(s_free["act"], fk[hh]), (s_free["act"], f0 + 6)], a))
            for i in range(17):
                if i < 16:
                    n_, src, rd, a = heads[i]
                    square(n_, src, rd, ((0, P), (a, 64)), T=T2)
                if i >= 1:
                    root(heads[i - 1][0], T2)
            attention("mla", 192 ** -0.5)
            norm_h("glu11", residual("mla_out"), T2)
            glu_up(1, 1)
            ple(1, residual("glu11_down"))

        @block.gpsimd
        def _(pool):
            def cos_part(r, raw, table, T, ready, rows=P):
                pool.wait_ge(*ready)
                if r >= 2:
                    pool.wait_ge(s_rope, r - 1)
                nc.gpsimd.tensor_tensor(t1[0:rows, r % 2, 0:T], raw, table[0:rows, 0:T], ALU.mult).then_inc(s_t1, 1)

            def act_chunk(c):
                return (s_free["act"], chunks[c]["nth"] + 1)

            pool.wait_ge(s_const, 48)
            pool.wait_ge(s_ang, 2)
            for j in range(16):
                cos_part(j, wide[:, j, :], cos1, T1, act_chunk(chunk_of("da_qkv", j)))
            for j in range(4):
                cos_part(ROPE_BASE["idx"] + j, wide[:, j, :], cos1, T1, act_chunk(chunk_of("dsa_in", j)))
            cos_part(ROPE_BASE["idx"] + 4, wide[0:64, 5, :], cos1, T1, (s_app, norms["ki"]["ap"] + 1), 64)
            for j in range(16):
                cos_part(ROPE_BASE["dsa"] + j, wide[:, 6 + j, :], cos1, T1, act_chunk(chunk_of("dsa_in", 14 + j)))
            pool.wait_ge(s_even, 16)
            wsT = even("wsT").rearrange("p (h t) -> p h t", h=8)
            nc.gpsimd.affine_select(out=wsT, in_=wsT, compare_op=ALU.is_ge, fill=0.0, base=0,
                                    pattern=[[0, 8], [1, P]], channel_multiplier=-1).then_inc(s_ws, 1)
            pool.wait_ge(s_sincos, 1)
            cos_part(ROPE_BASE["kr"], oT[:, 6, 0:T2], cs2[:, 0, :], T2, (s_kr, 1))
            for r in range(4):
                cos_part(ROPE_BASE["mq"] + r, wide[:, 14 + r, 0:T2], cs2[:, 0, :], T2,
                         (s_app, norms[f"q{2 * r + 1}"]["ap"] + 2))

        @block.vector
        def _(dve):
            V = nc.vector

            def step(ins):
                step.n += 1
                ins.then_inc(s_dve, 1)
                dve.wait_ge(s_dve, step.n)
            step.n = 0

            def norm_inv(name, T, dim):
                m = norms[name]
                b = rinv[:, m["id"] % 2, 0:T]
                dve.wait_ge(s_col, m["id"] + 1)
                if m["id"] >= 2:
                    dve.wait_ge(s_rstd, m["id"] - 1)
                step(V.tensor_scalar(b, bank[:, B_COL, 0:T], 1.0 / dim, EPS, ALU.mult, ALU.add))
                V.reciprocal(b, b).then_inc(s_rinv, 1)

            def norm_apply(name, T, ops, shift=0):
                m = norms[name]
                dve.wait_ge(s_rstd, m["id"] + 1)
                for o, s, g, a, n in ops:
                    V.scalar_tensor_tensor(out=o, in0=s, scalar=g, in1=rstd[a:a + n, m["id"] % 2, shift:shift + T],
                                           op0=ALU.mult, op1=ALU.mult).then_inc(s_app, 1)

            def norm_h(name, T, gain, at):
                norm_inv(name, T, D)
                norm_apply(name, T, [(hn[:, c, 0:T], h[:, c, 0:T], col(gain, at + c), 0, P) for c in range(KD)])

            def residual(stage, T, scale=None):
                for i in range(8):
                    c = chunk_of(stage, i)
                    dve.wait_ge(s_chunk, c + 1)
                    src, dst = dense_bank(c)[:, 0:T], h[:, i, 0:T]
                    if scale is None:
                        ins = V.tensor_tensor(dst, src, dst, ALU.add)
                    else:
                        ins = V.scalar_tensor_tensor(out=dst, in0=src, scalar=scale, in1=dst, op0=ALU.mult,
                                                     op1=ALU.add)
                    ins.then_inc(s_free["dve"], 1)

            def rope(r, out_, table, T, rows=P):
                dve.wait_ge(s_rot, r + 1)
                step(V.tensor_tensor(t2[0:rows, r % 2, 0:T], bank[0:rows, B_S + r % 2, 0:T], table[0:rows, 0:T],
                                     ALU.mult))
                dve.wait_ge(s_t1, r + 1)
                V.tensor_tensor(out_, t1[0:rows, r % 2, 0:T], t2[0:rows, r % 2, 0:T], ALU.add).then_inc(s_rope, 1)

            def attention(name, scale, mask):
                U = att[name]["units"]
                for i in range(len(U) + 1):
                    if i < len(U):
                        x = U[i]
                        q, k = x["qn"], x["kn"]
                        for s in x["scores"]:
                            dve.wait_ge(s_score, s + 1)
                            if s >= 4:
                                dve.wait_ge(s_exp, s - 3)
                            step(V.tensor_tensor_reduce(sm[0:q, s % 4, 0:k], bank[0:q, B_S + s % 2, 0:k],
                                                        mask[0:q, x["t"], 0:k], 1.0, -3e38, ALU.add, ALU.max,
                                                        mx[0:q, s % 8:s % 8 + 1]))
                            V.tensor_scalar(nmx[0:q, s % 8:s % 8 + 1], mx[0:q, s % 8:s % 8 + 1], -scale, None,
                                            ALU.mult).then_inc(s_max, 1)
                    if i >= 1:
                        x = U[i - 1]
                        q, k, u = x["qn"], x["kn"], x["u"]
                        s = x["scores"]
                        dve.wait_ge(s_exp, s[-1] + 1)
                        if u >= 2:
                            dve.wait_ge(s_tr, u - 1)
                        a = s[0] % 8
                        step(V.reciprocal(rs[0:q, a:a + len(s)], ssum[0:q, a:a + len(s)]))
                        if len(s) == 1:
                            V.tensor_scalar(pn[0:q, u % 2, 0:k], pr[0:q, s[0] % 4, 0:k], rs[0:q, a:a + 1], None,
                                            ALU.mult).then_inc(s_prob, 1)
                        else:
                            step(V.tensor_scalar(rl[0:q], rs[0:q, a + 1:a + 2], lam[0:q], None, ALU.mult))
                            p1 = pr[0:q, s[1] % 4, 0:k]
                            step(V.tensor_scalar(p1, p1, rl[0:q], None, ALU.mult))
                            V.scalar_tensor_tensor(out=pn[0:q, u % 2, 0:k], in0=pr[0:q, s[0] % 4, 0:k],
                                                   scalar=rs[0:q, a:a + 1], in1=p1, op0=ALU.mult,
                                                   op1=ALU.subtract).then_inc(s_prob, 1)

            dve.wait_ge(s_pos, 16)
            dve.wait_ge(s_const, 48)
            ang, kf = t1[:, 1, 0:T2], rinv[:, 0, 0:T2]
            step(V.tensor_copy(ang, t1[:, 0, 0:T2].bitcast(I32)))
            step(V.tensor_scalar(ang, ang, con("inv"), None, ALU.mult))
            magic = float(1.5 * 2 ** 23)
            for i, shift in enumerate((0.25, 0.0)):
                r = t2[:, i, 0:T2]
                step(V.tensor_scalar(kf, ang, 1.0 / TWO_PI, shift, ALU.mult, ALU.add))
                step(V.tensor_scalar(kf, kf, magic, None, ALU.add))
                step(V.tensor_scalar(kf, kf, -magic, -shift, ALU.add, ALU.add))
                c1 = 6.28125
                c2 = float(np.float32(np.round((TWO_PI - c1) * 2 ** 19) / 2 ** 19))
                c3 = float(np.float32(TWO_PI - c1 - c2))
                src = ang
                for cc in (c1, c2, c3):
                    step(V.scalar_tensor_tensor(out=r, in0=kf, scalar=-cc, in1=src, op0=ALU.mult, op1=ALU.add))
                    src = r
                V.tensor_scalar(r, r, float(np.float32(3.1415925)), -float(np.float32(3.1415925)),
                                ALU.min, ALU.max).then_inc(s_ang, 1)
            la = VEC_AT["lam"][0]
            V.tensor_tensor(lam_p[0:64, :], vec[0:64, la:la + 2], vec[0:64, la + 2:la + 4], ALU.mult)\
                .then_inc(s_lam, 1)
            V.tensor_scalar(subln8, col("subln"), 1.0 - LAMBDA_INIT, None, ALU.mult)
            lr = vec[:, VEC_AT["lb_raw"][0]:VEC_AT["lb_raw"][0] + 4]
            V.tensor_tensor(lb_t, lr, lr, ALU.subtract).then_inc(s_lbd, 1)
            dve.wait_ge(s_lbe, 1)
            step(V.reciprocal(oml, lb))
            step(V.tensor_tensor(lb_t, lb, oml, ALU.mult))
            step(V.tensor_tensor(lb, lb_t, lb_t, ALU.subtract))
            step(V.tensor_scalar(lb, lb, 0.0, 0.999, ALU.max, ALU.min))
            step(V.tensor_scalar(oml, lb, -1.0, 1.0, ALU.mult, ALU.add))
            dve.wait_ge(s_lame, 1)
            step(V.tensor_tensor(lam, lam_e[:, 0:1], lam_e[:, 1:2], ALU.subtract))
            step(V.tensor_scalar(lam, lam, LAMBDA_INIT, None, ALU.add))

            norm_h("da", T1, "da_norm", 0)
            for j in range(16):
                rope(j, (qT if j < 8 else kT)[:, j % 8, :], sin1, T1)
            attention("da", 64 ** -0.5, causal)
            for hh in range(9):
                if hh < 8:
                    norm_inv(f"o{hh}", T1, P)
                if hh >= 1:
                    o = oT[:, hh - 1, :]
                    norm_apply(f"o{hh - 1}", T1, [(o, o, subln8, 0, P)])
            residual("da_out", T1)
            norm_h("conv0", T1, "ffn_norm", 0)

            def conv_up(i):
                for j in range(KF + 1):
                    if j < KF:
                        for g in range(2):
                            c = chunk_of(f"conv{i}_up", 2 * j + g)
                            n = i * 2 * KF + 2 * j + g
                            ch = j + g * KF
                            cb, b = conv_buf(n), dense_bank(c)
                            dve.wait_ge(s_conv, n + 1)
                            step(V.scalar_tensor_tensor(out=cb[:, 1:T1], in0=b[:, 0:T1 - 1],
                                                        scalar=col("conv_w", (i * 3 + 1) * 44 + ch),
                                                        in1=cb[:, 1:T1], op0=ALU.mult, op1=ALU.add))
                            V.scalar_tensor_tensor(out=cb[:, 2:T1], in0=b[:, 0:T1 - 2],
                                                   scalar=col("conv_w", (i * 3) * 44 + ch), in1=cb[:, 2:T1],
                                                   op0=ALU.mult, op1=ALU.add).then_inc(s_free["dve"], 1)
                    if j >= 1:
                        n = i * 2 * KF + 2 * (j - 1)
                        dve.wait_ge(s_silu, n // 2 + 1)
                        c = chunk_of(f"conv{i}_up", 2 * (j - 1) + 1)
                        dve.wait_ge(s_free["dve"], chunks[c]["nth"] + 1)
                        V.tensor_tensor(wide[:, j - 1, :], silu_buf(n // 2), conv_buf(n + 1), ALU.mult)\
                            .then_inc(s_hid, 1)
            conv_up(0)
            residual("conv0_down", T1)

            norm_h("dsa", T1, "dsa_norm", 0)
            for j in range(4):
                rope(ROPE_BASE["idx"] + j, qT[:, 8 + j, :], sin1, T1)
            norm_inv("ki", T1, 64)
            norm_apply("ki", T1, [(wide[0:64, 5, :], wide[0:64, 4, :], col("idxk", 0, 0, 64), 0, 64)])
            rope(ROPE_BASE["idx"] + 4, kT[0:64, 8, :], sin1, T1, 64)
            work = sm
            f5 = chunks[chunk_of("dsa_in", 7)]["nth"] + 1
            dve.wait_ge(s_free["act"], f5)
            for x in range(24):
                t, hh = divmod(x, 8)
                q0, q = TILES1[t]
                k = q0 + q
                dve.wait_ge(s_relu, x + 1)
                rx, w = pr[0:q, x % 2, 0:k], wi_tok[0:q, t, hh:hh + 1]
                acc = work[0:q, t, 0:k]
                if hh == 0:
                    ins = V.tensor_scalar(acc, rx, w, None, ALU.mult)
                else:
                    ins = V.scalar_tensor_tensor(out=acc, in0=rx, scalar=w, in1=acc, op0=ALU.mult, op1=ALU.add)
                ins.then_inc(s_idxa, 1)
                dve.wait_ge(s_idxa, x + 1)
            dve.wait_ge(s_idxc, 16)
            for t, (q0, q) in enumerate(TILES1):
                k = q0 + q
                a, b = work[0:q, t, 0:k], work[0:q, 3, 0:k]
                step(V.tensor_tensor(a, a, keep[0:q, t, 0:k], ALU.mult))
                step(V.tensor_tensor(a, a, addm[0:q, t, 0:k], ALU.add))
                for r in range(TOPK // 8):
                    step(V.max(max8[0:q], a))
                    step(V.match_replace(b, max8[0:q], a, -3e38))
                    a, b = b, a
                step(V.tensor_scalar(b, a, -2e38, NEG, ALU.is_gt, ALU.mult))
                step(V.tensor_tensor(amask[0:q, t, 0:k], b, causal[0:q, t, 0:k], ALU.add))
            for j in range(16):
                rope(ROPE_BASE["dsa"] + j, (qT if j < 8 else kT)[:, j % 8, :], sin1, T1)
            attention("dsa", 64 ** -0.5, amask)
            residual("dsa_out", T1)
            norm_h("conv1", T1, "ffn_norm", 8)
            conv_up(1)
            residual("conv1_down", T1)
            norm_inv("final", T1, D)
            norm_apply("final", T2, [(wide[:, c, 0:T2], h[:, c, META:T1], col("final", c), 0, P) for c in range(KD)],
                       shift=META)

            def glu(i, j):
                norm_h(f"glu{i}{j}", T2, "gains", 8 * (5 * i + 2 * j))
                for n in range(KF):
                    c = chunk_of(f"glu{i}{j}_up", 2 * n)
                    g = 2 * KF + (2 * i + j) * KF + n
                    dve.wait_ge(s_free["act"], chunks[c]["nth"] + 1)
                    dve.wait_ge(s_chunk, c + 2)
                    V.tensor_tensor(wide[:, n, 0:T2], dense_bank(c + 1)[:, 0:T2], silu_buf(g)[:, 0:T2], ALU.mult)\
                        .then_inc(s_hid, 1)
                residual(f"glu{i}{j}_down", T2, 0.5)

            def ple(i):
                norm_h(f"pleh{i}", T2, "gains", 8 * (5 * i + 3))
                for c in range(KD):
                    cc = chunk_of(f"ple{i}_proj", c)
                    dve.wait_ge(s_chunk, cc + 1)
                    dve.wait_ge(s_free["act"], chunks[chunk_of(f"ple{i}_gate", c)]["nth"] + 1)
                    V.tensor_tensor(wide[:, 8 + c, 0:T2], dense_bank(cc)[:, 0:T2], wide[:, c, 0:T2], ALU.mult)\
                        .then_inc(s_free["dve"], 1)
                norm_inv(f"pleo{i}", T2, D)
                norm_apply(f"pleo{i}", T2, [(wide[:, c, 0:T2], wide[:, 8 + c, 0:T2],
                                             col("gains", 8 * (5 * i + 4) + c), 0, P) for c in range(KD)])
                for c in range(KD):
                    dve.wait_ge(s_app, norms[f"pleo{i}"]["ap"] + c + 1)
                    V.tensor_tensor(h[:, c, 0:T2], wide[:, c, 0:T2], h[:, c, 0:T2], ALU.add).then_inc(s_final, 1)

            dve.wait_ge(s_final, 8)
            glu(0, 0)
            norm_h("ev", T2, "gains", 8)
            slot = lambda i: part(i * 1024, 1024)
            n0 = chunks[chunk_of("ev_in", 0)]["nth"]
            dve.wait_ge(s_free["act"], n0 + 4)
            sig, kf_ = slot(1), slot(3)
            for hh in range(4):
                ps_ = slice(hh * T2, (hh + 1) * T2)
                ins = V.tensor_scalar(sig[:, ps_], sig[:, ps_], oml[:, hh:hh + 1], lb[:, hh:hh + 1], ALU.mult, ALU.add)
            step(ins)
            V.tensor_scalar(kf_, sig, 1e-6, None, ALU.max).then_inc(s_f, 1)
            dve.wait_ge(s_f, 1)
            V.tensor_scalar(sig, sig, -1.0, 1.0, ALU.mult, ALU.add).then_inc(s_lvq, 1)
            dve.wait_ge(s_lvq, 1)
            dve.wait_ge(s_free["act"], n0 + 8)
            dve.wait_ge(s_ln, 1)
            a, b = 2, 3
            c64 = lambda i: slot(i).rearrange("p (n c) -> p n c", c=CHUNK)
            for s in (1, 2, 4, 8, 16, 32):
                V.tensor_copy(c64(b)[:, :, 0:s], c64(a)[:, :, 0:s])
                step(V.tensor_tensor(c64(b)[:, :, s:CHUNK], c64(a)[:, :, s:CHUNK], c64(a)[:, :, 0:CHUNK - s],
                                     ALU.add))
                a, b = b, a
            assert a == 2
            lmask = even("lmask").rearrange("p (l t) -> p l t", l=7)
            scT = part(10 * 1024, 1024, 512)
            tmp = pT[:, :, :].rearrange("p a b -> p (a b)")[:, 0:512]
            dve.wait_ge(s_even, 16)

            def add_level(lv):
                for t in range(2):
                    dve.wait_ge(s_lvm, 2 * lv + t + 1)
                    v3 = lambda z: z.rearrange("p (h t) -> p h t", h=4)
                    mk = lmask[:, lv:lv + 1, :].to_broadcast([P, 4, P])
                    if lv == 0:
                        V.tensor_tensor(v3(scT[:, t, :]), v3(bank[:, B_S + t, :]), mk, ALU.mult).then_inc(s_lva, 1)
                    else:
                        step(V.tensor_tensor(v3(tmp), v3(bank[:, B_S + t, :]), mk, ALU.mult))
                        V.tensor_tensor(scT[:, t, :], scT[:, t, :], tmp, ALU.add).then_inc(s_lva, 1)
                    dve.wait_ge(s_lva, 2 * lv + t + 1)

            def exponents(lv):
                m = LEVELS[lv - 1]
                v = lambda i: slot(i).rearrange("p (n s m) -> p n s m", s=2, m=m)
                e, bb = v(4 + lv % 2), v(2)
                nb = 512 // m
                ref = bb[:, :, 0, m - 1:m].to_broadcast([P, nb, m])
                V.tensor_tensor(e[:, :, 0, :], ref, bb[:, :, 0, :], ALU.subtract)
                V.tensor_tensor(e[:, :, 1, :], bb[:, :, 1, :], ref, ALU.subtract).then_inc(s_lvd, 1)

            def operands(lv):
                dve.wait_ge(s_lve, lv)
                if lv >= 3:
                    dve.wait_ge(s_lvm, 2 * (lv - 2) + 2)
                V.tensor_tensor(slot(6 + lv % 2), slot(0), slot(4 + lv % 2), ALU.mult)
                V.tensor_tensor(slot(8 + lv % 2), slot(1), slot(4 + lv % 2), ALU.mult).then_inc(s_lvq, 1)

            exponents(1)
            gv = slot(14)
            dve.wait_ge(s_free["act"], n0 + 12)
            step(V.tensor_tensor(slot(10), gv, gv, ALU.mult))
            step(V.tensor_reduce(vms, slot(10).rearrange("p (g d) -> p g d", d=64), AX.X, ALU.add))
            step(V.tensor_scalar(vms, vms, 1.0 / 64, EPS, ALU.mult, ALU.add))
            V.reciprocal(vms, vms).then_inc(s_vms, 1)
            dve.wait_ge(s_vrs, 1)
            g64 = lambda z: z.rearrange("p (g d) -> p g d", d=64)
            step(V.tensor_tensor(g64(gv), g64(gv), vms.rearrange("p (g o) -> p g o", o=1).to_broadcast([P, 16, 64]),
                                 ALU.mult))
            vn = even("vnorm")
            for t in range(2):
                ins = V.tensor_tensor(gv[:, t * 512:(t + 1) * 512], gv[:, t * 512:(t + 1) * 512], vn, ALU.mult)
            ins.then_inc(s_gv, 1)
            add_level(0)
            for lv in range(1, 7):
                if lv < 6:
                    exponents(lv + 1)
                operands(lv)
                add_level(lv)
            c5_, b5 = c64(5), c64(2)
            V.tensor_tensor(c5_, b5[:, :, CHUNK - 1:CHUNK].to_broadcast([P, 16, CHUNK]), b5, ALU.subtract)\
                .then_inc(s_lvd, 1)
            dve.wait_ge(s_lve, 7)
            V.tensor_tensor(slot(6), slot(0), slot(4), ALU.mult)
            V.tensor_tensor(slot(7), slot(1), slot(5), ALU.mult).then_inc(s_gate, 1)
            bs = even("bs").rearrange("p (c t) -> p c t", c=4)
            gu = slot(12).rearrange("p (c t) -> p c t", c=4)
            dve.wait_ge(s_free["act"], n0 + 16)
            for t in range(2):
                dve.wait_ge(s_mixp, t + 1)
                v3 = lambda z: z.rearrange("p (h t) -> p h t", h=4)
                step(V.tensor_tensor(v3(tmp), v3(bank[:, B_COL + t, :]), bs, ALU.add))
                V.tensor_tensor(oT[:, 0:4, t * P:(t + 1) * P], v3(tmp), gu[:, :, t * P:(t + 1) * P], ALU.mult)\
                    .then_inc(s_mix, 1)
                dve.wait_ge(s_mix, t + 1)
            states = part(8 * 1024, 1536, 512)
            el = e_last.rearrange("p (h n) -> p h n", h=4)
            for n in range(3):
                dve.wait_ge(s_upd, n + 1)
                v3 = lambda z: z.rearrange("p (h t) -> p h t", h=4)
                if n == 0:
                    V.tensor_copy(states[:, 0, :], bank[:, B_S, :]).then_inc(s_st, 1)
                else:
                    step(V.tensor_tensor(v3(tmp), v3(states[:, n - 1, :]), el[:, :, n:n + 1].to_broadcast([P, 4, P]),
                                         ALU.mult))
                    V.tensor_tensor(states[:, n, :], bank[:, B_S + n % 2, :], tmp, ALU.add).then_inc(s_st, 1)
                dve.wait_ge(s_st, n + 1)
            dve.wait_ge(s_free["act"], n0 + 20)
            for hh in range(5):
                if hh < 4:
                    norm_inv(f"hg{hh}", T2, P)
                if hh >= 1:
                    i = hh - 1
                    o = slot(3)[:, i * T2:(i + 1) * T2]
                    norm_apply(f"hg{i}", T2, [(o, o, col("hg_out"), 0, P)])
                    dve.wait_ge(s_app, norms[f"hg{i}"]["ap"] + 1)
                    V.tensor_tensor(oT[:, 4 + i, 0:T2], o, slot(13)[:, i * T2:(i + 1) * T2], ALU.mult)\
                        .then_inc(s_gate, 1)
            residual("ev_out", T2)
            glu(0, 1)
            ple(0)
            glu(1, 0)
            norm_h("mla", T2, "gains", 8 * 6)
            norm_inv("cq", T2, 384)
            norm_inv("ckv", T2, 256)
            norm_apply("cq", T2, [(hn[:, c, 0:T2], wide[:, c, 0:T2], col("qa", c), 0, P) for c in range(3)])
            norm_apply("ckv", T2, [(hn[:, 3 + c, 0:T2], wide[:, 3 + c, 0:T2], col("kva", c), 0, P) for c in range(2)])
            f0 = chunks[chunk_of("mla_in", 0)]["nth"]
            dve.wait_ge(s_free["act"], f0 + 6)
            V.tensor_scalar(oT[:, 6, 0:T2], wide[:, 5, 0:T2], col("kr"), None, ALU.mult).then_inc(s_kr, 1)
            dve.wait_ge(s_sincos, 1)
            rope(ROPE_BASE["kr"], oT[:, 7, 0:T2], cs2[:, 1, :], T2)
            dve.wait_ge(s_rope, ROPE_BASE["kr"] + 1)
            heads = []
            for hh in range(8):
                a = 64 * (hh % 2)
                heads.append((f"q{hh}", [(qT[:, hh, 0:T2], wide[:, 6 + hh, 0:T2], col("qn"), 0, P),
                                         (wide[a:a + 64, 14 + hh // 2, 0:T2], wide[a:a + 64, 14 + hh // 2, 0:T2],
                                          col("qr", 0, a, 64), a, 64)]))
            for hh in range(8):
                a = 64 * (hh % 2)
                heads.append((f"k{hh}", [(kT[:, hh, 0:T2], kT[:, hh, 0:T2], col("kn"), 0, P),
                                         (kT[a:a + 64, 8 + hh // 2, 0:T2], oT[a:a + 64, 7, 0:T2],
                                          1.0, a, 64)]))
            for i in range(17):
                if i < 16:
                    norm_inv(heads[i][0], T2, 192)
                if i >= 1:
                    norm_apply(heads[i - 1][0], T2, heads[i - 1][1])
            for r in range(4):
                rope(ROPE_BASE["mq"] + r, qT[:, 8 + r, 0:T2], cs2[:, 1, :], T2)
            attention("mla", 192 ** -0.5, causal)
            residual("mla_out", T2)
            glu(1, 1)
            ple(1)


WEIGHTS = [("da_w_qkv", "da_w_qkv"), ("da_w_o", "da_w_o"), ("dsa_w_in", "dsa_w_in"), ("dsa_w_o", "dsa_w_o"),
           ("ffn_w_up", "ffn_w_up"), ("ffn_w_down", "ffn_w_down"), ("ffn_w_gate", "ffn_w_gate_2"),
           ("ffn_w_up_2", "ffn_w_up_2"), ("ffn_w_down_2", "ffn_w_down_2"), ("ple_w_gate", "ple_w_gate_2"),
           ("ple_w_proj", "ple_w_proj_2"), ("even_w_in", "even_w_in_2"), ("even_w_out", "even_w_out_2"),
           ("mla_w_in", "mla_w_in_2"), ("mla_w_q_b", "mla_w_q_b_2"), ("mla_w_kv_b", "mla_w_kv_b_2"),
           ("mla_w_out", "mla_w_out_2")]


def kernel(**inputs):
    import concourse.bacc as bacc
    from concourse.bass_utils import run_bass_kernel_spmd

    a = {k: np.asarray(v) for k, v in inputs.items()}

    def cols(v):
        return v.reshape(-1, P).T

    def twice(v):
        return np.concatenate([v, v]).reshape(P, 1)

    sc = shape_constants()
    z = np.zeros((64,), np.float32)
    pad = lambda v: np.concatenate([v.reshape(-1), z]).reshape(P, 1)
    v = {
        "da_norm": cols(a["da_norm"]), "subln": cols(a["da_subln"]), "dsa_norm": cols(a["dsa_norm"]),
        "idxk": pad(a["dsa_idx_k_norm"]), "ffn_norm": cols(a["ffn_norm"]), "conv_w": cols(a["ffn_conv_w"]),
        "conv_b": cols(a["ffn_conv_b"]), "final": cols(a["final_norm"]), "gains": cols(a["norm_gains_2"]),
        "lb_raw": cols(a["hgrn_lb_raw_2"]), "hg_out": cols(a["hgrn_out_norm_2"]), "qa": cols(a["mla_q_a_norm_2"]),
        "kva": cols(a["mla_kv_a_norm_2"]), "qn": cols(a["mla_q_norm_2"][0, 0:P]), "qr": twice(a["mla_q_norm_2"][0, P:]),
        "kn": cols(a["mla_k_norm_2"][0, 0:P]), "kr": twice(a["mla_k_norm_2"][0, P:]),
        "lam": np.concatenate([pad(a[f"da_lambda_{n}"][0]) for n in ("q1", "q2", "k1", "k2")], 1),
    }
    bs = a["gmlp_b_s_2"][0].reshape(4, 2, 1, P)
    e = {
        "lmask": level_masks(),
        "wsT": a["gmlp_w_s_2"][0].transpose(2, 0, 1).reshape(P, -1),
        "bs": np.broadcast_to(bs, (4, 2, 64, P)).transpose(1, 2, 0, 3).reshape(P, -1),
        "vnorm": np.broadcast_to(a["gmlp_v_norm_2"][0].reshape(1, -1), (P, 512)),
    }
    arrays = {
        "hT": np.concatenate([a["meta_tokens"], a["x"][0]], 0).T,
        "consts": np.concatenate([sc[n] for n, _ in CONST_PARTS], 1),
        "idxc": index_constants(),
        "vecs": np.concatenate([v[n] for n, _ in VEC_PARTS], 1),
        "evenc": np.concatenate([e[n] for n, _ in EVEN_PARTS], 1),
        "pleT": a["p_2"][:, 0].transpose(0, 2, 1),
        "pos": np.broadcast_to(a["positions_2"].reshape(1, -1), (P, T2)),
    }
    for name, src in WEIGHTS:
        arrays["w_" + name] = a[src]
    arrays = {k: np.ascontiguousarray(x) for k, x in arrays.items()}

    nc = bacc.Bacc("TRN2", target_bir_lowering=False, num_devices=1)
    ap = {k: nc.dram_tensor(k, x.shape, mybir.dt.from_np(x.dtype), kind="ExternalInput").ap()
          for k, x in arrays.items()}
    out = nc.dram_tensor("outT", (D, T2), F32, kind="ExternalOutput").ap()
    build(nc, {n: ap["w_" + n] for n, _ in WEIGHTS}, ap["hT"], ap["consts"], ap["idxc"], ap["vecs"], ap["evenc"],
          ap["pleT"], ap["pos"], out)
    r = run_bass_kernel_spmd(nc, [arrays], core_ids=[0])
    return r.results[0]["outT"].T[None].copy()
```

```python
from contextlib import ExitStack

import numpy as np
import concourse.bass as bass
from concourse import mybir

F32 = mybir.dt.float32
F32R = mybir.dt.float32r
I32 = mybir.dt.int32
ACT = mybir.ActivationFunctionType
ALU = mybir.AluOpType
AX = mybir.AxisListType

P = 128
D = 1024
KD = D // P
META = 16
T2 = 256
T1 = T2 + META
F = 2816
KF = F // P
EPS = 1e-6
THETA = 10000.0
NEG = -1e30
LAMBDA_INIT = 0.2
TOPK = 64
IDX_HEADS = 8
CHUNK = 64
TILES1 = [(0, 128), (128, 128), (256, 16)]
TILES2 = [(0, 128), (128, 128)]
SLOT = 2048
RAW = 3
SPLIT = 3
AHEAD = 2
DENSE_BANKS = 3
B_COL, B_O, B_S, B_PT = 3, 4, 5, 7
SQ_SLOTS = 8
MASK_AT = (0, 128, 384)
MASK_N = 656
TWO_PI = 2.0 * np.pi


def shape_constants():
    c = {}
    c["ident"] = np.eye(P, dtype=np.float32)
    c["ones"] = np.ones((P, P), np.float32)
    rot = np.zeros((P, P), np.float32)
    for i in range(P):
        if i % 64 < 32:
            rot[i + 32, i] = -1.0
        else:
            rot[i - 32, i] = 1.0
    c["rot"] = rot
    inv = np.float32(THETA) ** (-np.arange(0, 64, 2, dtype=np.float32) / np.float32(64))
    ang = np.arange(T1, dtype=np.float32)[None, :] * inv.astype(np.float32)[:, None]
    c["cos"] = np.tile(np.cos(ang), (4, 1)).astype(np.float32)
    c["sin"] = np.tile(np.sin(ang), (4, 1)).astype(np.float32)
    c["inv"] = np.tile(inv[:, None], (4, 1)).astype(np.float32)
    q = np.arange(P)[:, None, None] + 128 * np.arange(3)[None, :, None]
    k = np.arange(T1)[None, None, :]
    causal = k <= q
    c["causal"] = packed(np.where(causal, 0.0, NEG))
    return c


def packed(m):
    return np.concatenate([m[:, t, :q0 + qn] for t, (q0, qn) in enumerate(TILES1)], 1).astype(np.float32)


def index_constants():
    q = np.arange(P)[:, None, None] + 128 * np.arange(3)[None, :, None]
    k = np.arange(T1)[None, None, :]
    causal = k <= q
    keep = causal & (k >= META)
    add = np.where(causal, np.where(k < META, 1e30, 0.0), -1e38)
    return np.concatenate([packed(keep), packed(add)], 1)


def level_masks():
    s = np.arange(P)[:, None]
    t = np.arange(P)[None, :]
    out = [(s == t)]
    for m in LEVELS:
        out.append((s // (2 * m) == t // (2 * m)) & (s % (2 * m) < m) & (t % (2 * m) >= m))
    return np.concatenate(out, 1).astype(np.float32)


LEVELS = [32, 16, 8, 4, 2, 1]

CONST_PARTS = [("ident", P), ("ones", P), ("rot", P), ("cos", T1), ("sin", T1), ("inv", 1), ("causal", MASK_N)]
VEC_PARTS = [("da_norm", 8), ("subln", 1), ("dsa_norm", 8), ("idxk", 1), ("ffn_norm", 16), ("conv_w", 2 * 3 * 44),
             ("conv_b", 2 * 44), ("final", 8), ("gains", 80), ("lb_raw", 4), ("hg_out", 1), ("qa", 3), ("kva", 2),
             ("qn", 1), ("qr", 1), ("kn", 1), ("kr", 1), ("lam", 4)]
EVEN_PARTS = [("lmask", 7 * P), ("wsT", 8 * P), ("bs", 4 * P), ("vnorm", 512)]


def offsets(parts):
    o, at = {}, 0
    for name, n in parts:
        o[name] = (at, n)
        at += n
    return o, at


CONST_AT, CONST_N = offsets(CONST_PARTS)
VEC_AT, VEC_N = offsets(VEC_PARTS)
EVEN_AT, EVEN_N = offsets(EVEN_PARTS)


class Plan:

    def __init__(self):
        self.panels = []
        self.chunks = []
        self.half = 0
        self.begin = {}
        self.stages = {}
        self.owned = {"act": 0, "dve": 0, "hid": 2 * KF}

    def stage(self, name):
        self.stages[name] = {"steps": [], "first": len(self.chunks), "n": 0}
        self.now = self.stages[name]

    def panel(self, loads, k, n):
        self.panels.append({"loads": loads, "k": k, "n": n})
        return len(self.panels) - 1

    def step(self, panel, kind, cols, size, k0, k, owner=None, tile=None, chunk=None, last=True):
        start = chunk is None
        if start:
            chunk = len(self.chunks)
            self.begin.setdefault(chunk, [])
            self.chunks.append({"owner": owner, "nth": self.owned[owner]})
            self.owned[owner] += 1
            self.now["n"] += 1
        if "free" not in self.panels[panel]:
            self.begin[chunk].append(panel)
        self.now["steps"].append(dict(panel=panel, kind=kind, cols=cols, size=size, k0=k0, k=k, tile=tile,
                                      chunk=chunk, start=start, stop=last))
        if last:
            self.panels[panel]["free"] = ("chunk", chunk + 1)
        else:
            self.half += 1
            self.panels[panel]["free"] = ("half", self.half)
        return chunk


def cut(a, n):
    return lambda v, k: v[:, k, a:a + n]


def make_plan(W):
    pl = Plan()

    def rows(w):
        return w.rearrange("(k p) n -> p k n", p=P)

    def feature_panels(w, c0, c1, owner, k=KD, width=256):
        for c in range(c0, c1, width):
            n = min(width, c1 - c)
            full = -(-n // P) * P
            loads = [(0, n, rows(w)[:, :, c:c + n])]
            if full > n:
                loads.append((n, full, rows(w)[:, :, 0:full - n]))
            p = pl.panel(loads, k, full)
            for m in range(0, full, P):
                pl.step(p, "fm", cut(m, P), P, 0, k, owner)

    def token_panels(w, c0, c1, owner, tiles):
        for c in range(c0, c1, 256):
            p = pl.panel([(0, 256, rows(w)[:, :, c:c + 256])], KD, 256)
            for t in range(len(tiles)):
                pl.step(p, "tm", cut(0, 256), 256, 0, KD, owner, tile=tiles[t])

    def up_panels(wg, wu, gate_owner, up_owner):
        for c in range(0, F, P):
            p = pl.panel([(0, P, rows(wg)[:, :, c:c + P]), (P, 2 * P, rows(wu)[:, :, c:c + P])], KD, 2 * P)
            pl.step(p, "fm", cut(0, P), P, 0, KD, gate_owner)
            pl.step(p, "fm", cut(P, P), P, 0, KD, up_owner)

    def down_panels(w):
        for c in range(0, D, 256):
            ids = [None, None]
            for k0, k in ((0, 8), (8, 8), (16, 6)):
                p = pl.panel([(0, 256, rows(w)[:, k0:k0 + k, c:c + 256])], k, 256)
                ids = [pl.step(p, "fm", cut(m * P, P), P, k0, k, "dve", chunk=ids[m], last=k0 + k == KF)
                       for m in range(2)]

    pl.stage("da_qkv")
    feature_panels(W["da_w_qkv"][0], 0, 2 * D, "act")
    token_panels(W["da_w_qkv"][0], 2 * D, 3 * D, "act", TILES1)
    pl.stage("da_out")
    feature_panels(W["da_w_o"][0], 0, D, "dve")
    for i in range(2):
        if i == 1:
            w = W["dsa_w_in"][0]
            pl.stage("dsa_in")
            feature_panels(w, 3072, 3584, "act")
            p = pl.panel([(0, 72, rows(w)[:, :, 3584:3656]), (72, P, rows(w)[:, :, 0:P - 72])], KD, P)
            pl.step(p, "fm", cut(0, P), P, 0, KD, "act")
            for t in range(3):
                pl.step(p, "tm", cut(64, 8), 8, 0, KD, "act", tile=TILES1[t])
            token_panels(w, 2 * D, 3 * D, "act", TILES1)
            feature_panels(w, 0, 2 * D, "act")
            pl.stage("dsa_out")
            feature_panels(W["dsa_w_o"][0], 0, D, "dve")
        pl.stage(f"conv{i}_up")
        up_panels(W["ffn_w_up"][i][:, 0:F], W["ffn_w_up"][i][:, F:2 * F], "dve", "dve")
        pl.stage(f"conv{i}_down")
        down_panels(W["ffn_w_down"][i])
    for i in range(2):
        for j in range(2):
            if j == 1 and i == 0:
                w = W["even_w_in"][0]
                pl.stage("ev_in")
                feature_panels(w, 1536, 2048, "act")
                feature_panels(w, 1024, 1536, "act")
                token_panels(w, 2048, 2560, "act", TILES2)
                token_panels(w, 512, 1024, "act", TILES2)
                feature_panels(w, 0, 512, "act")
                feature_panels(w, 2560, 3072, "act")
                pl.stage("ev_out")
                feature_panels(W["even_w_out"][0], 0, D, "dve")
            if j == 1 and i == 1:
                pl.stage("mla_in")
                feature_panels(W["mla_w_in"][0], 0, 704, "act")
                pl.stage("mla_q")
                for g in range(4):
                    w = W["mla_w_q_b"][0]
                    loads = []
                    for hh in range(2):
                        c = (2 * g + hh) * 192
                        loads.append((hh * P, (hh + 1) * P, rows(w)[:, :, c:c + P]))
                        loads.append((256 + hh * 64, 256 + hh * 64 + 64, rows(w)[:, :, c + P:c + 192]))
                    p = pl.panel(loads, 3, 384)
                    for m in range(0, 384, P):
                        pl.step(p, "fm", cut(m, P), P, 0, 3, "act")
                pl.stage("mla_kv")
                for g in range(2):
                    p = pl.panel([(0, 1024, rows(W["mla_w_kv_b"][0])[:, :, g * 1024:(g + 1) * 1024])], 2, 1024)
                    for hh in range(4):
                        pl.step(p, "fm", cut(hh * 256, P), P, 0, 2, "act")
                    for t in range(2):
                        pl.step(p, "tm", lambda v, k: v.rearrange("p k (h c) -> p k h c", c=256)[
                            :, k, :, 128:256], 512, 0, 2, "act", tile=TILES2[t])
                pl.stage("mla_out")
                feature_panels(W["mla_w_out"][0], 0, D, "dve")
            pl.stage(f"glu{i}{j}_up")
            up_panels(W["ffn_w_gate"][i][j], W["ffn_w_up_2"][i][j], "act", "hid")
            pl.stage(f"glu{i}{j}_down")
            down_panels(W["ffn_w_down_2"][i][j])
        pl.stage(f"ple{i}_gate")
        feature_panels(W["ple_w_gate"][i], 0, D, "act")
        pl.stage(f"ple{i}_proj")
        feature_panels(W["ple_w_proj"][i], 0, D, "dve", k=2, width=1024)
    return pl


def make_norms():
    order = [("da", 8, 8)] + [(f"o{h}", 1, 1) for h in range(8)] + [("conv0", 8, 8), ("dsa", 8, 8), ("ki", 1, 1),
             ("conv1", 8, 8), ("final", 8, 8), ("glu00", 8, 8), ("ev", 8, 8)]
    order += [(f"hg{h}", 1, 1) for h in range(4)] + [("glu01", 8, 8), ("pleh0", 8, 8), ("pleo0", 8, 8),
             ("glu10", 8, 8), ("mla", 8, 8), ("cq", 3, 3), ("ckv", 2, 2)]
    order += [(f"q{h}", 2, 2) for h in range(8)] + [(f"k{h}", 2, 2) for h in range(8)]
    order += [("glu11", 8, 8), ("pleh1", 8, 8), ("pleo1", 8, 8)]
    out, sq, ap = {}, 0, 0
    for i, (name, n, m) in enumerate(order):
        prev = order[i - 1][1] if i else 0
        out[name] = dict(id=i, sq=sq, n=n, ap=ap, m=m, alone=prev + n > SQ_SLOTS)
        sq, ap = sq + n, ap + m
    out["by_id"] = [out[name] for name, _, _ in order]
    return out


def make_attention():
    out, s, u, oc = {}, 0, 0, 0
    for name, heads, tiles, comps, dv in (("da", 8, TILES1, 2, 128), ("dsa", 16, TILES1, 1, 64),
                                          ("mla", 8, TILES2, 1, 128)):
        units = []
        for h in range(heads):
            for t, (q0, qn) in enumerate(tiles):
                per = P // dv
                units.append(dict(h=h, t=t, q0=q0, qn=qn, kn=q0 + qn, u=u, scores=list(range(s, s + comps)),
                                  oc=oc + h // per, first=(h % per == 0 and t == 0),
                                  last=(h % per == per - 1 and t == len(tiles) - 1), part=dv * (h % per), dv=dv,
                                  chunk=h // per, ktiles=[(a, min(n, P)) for a, n in tiles if a < q0 + qn]))
                s += comps
                u += 1
        out[name] = dict(units=units, tiles=tiles, heads=heads)
        oc += heads * dv // P
    unit_of_score = [x["u"] for a in ("da", "dsa", "mla") for x in out[a]["units"] for _ in x["scores"]]
    return out, unit_of_score


def make_splits():
    order = [("da", 8), ("da_mix", 8), ("conv0", 8), ("hid0", KF), ("dsa", 8), ("dsa_mix", 8), ("conv1", 8),
             ("hid1", KF), ("glu00", 8), ("hid2", KF), ("ev", 8), ("ev_mix", 8), ("glu01", 8), ("hid3", KF),
             ("pleh0", 8), ("ple0", 2), ("glu10", 8), ("hid4", KF), ("mla", 8), ("cq", 3), ("ckv", 2),
             ("mla_mix", 8), ("glu11", 8), ("hid5", KF), ("pleh1", 8), ("ple1", 2)]
    out, at = {}, 0
    for name, n in order:
        out[name] = at
        at += n
    return out


ROPE_BASE = {"da": 0, "idx": 16, "dsa": 21, "kr": 37, "mq": 38}


def build(nc, W, hT, consts, idxc, vecs, evenc, pT_in, pos, out):
    plan = make_plan(W)
    norms = make_norms()
    att, unit_of_score = make_attention()
    chunks, stages, panels = plan.chunks, plan.stages, plan.panels
    splits = make_splits()

    with ExitStack() as ctx:
        def sb(name, shape, dt=F32):
            return ctx.enter_context(nc.sbuf_tensor(name, shape, dt))

        def sem(name):
            return ctx.enter_context(nc.semaphore(name))

        bank = ctx.enter_context(nc.psum_tensor("bank", [P, 8, 512], F32))
        arena_at = -(-nc.sbuf_base // 32) * 32
        arena = sb("arena", [P, 22 * T1 + 24 * T1 + 3072 + 8 * T1])

        def over(name, floats, shape):
            return nc.alloc_sbuf_tensor_at(name, shape, F32R, offset=arena_at + 4 * floats)

        raw = sb("weights_raw", [P, RAW, SLOT])
        w_hi = sb("weights_hi", [P, SPLIT, SLOT], F32R)
        w_lo = sb("weights_lo", [P, SPLIT, SLOT], F32R)
        h = sb("h", [P, KD, T1])
        x_hi = sb("x_hi", [P, KD * T1 + 112], F32R)
        x_lo = sb("x_lo", [P, KD * T1 + 112], F32R)
        hid_hi = over("hidden_hi", 0, [P, KF, T1])
        hid_lo = over("hidden_lo", 22 * T1, [P, KF, T1])
        mix_hi = over("mix_hi", 0, [P, KD, T1])
        mix_lo = over("mix_lo", 8 * T1, [P, KD, T1])
        ple_hi = over("ple_hi", 46 * T1, [P, 2, T1])
        ple_lo = over("ple_lo", 48 * T1, [P, 2, T1])
        sq = sb("sq", [P, SQ_SLOTS, T1])
        cst = sb("cst", [P, CONST_N])
        vec = sb("vec", [P, VEC_N])
        late = sb("late", [P, 1024])
        smpr = sb("smpr", [P, 8, T1])
        pn = sb("pn", [P, 2, T1])
        pT = sb("pT", [P, 2, 3 * P])
        rinv = sb("rinv", [P, 2, T1])
        rstd = sb("rstd", [P, 2, T1])
        small = sb("small", [P, 128])
        pos_sb = sb("pos_sb", [P, T2], I32)
        sm, pr = smpr[:, 0:4, :], smpr[:, 4:8, :]
        t1, t2 = pr[:, 0:2, :], pr[:, 2:4, :]

        def part(off, n, width=None):
            v = arena[:, off:off + n]
            return v.rearrange("p (c t) -> p c t", t=width) if width else v

        wide = part(0, 22 * T1, T1)
        qT = part(22 * T1, 12 * T1, T1)
        kT = part(34 * T1, 12 * T1, T1)
        v_tok = part(46 * T1, 3072, 1024)
        oT = part(46 * T1 + 3072, 8 * T1, T1)

        def con(name, rows=P):
            a, n = CONST_AT[name]
            return cst[0:rows, a:a + n]

        ident, ones, rot = con("ident"), con("ones"), con("rot")
        cos1, sin1 = con("cos"), con("sin")
        causal = con("causal")
        cs2 = cst[:, CONST_AT["cos"][0]:CONST_AT["cos"][0] + 2 * T2].rearrange("p (i t) -> p i t", i=2)

        def tile_of(mask, t):
            return mask[:, MASK_AT[t]:MASK_AT[t] + TILES1[t][0] + TILES1[t][1]]

        def col(name, i=0, p0=0, pn_=P):
            a, _ = VEC_AT[name]
            return vec[p0:p0 + pn_, a + i:a + i + 1]

        idx_const = part(46 * T1 + 3072, 2 * MASK_N)
        keep, addm = idx_const[:, 0:MASK_N], idx_const[:, MASK_N:2 * MASK_N]
        amask = late[:, 0:MASK_N]
        lmask = smpr.rearrange("p a b -> p (a b)")[:, 0:7 * P].rearrange("p (l t) -> p l t", l=7)
        wsT = smpr.rearrange("p a b -> p (a b)")[:, 4 * T1:4 * T1 + 8 * P].rearrange("p (h t) -> p h t", h=8)
        bs = late[:, 0:512].rearrange("p (c t) -> p c t", c=4)
        vn = late[:, 512:1024]

        mx, nmx, ssum, rs = small[:, 0:8], small[:, 8:16], small[:, 16:24], small[:, 24:32]
        wi_tok = small[:, 32:56].rearrange("p (t h) -> p t h", t=3)
        lam, lam_e, subln8, lam_p = small[:, 56:57], small[:, 57:59], small[:, 59:60], small[:, 60:62]
        max8 = small[:, 62:70]
        lb_t, lb, oml = small[:, 70:74], small[:, 74:78], small[:, 78:82]
        rl = small[:, 82:83]
        vms = small[:, 84:100]
        e_last = small[:, 100:116]

        s_const = sem("constants_loaded")
        s_idxc = sem("index_constants_loaded")
        s_pos = sem("positions_loaded")
        s_even = sem("even_constants_loaded")
        s_slot = [sem(f"slot{i}_loaded") for i in range(RAW)]
        s_whi = sem("weights_hi_ready")
        s_wlo = sem("weights_lo_ready")
        s_xhi = sem("activation_hi_ready")
        s_xlo = sem("activation_lo_ready")
        s_pad = sem("padding_written")
        s_ple = sem("layer_embedding_loaded")
        s_chunk = sem("chunk_ready")
        s_half = sem("half_chunk_ready")
        s_free = {"act": sem("chunk_emptied_by_act"), "dve": sem("chunk_emptied_by_dve")}
        s_sq = sem("squares_ready")
        s_col = sem("square_sum_ready")
        s_rinv = sem("mean_square_inverse_ready")
        s_rstd = sem("rstd_ready")
        s_app = sem("norm_applied")
        s_rot = sem("rotated_ready")
        s_t1 = sem("cos_part_ready")
        s_rope = sem("rope_ready")
        s_score = sem("scores_ready")
        s_max = sem("row_max_ready")
        s_exp = sem("exp_ready")
        s_prob = sem("probs_ready")
        s_tr = sem("probs_transposed")
        s_ptc = sem("probsT_copied")
        s_pv = sem("pv_done")
        s_oev = sem("attention_out_ready")
        s_idx = sem("index_raw_ready")
        s_relu = sem("index_relu_ready")
        s_idxa = sem("index_sum_ready")
        s_top = sem("topk_mask_ready")
        s_hid = sem("hidden_ready")
        s_conv = sem("conv_first_tap_ready")
        s_free["hid"] = s_hid
        s_silu = sem("silu_ready")
        s_lam = sem("lambda_products_ready")
        s_lams = sem("lambda_sums_ready")
        s_lame = sem("lambda_exp_ready")
        s_final = sem("second_block_input_ready")
        s_ang = sem("angles_ready")
        s_sincos = sem("sincos_ready")
        s_lbd = sem("lb_difference_ready")
        s_lbe = sem("lb_exp_ready")
        s_f = sem("forget_floor_ready")
        s_ln = sem("log_forget_ready")
        s_lvd = sem("level_exponent_ready")
        s_lve = sem("level_decay_ready")
        s_lvq = sem("level_operands_ready")
        s_lvm = sem("level_scores_ready")
        s_lva = sem("level_scores_added")
        s_ws = sem("spatial_weights_masked")
        s_vms = sem("value_mean_square_ready")
        s_vrs = sem("value_rstd_ready")
        s_gv = sem("value_normed")
        s_mixp = sem("spatial_product_ready")
        s_mix = sem("mixed_ready")
        s_kkt = sem("key_transposed")
        s_kkc = sem("key_copied")
        s_upd = sem("state_update_ready")
        s_st = sem("state_ready")
        s_hgo = sem("hgrn_product_ready")
        s_hge = sem("hgrn_out_ready")
        s_gate = sem("hgrn_gated")
        s_kr = sem("shared_rope_key_gained")
        s_out = sem("output_stored")
        s_dve = sem("dve_step")
        s_act = sem("act_step")

        def emptied(eng, c):
            eng.wait_ge(s_free[chunks[c]["owner"]], chunks[c]["nth"] + 1)

        def chunk_of(stage, i):
            return stages[stage]["first"] + i

        def dense_bank(c):
            return bank[:, c % DENSE_BANKS, :]

        def conv_buf(n):
            return sm[:, n % 4, :]

        def silu_buf(n):
            return pn[:, n % 2, :]

        def hid_buf(n):
            return pT[:, n % 2, 0:T1]

        block = ctx.enter_context(nc.Block())

        @block.sync
        def _(sp):
            for n, p in enumerate(panels):
                if n >= RAW:
                    sp.wait_ge(s_wlo, n - RAW + 1)
                view = raw[:, n % RAW, 0:p["k"] * p["n"]].rearrange("p (k n) -> p k n", n=p["n"])
                for a, b, src in p["loads"]:
                    sp.dma_start(view[:, :, a:b], src).then_inc(s_slot[n % RAW], 16)
            sp.wait_ge(s_free["dve"], plan.owned["dve"])
            sp.wait_ge(s_final, 8 + 16)
            sp.dma_start(out.rearrange("(c p) t -> p c t", p=P), h[:, :, 0:T2]).then_inc(s_out, 16)
            sp.wait_ge(s_out, 16)

        loaded = []
        seen = [0] * RAW
        for n, p in enumerate(panels):
            seen[n % RAW] += 16 * len(p["loads"])
            loaded.append(seen[n % RAW])

        def panel_freed(eng, n):
            kind, v = panels[n]["free"]
            eng.wait_ge(s_chunk if kind == "chunk" else s_half, v)

        def round_panel(act, n):
            size = panels[n]["k"] * panels[n]["n"]
            act.wait_ge(s_slot[n % RAW], loaded[n])
            if n >= SPLIT:
                panel_freed(act, n - SPLIT)
            nc.scalar.activation(w_hi[:, n % SPLIT, 0:size], raw[:, n % RAW, 0:size], ACT.Copy).then_inc(s_whi, 1)

        def rest_panel(dve, n):
            size = panels[n]["k"] * panels[n]["n"]
            dve.wait_ge(s_whi, n + 1)
            nc.vector.tensor_tensor(w_lo[:, n % SPLIT, 0:size], raw[:, n % RAW, 0:size],
                                    w_hi[:, n % SPLIT, 0:size].bitcast(F32), ALU.subtract).then_inc(s_wlo, 1)

        def weights_ahead(eng, split_one, c):
            for n in plan.begin[c]:
                if n + AHEAD < len(panels):
                    split_one(eng, n + AHEAD)

        @block.tensor
        def _(pe):
            def dense(stage, src, T, split, after=None):
                waited, now = set(), -1
                for s in stages[stage]["steps"]:
                    p = panels[s["panel"]]
                    if s["panel"] != now:
                        now = s["panel"]
                        pe.wait_ge(s_wlo, now + 1)
                        wh, wl = [r[:, now % SPLIT, 0:p["k"] * p["n"]].rearrange("p (k n) -> p k n", n=p["n"])
                                  for r in (w_hi, w_lo)]
                    if s["start"] and s["chunk"] >= DENSE_BANKS:
                        emptied(pe, s["chunk"] - DENSE_BANKS)
                    b = dense_bank(s["chunk"])
                    for k in range(s["k"]):
                        kk = s["k0"] + k
                        if kk not in waited:
                            pe.wait_ge(s_xlo, split + kk + 1)
                            waited.add(kk)
                        ch, cl = s["cols"](wh, k), s["cols"](wl, k)
                        if s["kind"] == "fm":
                            xh, xl = [x[:, kk * T1:kk * T1 + T] for x in src]
                            passes, o = ((ch, xh), (ch, xl), (cl, xh)), b[:, 0:T]
                        else:
                            q0 = kk * T1 + s["tile"][0]
                            xh, xl = [x[:, q0:q0 + P] for x in src]
                            passes, o = ((xh, ch), (xh, cl), (xl, ch)), b[:, 0:s["size"]]
                        for i, (lhs, rhs) in enumerate(passes):
                            mm = nc.tensor.matmul(o, lhs, rhs, start=s["start"] and k == 0 and i == 0,
                                                  stop=s["stop"] and k == s["k"] - 1 and i == 2)
                    mm.then_inc(s_chunk if s["stop"] else s_half, 1)
                    if after and s["stop"]:
                        after(s["chunk"] - stages[stage]["first"])

            def norm_sum(name, T, parts=((0, P),) * 8):
                m = norms[name]
                if m["id"]:
                    pe.wait_ge(s_rinv, m["id"])
                for i in range(m["n"]):
                    a, n = parts[i]
                    pe.wait_ge(s_sq, m["sq"] + i + 1)
                    mm = nc.tensor.matmul(bank[:, B_COL, 0:T], ones[a:a + n, :],
                                          sq[a:a + n, (m["sq"] + i) % SQ_SLOTS, 0:T],
                                          start=(i == 0), stop=(i == m["n"] - 1))
                mm.then_inc(s_col, 1)

            def rotate(r, raw, T, ready, rows=P):
                pe.wait_ge(*ready)
                if r >= 2:
                    pe.wait_ge(s_rope, r - 1)
                nc.tensor.matmul(bank[0:rows, B_S + r % 2, 0:T], rot[0:rows, 0:rows], raw,
                                 start=True, stop=True).then_inc(s_rot, 1)

            def attention(name, score_ops):
                A = att[name]
                U = A["units"]
                for i in range(len(U) + 3):
                    if i < len(U):
                        x = U[i]
                        for c, s in enumerate(x["scores"]):
                            if s >= 2:
                                pe.wait_ge(s_max, s - 1)
                            ops = score_ops(x, c)
                            for j, (a, b) in enumerate(ops):
                                mm = nc.tensor.matmul(bank[0:x["qn"], B_S + s % 2, 0:x["kn"]], a, b,
                                                      start=(j == 0), stop=(j == len(ops) - 1))
                            mm.then_inc(s_score, 1)
                    if 2 <= i < len(U) + 2:
                        x = U[i - 2]
                        pe.wait_ge(s_prob, x["u"] + 1)
                        if x["u"]:
                            pe.wait_ge(s_ptc, x["u"])
                        for kt, (a, n) in enumerate(x["ktiles"]):
                            mm = nc.tensor.transpose(bank[0:n, B_PT, kt * P:kt * P + x["qn"]],
                                                     pn[0:x["qn"], x["u"] % 2, a:a + n],
                                                     ident[0:x["qn"], 0:x["qn"]])
                        mm.then_inc(s_tr, 1)
                    if i >= 3:
                        x = U[i - 3]
                        pe.wait_ge(s_ptc, x["u"] + 1)
                        if x["first"] and x["oc"] >= 2:
                            pe.wait_ge(s_oev, x["oc"] - 1)
                        ob = bank[x["part"]:x["part"] + x["dv"], B_O - x["oc"] % 2, x["q0"]:x["q0"] + x["qn"]]
                        for kt, (a, n) in enumerate(x["ktiles"]):
                            mm = nc.tensor.matmul(ob, v_tok[0:n, kt, x["h"] * x["dv"]:(x["h"] + 1) * x["dv"]],
                                                  pT[0:n, x["u"] % 2, kt * P:kt * P + x["qn"]],
                                                  start=(kt == 0), stop=(kt == len(x["ktiles"]) - 1))
                        mm.then_inc(s_pv, 1)

            def act_chunk(c):
                return (s_free["act"], chunks[c]["nth"] + 1)

            flat = lambda x: x.rearrange("p k t -> p (k t)")
            X = (x_hi, x_lo)
            HID = (flat(hid_hi[:, :, :]), flat(hid_lo[:, :, :]))
            MIX = (flat(mix_hi[:, :, :]), flat(mix_lo[:, :, :]))
            PLE = (flat(ple_hi[:, :, :]), flat(ple_lo[:, :, :]))

            pe.wait_ge(s_const, 48)
            pe.wait_ge(s_lam, 1)
            nc.tensor.matmul(bank[:, B_PT, 0:2], ones[0:64, :], lam_p[0:64, :], start=True, stop=True)\
                .then_inc(s_lams, 1)
            norm_sum("da", T1)

            def da_after(j):
                if 2 <= j < 18:
                    rotate(j - 2, wide[:, j - 2, :], T1, act_chunk(chunk_of("da_qkv", j - 2)))
            pe.wait_ge(s_pad, 2)
            dense("da_qkv", X, T1, splits["da"], da_after)
            pe.wait_ge(s_rope, 16)

            def da_ops(x, c):
                return [(qT[64 * c:64 * c + 64, x["h"], x["q0"]:x["q0"] + x["qn"]],
                         kT[64 * c:64 * c + 64, x["h"], 0:x["kn"]])]
            attention("da", da_ops)
            for hh in range(8):
                norm_sum(f"o{hh}", T1)
            dense("da_out", MIX, T1, splits["da_mix"])
            norm_sum("conv0", T1)
            dense("conv0_up", X, T1, splits["conv0"])
            dense("conv0_down", HID, T1, splits["hid0"])

            norm_sum("dsa", T1)
            rb = ROPE_BASE["idx"]

            def index_scores(x):
                t, hh = divmod(x, 8)
                q0, qn = TILES1[t]
                a = 64 * (hh % 2)
                if x >= 2:
                    pe.wait_ge(s_relu, x - 1)
                nc.tensor.matmul(bank[0:qn, B_S + x % 2, 0:q0 + qn], qT[a:a + 64, 8 + hh // 2, q0:q0 + qn],
                                 kT[a:a + 64, 8, 0:q0 + qn], start=True, stop=True).then_inc(s_idx, 1)

            def dsa_after(j):
                if 2 <= j < 6:
                    rotate(rb + j - 2, wide[:, j - 2, :], T1, act_chunk(chunk_of("dsa_in", j - 2)))
                if j == 6:
                    norm_sum("ki", T1, ((0, 64),))
                if j == 7:
                    rotate(rb + 4, wide[0:64, 5, :], T1, (s_app, norms["ki"]["ap"] + 1), rows=64)
                if 8 <= j < 20:
                    if j == 8:
                        pe.wait_ge(s_rope, rb + 5)
                        pe.wait_ge(s_top, 1)
                    index_scores(2 * (j - 8))
                    index_scores(2 * (j - 8) + 1)
                if j == 20:
                    pe.wait_ge(s_relu, 24)
                if j >= 22:
                    i = j - 22
                    rotate(ROPE_BASE["dsa"] + i, wide[:, 6 + i, :], T1, act_chunk(chunk_of("dsa_in", 20 + i)))
            dense("dsa_in", X, T1, splits["dsa"], dsa_after)
            for i in (14, 15):
                rotate(ROPE_BASE["dsa"] + i, wide[:, 6 + i, :], T1, act_chunk(chunk_of("dsa_in", 20 + i)))
            pe.wait_ge(s_rope, ROPE_BASE["dsa"] + 16)

            def dsa_ops(x, c):
                a = 64 * (x["h"] % 2)
                return [(qT[a:a + 64, x["h"] // 2, x["q0"]:x["q0"] + x["qn"]], kT[a:a + 64, x["h"] // 2, 0:x["kn"]])]
            attention("dsa", dsa_ops)
            dense("dsa_out", MIX, T1, splits["dsa_mix"])
            norm_sum("conv1", T1)
            dense("conv1_up", X, T1, splits["conv1"])
            dense("conv1_down", HID, T1, splits["hid1"])
            norm_sum("final", T1)

            def glu(i, j):
                norm_sum(f"glu{i}{j}", T2)
                dense(f"glu{i}{j}_up", X, T2, splits[f"glu{i}{j}"])
                dense(f"glu{i}{j}_down", HID, T2, splits[f"hid{2 + 2 * i + j}"])

            def ple(i):
                norm_sum(f"pleh{i}", T2)
                dense(f"ple{i}_gate", X, T2, splits[f"pleh{i}"])
                dense(f"ple{i}_proj", PLE, T2, splits[f"ple{i}"])
                norm_sum(f"pleo{i}", T2)

            glu(0, 0)
            norm_sum("ev", T2)
            dense("ev_in", X, T2, splits["ev"])
            slot = lambda i: part(i * 1024, 1024)
            hg_v = part(11 * 1024, 1024, 512)
            scT = part(10 * 1024, 1024, 512)
            nq = chunks[chunk_of("ev_in", 4)]["nth"]
            pe.wait_ge(s_free["act"], nq + 8)
            for lv in range(7):
                pe.wait_ge(s_lvq, lv + 1)
                if lv == 0:
                    qe_, ke_ = slot(0), slot(1)
                else:
                    qe_, ke_ = slot(6 + lv % 2), slot(8 + lv % 2)
                for t in range(2):
                    if lv:
                        pe.wait_ge(s_lva, 2 * (lv - 1) + t + 1)
                    for hh in range(4):
                        o = hh * T2 + t * P
                        mm = nc.tensor.matmul(bank[:, B_S + t, hh * P:(hh + 1) * P], ke_[:, o:o + P],
                                              qe_[:, o:o + P], start=True, stop=True)
                    mm.then_inc(s_lvm, 1)
            pe.wait_ge(s_gv, 1)
            pe.wait_ge(s_ws, 1)
            gvn = part(14 * 1024, 1024, 512)
            for t in range(2):
                for hh in range(8):
                    a = 64 * (hh % 2)
                    mm = nc.tensor.matmul(bank[a:a + 64, B_COL + t, (hh // 2) * P:(hh // 2 + 1) * P],
                                          gvn[:, t, hh * 64:hh * 64 + 64], wsT[:, hh, :], start=True, stop=True)
                mm.then_inc(s_mixp, 1)
            pe.wait_ge(s_gate, 1)
            kk = slot(7)
            for t in range(2):
                if t == 1:
                    pe.wait_ge(s_kkc, 1)
                for hh in range(4):
                    mm = nc.tensor.transpose(bank[:, B_PT, hh * P:(hh + 1) * P],
                                             kk[:, hh * T2 + t * P:hh * T2 + t * P + P], ident)
                mm.then_inc(s_kkt, 1)
            kk_tok = part(14 * 1024, 1024, 512)
            pe.wait_ge(s_kkc, 2)
            pe.wait_ge(s_lva, 14)
            for n in range(3):
                a, t = 64 * (n % 2), n // 2
                if n >= 2:
                    pe.wait_ge(s_st, n - 1)
                for hh in range(4):
                    mm = nc.tensor.matmul(bank[:, B_S + n % 2, hh * P:(hh + 1) * P],
                                          kk_tok[a:a + 64, t, hh * P:(hh + 1) * P],
                                          hg_v[a:a + 64, t, hh * P:(hh + 1) * P], start=True, stop=True)
                mm.then_inc(s_upd, 1)
            states = part(8 * 1024, 1536, 512)
            qe = slot(6)
            pe.wait_ge(s_mix, 2)
            pe.wait_ge(s_st, 3)
            for hh in range(4):
                b = B_COL + hh // 2
                for t in range(2):
                    o = (hh % 2) * T2 + t * P
                    nc.tensor.matmul(bank[:, b, o:o + P], hg_v[:, t, hh * P:(hh + 1) * P],
                                     scT[:, t, hh * P:(hh + 1) * P], start=True, stop=False)
                    for n in range(max(1, 2 * t), 2 * t + 2):
                        oo = (hh % 2) * T2 + n * CHUNK
                        mm = nc.tensor.matmul(bank[:, b, oo:oo + CHUNK], states[:, n - 1, hh * P:(hh + 1) * P],
                                              qe[:, hh * T2 + n * CHUNK:hh * T2 + (n + 1) * CHUNK],
                                              start=False, stop=(n == 2 * t + 1))
                mm.then_inc(s_hgo, 1)
            pe.wait_ge(s_hge, 4)
            for hh in range(4):
                norm_sum(f"hg{hh}", T2)
            dense("ev_out", MIX, T2, splits["ev_mix"])
            glu(0, 1)
            ple(0)
            glu(1, 0)
            norm_sum("mla", T2)
            dense("mla_in", X, T2, splits["mla"])
            norm_sum("cq", T2)
            norm_sum("ckv", T2)
            dense("mla_q", X, T2, splits["cq"])
            dense("mla_kv", (x_hi[:, 3 * T1:], x_lo[:, 3 * T1:]), T2, splits["ckv"])
            rotate(ROPE_BASE["kr"], oT[:, 6, 0:T2], T2, (s_kr, 1))
            for hh in range(8):
                a = 64 * (hh % 2)
                norm_sum(f"q{hh}", T2, ((0, P), (a, 64)))
            for hh in range(8):
                a = 64 * (hh % 2)
                norm_sum(f"k{hh}", T2, ((0, P), (a, 64)))
            for r in range(4):
                rotate(ROPE_BASE["mq"] + r, wide[:, 6 + 8 + r, 0:T2], T2, (s_app, norms[f"q{2 * r + 1}"]["ap"] + 2))
            pe.wait_ge(s_rope, ROPE_BASE["mq"] + 4)
            pe.wait_ge(s_app, norms["k7"]["ap"] + 2)

            def mla_ops(x, c):
                a = 64 * (x["h"] % 2)
                hh = x["h"]
                q = slice(x["q0"], x["q0"] + x["qn"])
                return [(qT[:, hh, q], kT[:, hh, 0:x["kn"]]),
                        (qT[a:a + 64, 8 + hh // 2, q], kT[a:a + 64, 8 + hh // 2, 0:x["kn"]])]
            attention("mla", mla_ops)
            dense("mla_out", MIX, T2, splits["mla_mix"])
            glu(1, 1)
            ple(1)

        @block.scalar
        def _(act):
            def step(ins):
                step.n += 1
                ins.then_inc(s_act, 1)
                act.wait_ge(s_act, step.n)
            step.n = 0

            def square(name, srcs, ready, parts=((0, P),) * 8, T=T1):
                m = norms[name]
                need = m["id"] if m["alone"] else m["id"] - 1
                if need > 0:
                    act.wait_ge(s_col, need)
                for i, s in enumerate(srcs):
                    a, n = parts[i]
                    act.wait_ge(*ready[i])
                    nc.scalar.activation(sq[a:a + n, (m["sq"] + i) % SQ_SLOTS, 0:T], s, ACT.Square).then_inc(s_sq, 1)

            def root(name, T):
                m = norms[name]
                act.wait_ge(s_rinv, m["id"] + 1)
                if m["id"] >= 2:
                    act.wait_ge(s_app, norms["by_id"][m["id"] - 1]["ap"])
                nc.scalar.activation(rstd[:, m["id"] % 2, 0:T], rinv[:, m["id"] % 2, 0:T], ACT.Sqrt)\
                    .then_inc(s_rstd, 1)

            def residual(stage):
                c0 = stages[stage]["first"]
                return [(s_free["dve"], chunks[c0 + i]["nth"] + 1) for i in range(8)]

            def high(at, dst, src, ready):
                for i in range(len(dst)):
                    act.wait_ge(*ready[i])
                    nc.scalar.activation(dst[i], src[i], ACT.Copy).then_inc(s_xhi, 1)

            def high_normed(name, n=KD, first=0, T=T2):
                m = norms[name]
                high(splits[name], [x_hi[:, (first + c) * T1:(first + c) * T1 + T] for c in range(n)],
                     [sq[:, (m["sq"] + c) % SQ_SLOTS, 0:T] for c in range(n)],
                     [(s_app, m["ap"] + c + 1) for c in range(n)])

            def high_mix(name, T, ready):
                high(splits[name], [mix_hi[:, c, 0:T] for c in range(KD)], [oT[:, c, 0:T] for c in range(KD)], ready)

            def norm_h(name, ready, T):
                square(name, [h[:, c, 0:T] for c in range(KD)], ready, T=T)
                root(name, T)
                if name in splits:
                    high_normed(name, T=T)

            def ahead(c):
                weights_ahead(act, round_panel, c)

            def ahead_stage(stage):
                for i in range(stages[stage]["n"]):
                    ahead(chunk_of(stage, i))

            def evict(c, dst, func=ACT.Copy, src=None, scale=1.0, last=True, first=True):
                if first:
                    ahead(c)
                act.wait_ge(s_chunk, c + 1)
                b = dense_bank(c)
                src = b[0:dst.shape[0], 0:int(np.prod(dst.shape[1:]))] if src is None else src
                ins = nc.scalar.activation(dst, src, func, scale=scale)
                if last:
                    ins.then_inc(s_free["act"], 1)

            def attention(name, scale):
                U = att[name]["units"]
                for i in range(len(U) + 3):
                    if i < len(U):
                        x = U[i]
                        for s in x["scores"]:
                            act.wait_ge(s_max, s + 1)
                            if s >= 4:
                                act.wait_ge(s_prob, unit_of_score[s - 4] + 1)
                            q, k = x["qn"], x["kn"]
                            nc.scalar.activation(pr[0:q, s % 4, 0:k], sm[0:q, s % 4, 0:k], ACT.Exp,
                                                 bias=nmx[0:q, s % 8:s % 8 + 1], scale=scale,
                                                 accum_out=ssum[0:q, s % 8:s % 8 + 1]).then_inc(s_exp, 1)
                    if 2 <= i < len(U) + 2:
                        x = U[i - 2]
                        u, q = x["u"], x["qn"]
                        act.wait_ge(s_tr, u + 1)
                        if u >= 2:
                            act.wait_ge(s_pv, u - 1)
                        full = [kt for kt in x["ktiles"] if kt[1] == P]
                        v = lambda z: z.rearrange("p (k q) -> p k q", q=P)
                        ins = nc.scalar.activation(v(pT[:, u % 2, :])[:, 0:len(full), 0:q],
                                                   v(bank[:, B_PT, 0:3 * P])[:, 0:len(full), 0:q], ACT.Copy)
                        if len(full) < len(x["ktiles"]):
                            kt, n = len(full), x["ktiles"][-1][1]
                            ins = nc.scalar.activation(pT[0:n, u % 2, kt * P:kt * P + q],
                                                       bank[0:n, B_PT, kt * P:kt * P + q], ACT.Copy)
                        ins.then_inc(s_ptc, 1)
                    if i >= 3 and U[i - 3]["last"]:
                        x = U[i - 3]
                        T = T2 if name == "mla" else T1
                        act.wait_ge(s_pv, x["u"] + 1)
                        nc.scalar.activation(oT[:, x["chunk"], 0:T], bank[:, B_O - x["oc"] % 2, 0:T], ACT.Copy)\
                            .then_inc(s_oev, 1)

            act.dma_start(cst[:, :], consts).then_inc(s_const, 16)
            act.dma_start(vec[:, :], vecs).then_inc(s_const, 16)
            act.dma_start(h[:, :, :], hT.rearrange("(c p) t -> p c t", p=P)).then_inc(s_const, 16)
            act.dma_start(pos_sb[:, :], pos).then_inc(s_pos, 16)
            for n in range(AHEAD):
                round_panel(act, n)
            act.wait_ge(s_lbd, 1)
            nc.scalar.activation(lb, lb_t, ACT.Exp).then_inc(s_lbe, 1)
            act.wait_ge(s_lams, 1)
            nc.scalar.activation(lam_e, bank[:, B_PT, 0:2], ACT.Exp).then_inc(s_lame, 1)
            act.wait_ge(s_const, 48)
            norm_h("da", [(s_const, 48)] * 8, T1)
            for j in range(16):
                evict(chunk_of("da_qkv", j), wide[:, j, :])
            for j in range(12):
                g, t = divmod(j, 3)
                n = TILES1[t][1]
                c = chunk_of("da_qkv", 16 + j)
                evict(c, v_tok[0:n, t, g * 256:(g + 1) * 256])
            attention("da", 64 ** -0.5)
            oc0 = att["da"]["units"][0]["oc"]
            for hh in range(9):
                if hh < 8:
                    square(f"o{hh}", [oT[:, hh, :]], [(s_oev, oc0 + hh + 1)])
                if hh >= 1:
                    root(f"o{hh - 1}", T1)
            high_mix("da_mix", T1, [(s_app, norms["o0"]["ap"] + i + 1) for i in range(8)])
            ahead_stage("da_out")
            norm_h("conv0", residual("da_out"), T1)
            act.wait_ge(s_xlo, splits["da_mix"] + 8)
            act.dma_start(idx_const, idxc).then_inc(s_idxc, 16)

            def conv_up(i):
                for j in range(KF + 1):
                    if j < KF:
                        for g in range(2):
                            c = chunk_of(f"conv{i}_up", 2 * j + g)
                            n = i * 2 * KF + 2 * j + g
                            ch = j + g * KF
                            ahead(c)
                            act.wait_ge(s_chunk, c + 1)
                            if n >= 4:
                                act.wait_ge(s_hid, (n - 4) // 2 + 1)
                            nc.scalar.activation(conv_buf(n), dense_bank(c)[:, 0:T1], ACT.Identity,
                                                 bias=col("conv_b", i * 44 + ch),
                                                 scale=col("conv_w", (i * 3 + 2) * 44 + ch)).then_inc(s_conv, 1)
                    if j >= 1:
                        n = i * 2 * KF + 2 * (j - 1)
                        c = chunk_of(f"conv{i}_up", 2 * (j - 1))
                        act.wait_ge(s_free["dve"], chunks[c]["nth"] + 1)
                        nc.scalar.activation(silu_buf(n // 2), conv_buf(n), ACT.Silu).then_inc(s_silu, 1)
                        g = i * KF + j - 1
                        high(splits[f"hid{i}"] + j - 1, [hid_hi[:, j - 1, :]], [hid_buf(g)], [(s_hid, g + 1)])
            conv_up(0)
            ahead_stage("conv0_down")
            norm_h("dsa", residual("conv0_down"), T1)
            for j in range(4):
                evict(chunk_of("dsa_in", j), wide[:, j, :])
            evict(chunk_of("dsa_in", 4), wide[0:64, 4, :])
            square("ki", [wide[0:64, 4, :]], [(s_free["act"], chunks[chunk_of("dsa_in", 4)]["nth"] + 1)], ((0, 64),))
            for t in range(3):
                evict(chunk_of("dsa_in", 5 + t), wi_tok[0:TILES1[t][1], t, :], scale=IDX_HEADS ** -0.5)
            root("ki", T1)
            act.wait_ge(s_rope, ROPE_BASE["idx"] + 5)
            nc.scalar.activation(kT[64:128, 8, :], kT[0:64, 8, :], ACT.Copy).then_inc(s_top, 1)

            def index_relu(x):
                t, hh = divmod(x, 8)
                q0, qn = TILES1[t]
                act.wait_ge(s_idx, x + 1)
                if x >= 2:
                    act.wait_ge(s_idxa, x - 1)
                nc.scalar.activation(pr[0:qn, x % 2, 0:q0 + qn], bank[0:qn, B_S + x % 2, 0:q0 + qn],
                                     ACT.Relu, scale=0.125).then_inc(s_relu, 1)
            for j in range(12):
                g, t = divmod(j, 3)
                evict(chunk_of("dsa_in", 8 + j), v_tok[0:TILES1[t][1], t, g * 256:(g + 1) * 256])
                index_relu(2 * j)
                index_relu(2 * j + 1)
            for j in range(16):
                evict(chunk_of("dsa_in", 20 + j), wide[:, 6 + j, :])
            attention("dsa", 64 ** -0.5)
            high_mix("dsa_mix", T1, [(s_oev, att["dsa"]["units"][0]["oc"] + i + 1) for i in range(8)])
            ahead_stage("dsa_out")
            act.wait_ge(s_ang, 2)
            for i in range(2):
                ins = nc.scalar.activation(cs2[:, i, :], t2[:, i, 0:T2], ACT.Sin)
            ins.then_inc(s_sincos, 1)
            norm_h("conv1", residual("dsa_out"), T1)
            conv_up(1)
            ahead_stage("conv1_down")
            norm_h("final", residual("conv1_down"), T1)
            act.wait_ge(s_xlo, splits["hid1"] + KF)
            act.wait_ge(s_sincos, 1)
            flat_smpr = smpr.rearrange("p a b -> p (a b)")
            for name, dst in (("lmask", flat_smpr[:, 0:7 * P]), ("wsT", flat_smpr[:, 4 * T1:4 * T1 + 8 * P]),
                              ("bs", late[:, 0:512]), ("vnorm", late[:, 512:1024])):
                o, n = EVEN_AT[name]
                act.dma_start(dst, evenc[:, o:o + n]).then_inc(s_even, 16)
            for c in range(KD):
                act.wait_ge(s_app, norms["final"]["ap"] + c + 1)
                nc.scalar.activation(h[:, c, 0:T2], wide[:, c, 0:T2], ACT.Copy).then_inc(s_final, 1)

            def glu_up(i, j):
                for n in range(KF + 1):
                    c = chunk_of(f"glu{i}{j}_up", 2 * n)
                    g = 2 * KF + (2 * i + j) * KF + n
                    if n < KF:
                        ahead(c)
                        act.wait_ge(s_chunk, c + 1)
                        act.wait_ge(s_hid, g - 1)
                        nc.scalar.activation(silu_buf(g)[:, 0:T2], dense_bank(c)[:, 0:T2], ACT.Silu)\
                            .then_inc(s_free["act"], 1)
                    if n >= 1:
                        high(0, [hid_hi[:, n - 1, 0:T2]], [hid_buf(g - 1)[:, 0:T2]], [(s_hid, g)])
                ahead_stage(f"glu{i}{j}_down")

            def ple(i, before):
                act.dma_start(oT[:, 0:2, 0:T2], pT_in[i].rearrange("(c p) t -> p c t", p=P)).then_inc(s_ple, 16)
                norm_h(f"pleh{i}", before, T2)
                high(splits[f"ple{i}"], [ple_hi[:, c, 0:T2] for c in range(2)], [oT[:, c, 0:T2] for c in range(2)],
                     [(s_ple, 16 * (i + 1))] * 2)
                for c in range(KD):
                    evict(chunk_of(f"ple{i}_gate", c), wide[:, c, 0:T2], ACT.Sigmoid)
                ahead_stage(f"ple{i}_proj")
                square(f"pleo{i}", [wide[:, 8 + c, 0:T2] for c in range(KD)], residual(f"ple{i}_proj"), T=T2)
                root(f"pleo{i}", T2)

            norm_h("glu00", [(s_final, c + 1) for c in range(8)], T2)
            glu_up(0, 0)
            norm_h("ev", residual("glu00_down"), T2)
            slot = lambda i: part(i * 1024, 1024)
            for c in range(4):
                evict(chunk_of("ev_in", c), slot(1)[:, c * T2:(c + 1) * T2], ACT.Sigmoid)
            for c in range(4):
                evict(chunk_of("ev_in", 4 + c), slot(0)[:, c * T2:(c + 1) * T2])
            for j in range(4):
                g, t = divmod(j, 2)
                evict(chunk_of("ev_in", 8 + j), slot(11)[:, t * 512 + g * 256:t * 512 + g * 256 + 256])
            act.wait_ge(s_f, 1)
            nc.scalar.activation(slot(2), slot(3), ACT.Ln).then_inc(s_ln, 1)
            for j in range(4):
                g, t = divmod(j, 2)
                evict(chunk_of("ev_in", 12 + j), slot(14)[:, t * 512 + g * 256:t * 512 + g * 256 + 256],
                      ACT.Gelu_apprx_tanh)
            for c in range(4):
                evict(chunk_of("ev_in", 16 + c), slot(12)[:, c * T2:(c + 1) * T2], ACT.Gelu_apprx_tanh)
            for c in range(4):
                evict(chunk_of("ev_in", 20 + c), slot(13)[:, c * T2:(c + 1) * T2], ACT.Silu)
            act.wait_ge(s_vms, 1)
            nc.scalar.activation(vms, vms, ACT.Sqrt).then_inc(s_vrs, 1)
            for lv in range(1, 7):
                act.wait_ge(s_lvd, lv)
                e = slot(4 + lv % 2)
                nc.scalar.activation(e, e, ACT.Exp).then_inc(s_lve, 1)
            act.wait_ge(s_lvd, 7)
            nc.scalar.activation(e_last, slot(2).rearrange("p (n c) -> p n c", c=CHUNK)[:, :, CHUNK - 1], ACT.Exp)
            nc.scalar.activation(slot(4), slot(2), ACT.Exp)
            nc.scalar.activation(slot(5), slot(5), ACT.Exp).then_inc(s_lve, 1)
            for t in range(2):
                act.wait_ge(s_kkt, t + 1)
                nc.scalar.activation(slot(14)[:, t * 512:(t + 1) * 512], bank[:, B_PT, :], ACT.Copy)\
                    .then_inc(s_kkc, 1)
            for hh in range(4):
                act.wait_ge(s_hgo, 2 * (hh // 2) + 2)
                o = (hh % 2) * T2
                nc.scalar.activation(slot(3)[:, hh * T2:(hh + 1) * T2], bank[:, B_COL + hh // 2, o:o + T2], ACT.Copy)\
                    .then_inc(s_hge, 1)
            for hh in range(5):
                if hh < 4:
                    square(f"hg{hh}", [slot(3)[:, hh * T2:(hh + 1) * T2]], [(s_hge, hh + 1)], T=T2)
                if hh >= 1:
                    root(f"hg{hh - 1}", T2)
            high_mix("ev_mix", T2, [(s_mix, 2)] * 4 + [(s_gate, 5)] * 4)
            ahead_stage("ev_out")
            norm_h("glu01", residual("ev_out"), T2)
            glu_up(0, 1)
            ple(0, residual("glu01_down"))
            norm_h("glu10", [(s_final, 8 + c + 1) for c in range(8)], T2)
            glu_up(1, 0)
            norm_h("mla", residual("glu10_down"), T2)
            for c in range(5):
                evict(chunk_of("mla_in", c), wide[:, c, 0:T2])
            c5 = chunk_of("mla_in", 5)
            evict(c5, wide[0:64, 5, 0:T2], last=False)
            evict(c5, wide[64:128, 5, 0:T2], src=dense_bank(c5)[0:64, 0:T2], first=False)
            f0 = chunks[chunk_of("mla_in", 0)]["nth"]
            square("cq", [wide[:, c, 0:T2] for c in range(3)], [(s_free["act"], f0 + 1 + c) for c in range(3)], T=T2)
            square("ckv", [wide[:, 3 + c, 0:T2] for c in range(2)], [(s_free["act"], f0 + 4 + c) for c in range(2)],
                   T=T2)
            root("cq", T2)
            root("ckv", T2)
            high_normed("cq", 3)
            high_normed("ckv", 2, first=3)
            for g in range(4):
                for x in range(2):
                    evict(chunk_of("mla_q", 3 * g + x), wide[:, 6 + 2 * g + x, 0:T2])
                evict(chunk_of("mla_q", 3 * g + 2), wide[:, 14 + g, 0:T2])
            for g in range(2):
                for hh in range(4):
                    evict(chunk_of("mla_kv", 6 * g + hh), kT[:, 4 * g + hh, 0:T2])
                for t in range(2):
                    evict(chunk_of("mla_kv", 6 * g + 4 + t), v_tok[:, t, g * 512:(g + 1) * 512])
            fq = [chunks[chunk_of("mla_q", j)]["nth"] + 1 for j in range(12)]
            fk = [chunks[chunk_of("mla_kv", j)]["nth"] + 1 for j in range(12)]
            heads = []
            for hh in range(8):
                a = 64 * (hh % 2)
                heads.append((f"q{hh}", [wide[:, 6 + hh, 0:T2], wide[a:a + 64, 14 + hh // 2, 0:T2]],
                              [(s_free["act"], fq[3 * (hh // 2) + 2])] * 2 + [(s_free["act"], 1)], a))
            for hh in range(8):
                a = 64 * (hh % 2)
                heads.append((f"k{hh}", [kT[:, hh, 0:T2], wide[a:a + 64, 5, 0:T2]],
                              [(s_free["act"], fk[6 * (hh // 4) + hh % 4]), (s_free["act"], f0 + 6)], a))
            for i in range(17):
                if i < 16:
                    n_, src, rd, a = heads[i]
                    square(n_, src, rd, ((0, P), (a, 64)), T=T2)
                if i >= 1:
                    root(heads[i - 1][0], T2)
            attention("mla", 192 ** -0.5)
            high_mix("mla_mix", T2, [(s_oev, att["mla"]["units"][0]["oc"] + i + 1) for i in range(8)])
            ahead_stage("mla_out")
            norm_h("glu11", residual("mla_out"), T2)
            glu_up(1, 1)
            ple(1, residual("glu11_down"))

        @block.gpsimd
        def _(pool):
            def cos_part(r, raw, table, T, ready, rows=P):
                pool.wait_ge(*ready)
                if r >= 2:
                    pool.wait_ge(s_rope, r - 1)
                nc.gpsimd.tensor_tensor(t1[0:rows, r % 2, 0:T], raw, table[0:rows, 0:T], ALU.mult).then_inc(s_t1, 1)

            def act_chunk(c):
                return (s_free["act"], chunks[c]["nth"] + 1)

            nc.gpsimd.memset(x_hi[:, KD * T1:].bitcast(F32), 0.0).then_inc(s_pad, 1)
            nc.gpsimd.memset(x_lo[:, KD * T1:].bitcast(F32), 0.0).then_inc(s_pad, 1)
            pool.wait_ge(s_const, 48)
            for j in range(16):
                cos_part(j, wide[:, j, :], cos1, T1, act_chunk(chunk_of("da_qkv", j)))
            for j in range(4):
                cos_part(ROPE_BASE["idx"] + j, wide[:, j, :], cos1, T1, act_chunk(chunk_of("dsa_in", j)))
            cos_part(ROPE_BASE["idx"] + 4, wide[0:64, 5, :], cos1, T1, (s_app, norms["ki"]["ap"] + 1), 64)
            pool.wait_ge(s_idxa, 24)
            for j in range(16):
                cos_part(ROPE_BASE["dsa"] + j, wide[:, 6 + j, :], cos1, T1, act_chunk(chunk_of("dsa_in", 20 + j)))
            pool.wait_ge(s_even, 64)
            nc.gpsimd.affine_select(out=wsT, in_=wsT, compare_op=ALU.is_ge, fill=0.0, base=0,
                                    pattern=[[0, 8], [1, P]], channel_multiplier=-1).then_inc(s_ws, 1)
            pool.wait_ge(s_sincos, 1)
            cos_part(ROPE_BASE["kr"], oT[:, 6, 0:T2], cs2[:, 0, :], T2, (s_kr, 1))
            for r in range(4):
                cos_part(ROPE_BASE["mq"] + r, wide[:, 14 + r, 0:T2], cs2[:, 0, :], T2,
                         (s_app, norms[f"q{2 * r + 1}"]["ap"] + 2))

        @block.vector
        def _(dve):
            V = nc.vector

            def step(ins):
                step.n += 1
                ins.then_inc(s_dve, 1)
                dve.wait_ge(s_dve, step.n)
            step.n = 0

            def norm_inv(name, T, dim):
                m = norms[name]
                b = rinv[:, m["id"] % 2, 0:T]
                dve.wait_ge(s_col, m["id"] + 1)
                if m["id"] >= 2:
                    dve.wait_ge(s_rstd, m["id"] - 1)
                step(V.tensor_scalar(b, bank[:, B_COL, 0:T], 1.0 / dim, EPS, ALU.mult, ALU.add))
                V.reciprocal(b, b).then_inc(s_rinv, 1)

            def norm_apply(name, T, ops, shift=0):
                m = norms[name]
                dve.wait_ge(s_rstd, m["id"] + 1)
                for o, s, g, a, n in ops:
                    V.scalar_tensor_tensor(out=o, in0=s, scalar=g, in1=rstd[a:a + n, m["id"] % 2, shift:shift + T],
                                           op0=ALU.mult, op1=ALU.mult).then_inc(s_app, 1)

            def low(at, hi, lo, src):
                for i in range(len(src)):
                    dve.wait_ge(s_xhi, at + i + 1)
                    V.tensor_tensor(lo[i], src[i], hi[i].bitcast(F32), ALU.subtract).then_inc(s_xlo, 1)

            def norm_split(name, T, n, src, gain, at, first=0):
                m = norms[name]
                for c in range(n + 2):
                    if c < n:
                        norm_apply(name, T, [(sq[:, (m["sq"] + c) % SQ_SLOTS, 0:T], src[c], col(gain, at + c), 0, P)])
                    if c >= 2:
                        i = c - 2
                        o = slice((first + i) * T1, (first + i) * T1 + T)
                        low(splits[name] + i, [x_hi[:, o]], [x_lo[:, o]], [sq[:, (m["sq"] + i) % SQ_SLOTS, 0:T]])

            def norm_h(name, T, gain, at):
                norm_inv(name, T, D)
                norm_split(name, T, KD, [h[:, c, 0:T] for c in range(KD)], gain, at)

            def low_mix(name, T):
                low(splits[name], [mix_hi[:, c, 0:T] for c in range(KD)], [mix_lo[:, c, 0:T] for c in range(KD)],
                    [oT[:, c, 0:T] for c in range(KD)])

            def ahead(c):
                weights_ahead(dve, rest_panel, c)

            def residual(stage, T, scale=None):
                for i in range(8):
                    c = chunk_of(stage, i)
                    ahead(c)
                    dve.wait_ge(s_chunk, c + 1)
                    src, dst = dense_bank(c)[:, 0:T], h[:, i, 0:T]
                    if scale is None:
                        ins = V.tensor_tensor(dst, src, dst, ALU.add)
                    else:
                        ins = V.scalar_tensor_tensor(out=dst, in0=src, scalar=scale, in1=dst, op0=ALU.mult,
                                                     op1=ALU.add)
                    ins.then_inc(s_free["dve"], 1)

            def rope(r, out_, table, T, rows=P):
                dve.wait_ge(s_rot, r + 1)
                step(V.tensor_tensor(t2[0:rows, r % 2, 0:T], bank[0:rows, B_S + r % 2, 0:T], table[0:rows, 0:T],
                                     ALU.mult))
                dve.wait_ge(s_t1, r + 1)
                V.tensor_tensor(out_, t1[0:rows, r % 2, 0:T], t2[0:rows, r % 2, 0:T], ALU.add).then_inc(s_rope, 1)

            def attention(name, scale, mask):
                U = att[name]["units"]
                for i in range(len(U) + 1):
                    if i < len(U):
                        x = U[i]
                        q, k = x["qn"], x["kn"]
                        for s in x["scores"]:
                            dve.wait_ge(s_score, s + 1)
                            if s >= 4:
                                dve.wait_ge(s_exp, s - 3)
                            step(V.tensor_tensor_reduce(sm[0:q, s % 4, 0:k], bank[0:q, B_S + s % 2, 0:k],
                                                        tile_of(mask, x["t"])[0:q, :], 1.0, -3e38, ALU.add, ALU.max,
                                                        mx[0:q, s % 8:s % 8 + 1]))
                            V.tensor_scalar(nmx[0:q, s % 8:s % 8 + 1], mx[0:q, s % 8:s % 8 + 1], -scale, None,
                                            ALU.mult).then_inc(s_max, 1)
                    if i >= 1:
                        x = U[i - 1]
                        q, k, u = x["qn"], x["kn"], x["u"]
                        s = x["scores"]
                        dve.wait_ge(s_exp, s[-1] + 1)
                        if u >= 2:
                            dve.wait_ge(s_tr, u - 1)
                        a = s[0] % 8
                        step(V.reciprocal(rs[0:q, a:a + len(s)], ssum[0:q, a:a + len(s)]))
                        if len(s) == 1:
                            V.tensor_scalar(pn[0:q, u % 2, 0:k], pr[0:q, s[0] % 4, 0:k], rs[0:q, a:a + 1], None,
                                            ALU.mult).then_inc(s_prob, 1)
                        else:
                            step(V.tensor_scalar(rl[0:q], rs[0:q, a + 1:a + 2], lam[0:q], None, ALU.mult))
                            p1 = pr[0:q, s[1] % 4, 0:k]
                            step(V.tensor_scalar(p1, p1, rl[0:q], None, ALU.mult))
                            V.scalar_tensor_tensor(out=pn[0:q, u % 2, 0:k], in0=pr[0:q, s[0] % 4, 0:k],
                                                   scalar=rs[0:q, a:a + 1], in1=p1, op0=ALU.mult,
                                                   op1=ALU.subtract).then_inc(s_prob, 1)

            dve.wait_ge(s_const, 48)
            for n in range(AHEAD):
                rest_panel(dve, n)
            la = VEC_AT["lam"][0]
            V.tensor_tensor(lam_p[0:64, :], vec[0:64, la:la + 2], vec[0:64, la + 2:la + 4], ALU.mult)\
                .then_inc(s_lam, 1)
            V.tensor_scalar(subln8, col("subln"), 1.0 - LAMBDA_INIT, None, ALU.mult)
            lr = vec[:, VEC_AT["lb_raw"][0]:VEC_AT["lb_raw"][0] + 4]
            V.tensor_tensor(lb_t, lr, lr, ALU.subtract).then_inc(s_lbd, 1)
            dve.wait_ge(s_lbe, 1)
            step(V.reciprocal(oml, lb))
            step(V.tensor_tensor(lb_t, lb, oml, ALU.mult))
            step(V.tensor_tensor(lb, lb_t, lb_t, ALU.subtract))
            step(V.tensor_scalar(lb, lb, 0.0, 0.999, ALU.max, ALU.min))
            step(V.tensor_scalar(oml, lb, -1.0, 1.0, ALU.mult, ALU.add))
            dve.wait_ge(s_lame, 1)
            step(V.tensor_tensor(lam, lam_e[:, 0:1], lam_e[:, 1:2], ALU.subtract))
            step(V.tensor_scalar(lam, lam, LAMBDA_INIT, None, ALU.add))

            norm_h("da", T1, "da_norm", 0)
            for j in range(28):
                ahead(chunk_of("da_qkv", j))
                if 2 <= j < 18:
                    rope(j - 2, (qT if j < 10 else kT)[:, (j - 2) % 8, :], sin1, T1)
            attention("da", 64 ** -0.5, causal)
            for hh in range(9):
                if hh < 8:
                    norm_inv(f"o{hh}", T1, P)
                if hh >= 1:
                    o = oT[:, hh - 1, :]
                    norm_apply(f"o{hh - 1}", T1, [(o, o, subln8, 0, P)])
            low_mix("da_mix", T1)
            residual("da_out", T1)
            norm_h("conv0", T1, "ffn_norm", 0)

            def hid_split(g):
                return splits[f"hid{g // KF}"] + g % KF

            def low_hidden(g, T):
                j = g % KF
                low(hid_split(g), [hid_hi[:, j, 0:T]], [hid_lo[:, j, 0:T]], [hid_buf(g)[:, 0:T]])

            def conv_up(i):
                for j in range(KF + 1):
                    if j < KF:
                        for g in range(2):
                            c = chunk_of(f"conv{i}_up", 2 * j + g)
                            n = i * 2 * KF + 2 * j + g
                            ch = j + g * KF
                            cb, b = conv_buf(n), dense_bank(c)
                            ahead(c)
                            dve.wait_ge(s_conv, n + 1)
                            step(V.scalar_tensor_tensor(out=cb[:, 1:T1], in0=b[:, 0:T1 - 1],
                                                        scalar=col("conv_w", (i * 3 + 1) * 44 + ch),
                                                        in1=cb[:, 1:T1], op0=ALU.mult, op1=ALU.add))
                            V.scalar_tensor_tensor(out=cb[:, 2:T1], in0=b[:, 0:T1 - 2],
                                                   scalar=col("conv_w", (i * 3) * 44 + ch), in1=cb[:, 2:T1],
                                                   op0=ALU.mult, op1=ALU.add).then_inc(s_free["dve"], 1)
                    if j >= 1:
                        n = i * 2 * KF + 2 * (j - 1)
                        dve.wait_ge(s_silu, n // 2 + 1)
                        c = chunk_of(f"conv{i}_up", 2 * (j - 1) + 1)
                        dve.wait_ge(s_free["dve"], chunks[c]["nth"] + 1)
                        g = i * KF + j - 1
                        if g >= 2:
                            dve.wait_ge(s_xlo, hid_split(g - 2) + 1)
                        V.tensor_tensor(hid_buf(g), silu_buf(n // 2), conv_buf(n + 1), ALU.mult).then_inc(s_hid, 1)
                    if j >= 2:
                        low_hidden(i * KF + j - 2, T1)
                low_hidden(i * KF + KF - 1, T1)
            conv_up(0)
            residual("conv0_down", T1)

            norm_h("dsa", T1, "dsa_norm", 0)
            work = sm

            def index_add(x):
                t, hh = divmod(x, 8)
                q0, q = TILES1[t]
                dve.wait_ge(s_relu, x + 1)
                rx, w = pr[0:q, x % 2, 0:q0 + q], wi_tok[0:q, t, hh:hh + 1]
                acc = work[0:q, t, 0:q0 + q]
                if hh == 0:
                    ins = V.tensor_scalar(acc, rx, w, None, ALU.mult)
                else:
                    ins = V.scalar_tensor_tensor(out=acc, in0=rx, scalar=w, in1=acc, op0=ALU.mult, op1=ALU.add)
                ins.then_inc(s_idxa, 1)
                dve.wait_ge(s_idxa, x + 1)

            def top_eight(r):
                t, i = divmod(r, TOPK // 8)
                q0, q = TILES1[t]
                a, b = [work[0:q, y, 0:q0 + q] for y in ((t, 3) if i % 2 == 0 else (3, t))]
                if i == 0:
                    step(V.tensor_tensor(a, a, tile_of(keep, t)[0:q, :], ALU.mult))
                    step(V.tensor_tensor(a, a, tile_of(addm, t)[0:q, :], ALU.add))
                step(V.max(max8[0:q], a))
                step(V.match_replace(b, max8[0:q], a, -3e38))
                if i == TOPK // 8 - 1:
                    step(V.tensor_scalar(a, b, -2e38, NEG, ALU.is_gt, ALU.mult))
                    step(V.tensor_tensor(tile_of(amask, t)[0:q, :], a, tile_of(causal, t)[0:q, :], ALU.add))

            for j in range(36):
                ahead(chunk_of("dsa_in", j))
                if 2 <= j < 6:
                    rope(ROPE_BASE["idx"] + j - 2, qT[:, 8 + j - 2, :], sin1, T1)
                if j == 7:
                    norm_inv("ki", T1, 64)
                    norm_apply("ki", T1, [(wide[0:64, 5, :], wide[0:64, 4, :], col("idxk", 0, 0, 64), 0, 64)])
                    rope(ROPE_BASE["idx"] + 4, kT[0:64, 8, :], sin1, T1, 64)
                    dve.wait_ge(s_free["act"], chunks[chunk_of("dsa_in", 7)]["nth"] + 1)
                if 8 <= j < 20:
                    index_add(2 * (j - 8))
                    index_add(2 * (j - 8) + 1)
                if j == 20:
                    dve.wait_ge(s_idxc, 16)
                if j >= 20:
                    for r in range(3 * (j - 20) // 2, 3 * (j - 19) // 2):
                        top_eight(r)
                if j >= 22:
                    rope(ROPE_BASE["dsa"] + j - 22, (qT if j < 30 else kT)[:, (j - 22) % 8, :], sin1, T1)
            for i in (14, 15):
                rope(ROPE_BASE["dsa"] + i, kT[:, i % 8, :], sin1, T1)
            attention("dsa", 64 ** -0.5, amask)
            low_mix("dsa_mix", T1)
            dve.wait_ge(s_pos, 16)
            ang, kf = t1[:, 1, 0:T2], rinv[:, 0, 0:T2]
            step(V.tensor_copy(ang, pos_sb[:, :]))
            step(V.tensor_scalar(ang, ang, con("inv"), None, ALU.mult))
            magic = float(1.5 * 2 ** 23)
            for i, shift in enumerate((0.25, 0.0)):
                r = t2[:, i, 0:T2]
                step(V.tensor_scalar(kf, ang, 1.0 / TWO_PI, shift, ALU.mult, ALU.add))
                step(V.tensor_scalar(kf, kf, magic, None, ALU.add))
                step(V.tensor_scalar(kf, kf, -magic, -shift, ALU.add, ALU.add))
                c1 = 6.28125
                c2 = float(np.float32(np.round((TWO_PI - c1) * 2 ** 19) / 2 ** 19))
                c3 = float(np.float32(TWO_PI - c1 - c2))
                src = ang
                for cc in (c1, c2, c3):
                    step(V.scalar_tensor_tensor(out=r, in0=kf, scalar=-cc, in1=src, op0=ALU.mult, op1=ALU.add))
                    src = r
                V.tensor_scalar(r, r, float(np.float32(3.1415925)), -float(np.float32(3.1415925)),
                                ALU.min, ALU.max).then_inc(s_ang, 1)
            residual("dsa_out", T1)
            norm_h("conv1", T1, "ffn_norm", 8)
            conv_up(1)
            residual("conv1_down", T1)
            norm_inv("final", T1, D)
            norm_apply("final", T2, [(wide[:, c, 0:T2], h[:, c, META:T1], col("final", c), 0, P) for c in range(KD)],
                       shift=META)

            def glu(i, j):
                norm_h(f"glu{i}{j}", T2, "gains", 8 * (5 * i + 2 * j))
                for n in range(KF):
                    c = chunk_of(f"glu{i}{j}_up", 2 * n)
                    g = 2 * KF + (2 * i + j) * KF + n
                    ahead(c)
                    ahead(c + 1)
                    dve.wait_ge(s_free["act"], chunks[c]["nth"] + 1)
                    dve.wait_ge(s_chunk, c + 2)
                    dve.wait_ge(s_xlo, hid_split(g - 2) + 1)
                    V.tensor_tensor(hid_buf(g)[:, 0:T2], dense_bank(c + 1)[:, 0:T2], silu_buf(g)[:, 0:T2], ALU.mult)\
                        .then_inc(s_hid, 1)
                    if n >= 1:
                        low_hidden(g - 1, T2)
                low_hidden(g, T2)
                residual(f"glu{i}{j}_down", T2, 0.5)

            def ple(i):
                norm_h(f"pleh{i}", T2, "gains", 8 * (5 * i + 3))
                dve.wait_ge(s_ple, 16 * (i + 1))
                low(splits[f"ple{i}"], [ple_hi[:, c, 0:T2] for c in range(2)], [ple_lo[:, c, 0:T2] for c in range(2)],
                    [oT[:, c, 0:T2] for c in range(2)])
                for c in range(KD):
                    ahead(chunk_of(f"ple{i}_gate", c))
                for c in range(KD):
                    cc = chunk_of(f"ple{i}_proj", c)
                    ahead(cc)
                    dve.wait_ge(s_chunk, cc + 1)
                    dve.wait_ge(s_free["act"], chunks[chunk_of(f"ple{i}_gate", c)]["nth"] + 1)
                    V.tensor_tensor(wide[:, 8 + c, 0:T2], dense_bank(cc)[:, 0:T2], wide[:, c, 0:T2], ALU.mult)\
                        .then_inc(s_free["dve"], 1)
                norm_inv(f"pleo{i}", T2, D)
                norm_apply(f"pleo{i}", T2, [(wide[:, c, 0:T2], wide[:, 8 + c, 0:T2],
                                             col("gains", 8 * (5 * i + 4) + c), 0, P) for c in range(KD)])
                for c in range(KD):
                    dve.wait_ge(s_app, norms[f"pleo{i}"]["ap"] + c + 1)
                    V.tensor_tensor(h[:, c, 0:T2], wide[:, c, 0:T2], h[:, c, 0:T2], ALU.add).then_inc(s_final, 1)

            dve.wait_ge(s_final, 8)
            glu(0, 0)
            norm_h("ev", T2, "gains", 8)
            slot = lambda i: part(i * 1024, 1024)
            n0 = chunks[chunk_of("ev_in", 0)]["nth"]

            def ev_ahead(a, b):
                for c in range(a, b):
                    ahead(chunk_of("ev_in", c))
            ev_ahead(0, 6)
            dve.wait_ge(s_free["act"], n0 + 4)
            sig, kf_ = slot(1), slot(3)
            for hh in range(4):
                ps_ = slice(hh * T2, (hh + 1) * T2)
                ins = V.tensor_scalar(sig[:, ps_], sig[:, ps_], oml[:, hh:hh + 1], lb[:, hh:hh + 1], ALU.mult, ALU.add)
            step(ins)
            V.tensor_scalar(kf_, sig, 1e-6, None, ALU.max).then_inc(s_f, 1)
            dve.wait_ge(s_f, 1)
            V.tensor_scalar(sig, sig, -1.0, 1.0, ALU.mult, ALU.add).then_inc(s_lvq, 1)
            dve.wait_ge(s_lvq, 1)
            ev_ahead(6, 12)
            dve.wait_ge(s_free["act"], n0 + 8)
            dve.wait_ge(s_ln, 1)
            a, b = 2, 3
            c64 = lambda i: slot(i).rearrange("p (n c) -> p n c", c=CHUNK)
            for s in (1, 2, 4, 8, 16, 32):
                V.tensor_copy(c64(b)[:, :, 0:s], c64(a)[:, :, 0:s])
                step(V.tensor_tensor(c64(b)[:, :, s:CHUNK], c64(a)[:, :, s:CHUNK], c64(a)[:, :, 0:CHUNK - s],
                                     ALU.add))
                a, b = b, a
            assert a == 2
            ev_ahead(12, 16)
            scT = part(10 * 1024, 1024, 512)
            tmp = pT[:, :, :].rearrange("p a b -> p (a b)")[:, 0:512]
            dve.wait_ge(s_even, 64)

            def add_level(lv):
                for t in range(2):
                    dve.wait_ge(s_lvm, 2 * lv + t + 1)
                    v3 = lambda z: z.rearrange("p (h t) -> p h t", h=4)
                    mk = lmask[:, lv:lv + 1, :].to_broadcast([P, 4, P])
                    if lv == 0:
                        V.tensor_tensor(v3(scT[:, t, :]), v3(bank[:, B_S + t, :]), mk, ALU.mult).then_inc(s_lva, 1)
                    else:
                        step(V.tensor_tensor(v3(tmp), v3(bank[:, B_S + t, :]), mk, ALU.mult))
                        V.tensor_tensor(scT[:, t, :], scT[:, t, :], tmp, ALU.add).then_inc(s_lva, 1)
                    dve.wait_ge(s_lva, 2 * lv + t + 1)

            def exponents(lv):
                m = LEVELS[lv - 1]
                v = lambda i: slot(i).rearrange("p (n s m) -> p n s m", s=2, m=m)
                e, bb = v(4 + lv % 2), v(2)
                nb = 512 // m
                ref = bb[:, :, 0, m - 1:m].to_broadcast([P, nb, m])
                V.tensor_tensor(e[:, :, 0, :], ref, bb[:, :, 0, :], ALU.subtract)
                V.tensor_tensor(e[:, :, 1, :], bb[:, :, 1, :], ref, ALU.subtract).then_inc(s_lvd, 1)

            def operands(lv):
                dve.wait_ge(s_lve, lv)
                if lv >= 3:
                    dve.wait_ge(s_lvm, 2 * (lv - 2) + 2)
                V.tensor_tensor(slot(6 + lv % 2), slot(0), slot(4 + lv % 2), ALU.mult)
                V.tensor_tensor(slot(8 + lv % 2), slot(1), slot(4 + lv % 2), ALU.mult).then_inc(s_lvq, 1)

            exponents(1)
            gv = slot(14)
            ev_ahead(16, 24)
            dve.wait_ge(s_free["act"], n0 + 16)
            step(V.tensor_tensor(slot(10), gv, gv, ALU.mult))
            step(V.tensor_reduce(vms, slot(10).rearrange("p (g d) -> p g d", d=64), AX.X, ALU.add))
            step(V.tensor_scalar(vms, vms, 1.0 / 64, EPS, ALU.mult, ALU.add))
            V.reciprocal(vms, vms).then_inc(s_vms, 1)
            dve.wait_ge(s_vrs, 1)
            g64 = lambda z: z.rearrange("p (g d) -> p g d", d=64)
            step(V.tensor_tensor(g64(gv), g64(gv), vms.rearrange("p (g o) -> p g o", o=1).to_broadcast([P, 16, 64]),
                                 ALU.mult))
            for t in range(2):
                ins = V.tensor_tensor(gv[:, t * 512:(t + 1) * 512], gv[:, t * 512:(t + 1) * 512], vn, ALU.mult)
            ins.then_inc(s_gv, 1)
            add_level(0)
            for lv in range(1, 7):
                if lv < 6:
                    exponents(lv + 1)
                operands(lv)
                add_level(lv)
            c5_, b5 = c64(5), c64(2)
            V.tensor_tensor(c5_, b5[:, :, CHUNK - 1:CHUNK].to_broadcast([P, 16, CHUNK]), b5, ALU.subtract)\
                .then_inc(s_lvd, 1)
            dve.wait_ge(s_lve, 7)
            V.tensor_tensor(slot(6), slot(0), slot(4), ALU.mult)
            V.tensor_tensor(slot(7), slot(1), slot(5), ALU.mult).then_inc(s_gate, 1)
            gu = slot(12).rearrange("p (c t) -> p c t", c=4)
            dve.wait_ge(s_free["act"], n0 + 20)
            for t in range(2):
                dve.wait_ge(s_mixp, t + 1)
                v3 = lambda z: z.rearrange("p (h t) -> p h t", h=4)
                step(V.tensor_tensor(v3(tmp), v3(bank[:, B_COL + t, :]), bs, ALU.add))
                V.tensor_tensor(oT[:, 0:4, t * P:(t + 1) * P], v3(tmp), gu[:, :, t * P:(t + 1) * P], ALU.mult)\
                    .then_inc(s_mix, 1)
                dve.wait_ge(s_mix, t + 1)
            states = part(8 * 1024, 1536, 512)
            el = e_last.rearrange("p (h n) -> p h n", h=4)
            for n in range(3):
                dve.wait_ge(s_upd, n + 1)
                v3 = lambda z: z.rearrange("p (h t) -> p h t", h=4)
                if n == 0:
                    V.tensor_copy(states[:, 0, :], bank[:, B_S, :]).then_inc(s_st, 1)
                else:
                    step(V.tensor_tensor(v3(tmp), v3(states[:, n - 1, :]), el[:, :, n:n + 1].to_broadcast([P, 4, P]),
                                         ALU.mult))
                    V.tensor_tensor(states[:, n, :], bank[:, B_S + n % 2, :], tmp, ALU.add).then_inc(s_st, 1)
                dve.wait_ge(s_st, n + 1)
            dve.wait_ge(s_free["act"], n0 + 24)
            for hh in range(5):
                if hh < 4:
                    norm_inv(f"hg{hh}", T2, P)
                if hh >= 1:
                    i = hh - 1
                    o = slot(3)[:, i * T2:(i + 1) * T2]
                    norm_apply(f"hg{i}", T2, [(o, o, col("hg_out"), 0, P)])
                    dve.wait_ge(s_app, norms[f"hg{i}"]["ap"] + 1)
                    V.tensor_tensor(oT[:, 4 + i, 0:T2], o, slot(13)[:, i * T2:(i + 1) * T2], ALU.mult)\
                        .then_inc(s_gate, 1)
            low_mix("ev_mix", T2)
            residual("ev_out", T2)
            glu(0, 1)
            ple(0)
            glu(1, 0)
            norm_h("mla", T2, "gains", 8 * 6)
            for c in range(6):
                ahead(chunk_of("mla_in", c))
            norm_inv("cq", T2, 384)
            norm_inv("ckv", T2, 256)
            norm_split("cq", T2, 3, [wide[:, c, 0:T2] for c in range(3)], "qa", 0)
            norm_split("ckv", T2, 2, [wide[:, 3 + c, 0:T2] for c in range(2)], "kva", 0, first=3)
            for c in range(12):
                ahead(chunk_of("mla_q", c))
            for c in range(12):
                ahead(chunk_of("mla_kv", c))
            f0 = chunks[chunk_of("mla_in", 0)]["nth"]
            dve.wait_ge(s_free["act"], f0 + 6)
            V.tensor_scalar(oT[:, 6, 0:T2], wide[:, 5, 0:T2], col("kr"), None, ALU.mult).then_inc(s_kr, 1)
            dve.wait_ge(s_sincos, 1)
            rope(ROPE_BASE["kr"], oT[:, 7, 0:T2], cs2[:, 1, :], T2)
            dve.wait_ge(s_rope, ROPE_BASE["kr"] + 1)
            heads = []
            for hh in range(8):
                a = 64 * (hh % 2)
                heads.append((f"q{hh}", [(qT[:, hh, 0:T2], wide[:, 6 + hh, 0:T2], col("qn"), 0, P),
                                         (wide[a:a + 64, 14 + hh // 2, 0:T2], wide[a:a + 64, 14 + hh // 2, 0:T2],
                                          col("qr", 0, a, 64), a, 64)]))
            for hh in range(8):
                a = 64 * (hh % 2)
                heads.append((f"k{hh}", [(kT[:, hh, 0:T2], kT[:, hh, 0:T2], col("kn"), 0, P),
                                         (kT[a:a + 64, 8 + hh // 2, 0:T2], oT[a:a + 64, 7, 0:T2],
                                          1.0, a, 64)]))
            for i in range(17):
                if i < 16:
                    norm_inv(heads[i][0], T2, 192)
                if i >= 1:
                    norm_apply(heads[i - 1][0], T2, heads[i - 1][1])
            for r in range(4):
                rope(ROPE_BASE["mq"] + r, qT[:, 8 + r, 0:T2], cs2[:, 1, :], T2)
            attention("mla", 192 ** -0.5, causal)
            low_mix("mla_mix", T2)
            residual("mla_out", T2)
            glu(1, 1)
            ple(1)


WEIGHTS = [("da_w_qkv", "da_w_qkv"), ("da_w_o", "da_w_o"), ("dsa_w_in", "dsa_w_in"), ("dsa_w_o", "dsa_w_o"),
           ("ffn_w_up", "ffn_w_up"), ("ffn_w_down", "ffn_w_down"), ("ffn_w_gate", "ffn_w_gate_2"),
           ("ffn_w_up_2", "ffn_w_up_2"), ("ffn_w_down_2", "ffn_w_down_2"), ("ple_w_gate", "ple_w_gate_2"),
           ("ple_w_proj", "ple_w_proj_2"), ("even_w_in", "even_w_in_2"), ("even_w_out", "even_w_out_2"),
           ("mla_w_in", "mla_w_in_2"), ("mla_w_q_b", "mla_w_q_b_2"), ("mla_w_kv_b", "mla_w_kv_b_2"),
           ("mla_w_out", "mla_w_out_2")]


def kernel(**inputs):
    import concourse.bacc as bacc
    from concourse.bass_utils import run_bass_kernel_spmd

    a = {k: np.asarray(v) for k, v in inputs.items()}

    def cols(v):
        return v.reshape(-1, P).T

    def twice(v):
        return np.concatenate([v, v]).reshape(P, 1)

    sc = shape_constants()
    z = np.zeros((64,), np.float32)
    pad = lambda v: np.concatenate([v.reshape(-1), z]).reshape(P, 1)
    v = {
        "da_norm": cols(a["da_norm"]), "subln": cols(a["da_subln"]), "dsa_norm": cols(a["dsa_norm"]),
        "idxk": pad(a["dsa_idx_k_norm"]), "ffn_norm": cols(a["ffn_norm"]), "conv_w": cols(a["ffn_conv_w"]),
        "conv_b": cols(a["ffn_conv_b"]), "final": cols(a["final_norm"]), "gains": cols(a["norm_gains_2"]),
        "lb_raw": cols(a["hgrn_lb_raw_2"]), "hg_out": cols(a["hgrn_out_norm_2"]), "qa": cols(a["mla_q_a_norm_2"]),
        "kva": cols(a["mla_kv_a_norm_2"]), "qn": cols(a["mla_q_norm_2"][0, 0:P]), "qr": twice(a["mla_q_norm_2"][0, P:]),
        "kn": cols(a["mla_k_norm_2"][0, 0:P]), "kr": twice(a["mla_k_norm_2"][0, P:]),
        "lam": np.concatenate([pad(a[f"da_lambda_{n}"][0]) for n in ("q1", "q2", "k1", "k2")], 1),
    }
    bs = a["gmlp_b_s_2"][0].reshape(4, 2, 1, P)
    e = {
        "lmask": level_masks(),
        "wsT": a["gmlp_w_s_2"][0].transpose(2, 0, 1).reshape(P, -1),
        "bs": np.broadcast_to(bs, (4, 2, 64, P)).transpose(1, 2, 0, 3).reshape(P, -1),
        "vnorm": np.broadcast_to(a["gmlp_v_norm_2"][0].reshape(1, -1), (P, 512)),
    }
    arrays = {
        "hT": np.concatenate([a["meta_tokens"], a["x"][0]], 0).T,
        "consts": np.concatenate([sc[n] for n, _ in CONST_PARTS], 1),
        "idxc": index_constants(),
        "vecs": np.concatenate([v[n] for n, _ in VEC_PARTS], 1),
        "evenc": np.concatenate([e[n] for n, _ in EVEN_PARTS], 1),
        "pleT": a["p_2"][:, 0].transpose(0, 2, 1),
        "pos": np.broadcast_to(a["positions_2"].reshape(1, -1), (P, T2)),
    }
    for name, src in WEIGHTS:
        arrays["w_" + name] = a[src]
    arrays = {k: np.ascontiguousarray(x) for k, x in arrays.items()}

    nc = bacc.Bacc("TRN2", target_bir_lowering=False, num_devices=1)
    ap = {k: nc.dram_tensor(k, x.shape, mybir.dt.from_np(x.dtype), kind="ExternalInput").ap()
          for k, x in arrays.items()}
    out = nc.dram_tensor("outT", (D, T2), F32, kind="ExternalOutput").ap()
    build(nc, {n: ap["w_" + n] for n, _ in WEIGHTS}, ap["hT"], ap["consts"], ap["idxc"], ap["vecs"], ap["evenc"],
          ap["pleT"], ap["pos"], out)
    r = run_bass_kernel_spmd(nc, [arrays], core_ids=[0])
    return r.results[0]["outT"].T[None].copy()
```

```python
from contextlib import ExitStack

import numpy as np
import concourse.bass as bass
from concourse import mybir

F32 = mybir.dt.float32
F32R = mybir.dt.float32r
I32 = mybir.dt.int32
U32 = mybir.dt.uint32
ACT = mybir.ActivationFunctionType
ALU = mybir.AluOpType
AX = mybir.AxisListType

P = 128
D = 1024
KD = D // P
META = 16
T2 = 256
T1 = T2 + META
F = 2816
KF = F // P
EPS = 1e-6
THETA = 10000.0
NEG = -1e30
LAMBDA_INIT = 0.2
TOPK = 64
IDX_HEADS = 8
CHUNK = 64
TILES1 = [(0, 128), (128, 128), (256, 16)]
TILES2 = [(0, 128), (128, 128)]
SLOT = 2048
RAW = 3
SPLIT = 3
AHEAD = 2
DENSE_BANKS = (0, 1, 2, 4, 7)
B_COL, B_S, B_PT = 3, 5, 7
S_BANKS = (5, 6, 0, 1)
LEVEL_BANKS = ((5, 6), (0, 1))
B_LAST = 2
O_BANKS = (4, 3)
SQ_SLOTS = 8
MASK_AT = (0, 128, 384)
MASK_N = 656
TWO_PI = 2.0 * np.pi


def shape_constants():
    c = {}
    c["ident"] = np.eye(P, dtype=np.float32)
    c["ones"] = np.ones((P, P), np.float32)
    rot = np.zeros((P, P), np.float32)
    for i in range(P):
        if i % 64 < 32:
            rot[i + 32, i] = -1.0
        else:
            rot[i - 32, i] = 1.0
    c["rot"] = rot
    inv = np.float32(THETA) ** (-np.arange(0, 64, 2, dtype=np.float32) / np.float32(64))
    ang = np.arange(T1, dtype=np.float32)[None, :] * inv.astype(np.float32)[:, None]
    c["cos"] = np.tile(np.cos(ang), (4, 1)).astype(np.float32)
    c["sin"] = np.tile(np.sin(ang), (4, 1)).astype(np.float32)
    c["inv"] = np.tile(inv[:, None], (4, 1)).astype(np.float32)
    q = np.arange(P)[:, None, None] + 128 * np.arange(3)[None, :, None]
    q[:, 2] = 256 + q[:, 0] % 16
    k = np.arange(T1)[None, None, :]
    causal = k <= q
    c["causal"] = packed(np.where(causal, 0.0, NEG))
    return c


def packed(m):
    return np.concatenate([m[:, t, :q0 + qn] for t, (q0, qn) in enumerate(TILES1)], 1).astype(np.float32)


def index_constants():
    q = np.arange(P)[:, None, None] + 128 * np.arange(3)[None, :, None]
    k = np.arange(T1)[None, None, :]
    causal = k <= q
    keep = causal & (k >= META)
    add = np.where(causal, np.where(k < META, 1e30, 0.0), -1e38)
    return np.concatenate([packed(keep), packed(add)], 1)


def level_masks():
    s = np.arange(P)[:, None]
    t = np.arange(P)[None, :]
    out = [(s == t)]
    for m in LEVELS:
        out.append((s // (2 * m) == t // (2 * m)) & (s % (2 * m) < m) & (t % (2 * m) >= m))
    return np.concatenate(out, 1).astype(np.float32)


LEVELS = [32, 16, 8, 4, 2, 1]

CONST_PARTS = [("ident", P), ("ones", P), ("rot", P), ("cos", T1), ("sin", T1), ("inv", 1), ("causal", MASK_N)]
VEC_PARTS = [("da_norm", 8), ("subln", 1), ("dsa_norm", 8), ("idxk", 1), ("ffn_norm", 16), ("conv_w", 2 * 3 * 44),
             ("conv_b", 2 * 44), ("final", 8), ("gains", 80), ("lb_raw", 4), ("hg_out", 1), ("qa", 3), ("kva", 2),
             ("qn", 1), ("qr", 1), ("kn", 1), ("kr", 1), ("lam", 4)]
EVEN_PARTS = [("lmask", 7 * P), ("wsT", 8 * P), ("bs", 4 * P), ("vnorm", 512)]


def offsets(parts):
    o, at = {}, 0
    for name, n in parts:
        o[name] = (at, n)
        at += n
    return o, at


CONST_AT, CONST_N = offsets(CONST_PARTS)
VEC_AT, VEC_N = offsets(VEC_PARTS)
EVEN_AT, EVEN_N = offsets(EVEN_PARTS)


class Plan:

    def __init__(self):
        self.panels = []
        self.chunks = []
        self.half = 0
        self.begin = {}
        self.stages = {}
        self.owned = {"act": 0, "dve": 0, "hid": 2 * KF}

    def stage(self, name):
        self.stages[name] = {"steps": [], "first": len(self.chunks), "n": 0}
        self.now = self.stages[name]

    def panel(self, loads, k, n):
        self.panels.append({"loads": loads, "k": k, "n": n})
        return len(self.panels) - 1

    def step(self, panel, kind, cols, size, k0, k, owner=None, tile=None, chunk=None, last=True):
        start = chunk is None
        if start:
            chunk = len(self.chunks)
            self.begin.setdefault(chunk, [])
            self.chunks.append({"owner": owner, "nth": self.owned[owner]})
            self.owned[owner] += 1
            self.now["n"] += 1
        if "free" not in self.panels[panel]:
            self.begin[chunk].append(panel)
        self.now["steps"].append(dict(panel=panel, kind=kind, cols=cols, size=size, k0=k0, k=k, tile=tile,
                                      chunk=chunk, start=start, stop=last))
        if last:
            self.panels[panel]["free"] = ("chunk", chunk + 1)
        else:
            self.half += 1
            self.panels[panel]["free"] = ("half", self.half)
        return chunk


def cut(a, n):
    return lambda v, k: v[:, k, a:a + n]


def make_plan(W):
    pl = Plan()

    def rows(w):
        return w.rearrange("(k p) n -> p k n", p=P)

    def feature_panels(w, c0, c1, owner, k=KD, width=256):
        for c in range(c0, c1, width):
            n = min(width, c1 - c)
            full = -(-n // P) * P
            loads = [(0, n, rows(w)[:, :, c:c + n])]
            if full > n:
                loads.append((n, full, rows(w)[:, :, 0:full - n]))
            p = pl.panel(loads, k, full)
            for m in range(0, full, P):
                pl.step(p, "fm", cut(m, P), P, 0, k, owner)

    def token_panels(w, c0, c1, owner, tiles):
        for c in range(c0, c1, 256):
            p = pl.panel([(0, 256, rows(w)[:, :, c:c + 256])], KD, 256)
            for t in range(len(tiles)):
                pl.step(p, "tm", cut(0, 256), 256, 0, KD, owner, tile=tiles[t])

    def up_panels(wg, wu, gate_owner, up_owner):
        for c in range(0, F, P):
            p = pl.panel([(0, P, rows(wg)[:, :, c:c + P]), (P, 2 * P, rows(wu)[:, :, c:c + P])], KD, 2 * P)
            pl.step(p, "fm", cut(0, P), P, 0, KD, gate_owner)
            pl.step(p, "fm", cut(P, P), P, 0, KD, up_owner)

    def down_panels(w):
        for c in range(0, D, 256):
            ids = [None, None]
            for k0, k in ((0, 8), (8, 8), (16, 6)):
                p = pl.panel([(0, 256, rows(w)[:, k0:k0 + k, c:c + 256])], k, 256)
                ids = [pl.step(p, "fm", cut(m * P, P), P, k0, k, "dve", chunk=ids[m], last=k0 + k == KF)
                       for m in range(2)]

    pl.stage("da_qkv")
    feature_panels(W["da_w_qkv"][0], 0, 2 * D, "act")
    token_panels(W["da_w_qkv"][0], 2 * D, 3 * D, "act", TILES1)
    pl.stage("da_out")
    feature_panels(W["da_w_o"][0], 0, D, "dve")
    for i in range(2):
        if i == 1:
            w = W["dsa_w_in"][0]
            pl.stage("dsa_in")
            feature_panels(w, 3072, 3584, "act")
            p = pl.panel([(0, 72, rows(w)[:, :, 3584:3656]), (72, P, rows(w)[:, :, 0:P - 72])], KD, P)
            pl.step(p, "fm", cut(0, P), P, 0, KD, "dve")
            for t in range(3):
                pl.step(p, "tm", cut(64, 8), 8, 0, KD, "act", tile=TILES1[t])
            token_panels(w, 2 * D, 3 * D, "act", TILES1)
            feature_panels(w, 0, 2 * D, "act")
            pl.stage("dsa_out")
            feature_panels(W["dsa_w_o"][0], 0, D, "dve")
        pl.stage(f"conv{i}_up")
        up_panels(W["ffn_w_up"][i][:, 0:F], W["ffn_w_up"][i][:, F:2 * F], "dve", "dve")
        pl.stage(f"conv{i}_down")
        down_panels(W["ffn_w_down"][i])
    for i in range(2):
        for j in range(2):
            if j == 1 and i == 0:
                w = W["even_w_in"][0]
                pl.stage("ev_in")
                feature_panels(w, 1536, 2048, "dve")
                feature_panels(w, 1024, 1536, "dve")
                token_panels(w, 2048, 2560, "act", TILES2)
                token_panels(w, 512, 1024, "act", TILES2)
                feature_panels(w, 0, 512, "dve")
                feature_panels(w, 2560, 3072, "dve")
                pl.stage("ev_out")
                feature_panels(W["even_w_out"][0], 0, D, "dve")
            if j == 1 and i == 1:
                pl.stage("mla_in")
                feature_panels(W["mla_w_in"][0], 0, 704, "dve")
                pl.stage("mla_q")
                for g in range(4):
                    w = W["mla_w_q_b"][0]
                    loads = []
                    for hh in range(2):
                        c = (2 * g + hh) * 192
                        loads.append((hh * P, (hh + 1) * P, rows(w)[:, :, c:c + P]))
                        loads.append((256 + hh * 64, 256 + hh * 64 + 64, rows(w)[:, :, c + P:c + 192]))
                    p = pl.panel(loads, 3, 384)
                    for m in range(0, 384, P):
                        pl.step(p, "fm", cut(m, P), P, 0, 3, "act")
                pl.stage("mla_kv")
                for g in range(2):
                    p = pl.panel([(0, 1024, rows(W["mla_w_kv_b"][0])[:, :, g * 1024:(g + 1) * 1024])], 2, 1024)
                    for hh in range(4):
                        pl.step(p, "fm", cut(hh * 256, P), P, 0, 2, "act")
                    for t in range(2):
                        pl.step(p, "tm", lambda v, k: v.rearrange("p k (h c) -> p k h c", c=256)[
                            :, k, :, 128:256], 512, 0, 2, "act", tile=TILES2[t])
                pl.stage("mla_out")
                feature_panels(W["mla_w_out"][0], 0, D, "dve")
            pl.stage(f"glu{i}{j}_up")
            up_panels(W["ffn_w_gate"][i][j], W["ffn_w_up_2"][i][j], "dve", "hid")
            pl.stage(f"glu{i}{j}_down")
            down_panels(W["ffn_w_down_2"][i][j])
        pl.stage(f"ple{i}_gate")
        feature_panels(W["ple_w_gate"][i], 0, D, "dve")
        pl.stage(f"ple{i}_proj")
        feature_panels(W["ple_w_proj"][i], 0, D, "dve", k=2, width=1024)
    return pl


DEFERRED = {"da": ("da_norm", 0), "dsa": ("dsa_norm", 0), "ev": ("gains", 8), "mla": ("gains", 48)}
for _i in range(2):
    DEFERRED.update({f"glu{_i}0": ("gains", 40 * _i), f"glu{_i}1": ("gains", 40 * _i + 16),
                     f"pleh{_i}": ("gains", 40 * _i + 24)})


def make_norms():
    order = [("da", 8, 8)] + [(f"o{h}", 1, 1) for h in range(8)] + [("conv0", 8, 8), ("dsa", 8, 8), ("ki", 1, 1),
             ("conv1", 8, 8), ("final", 8, 8), ("glu00", 8, 8), ("ev", 8, 8)]
    order += [(f"hg{h}", 1, 1) for h in range(4)] + [("glu01", 8, 8), ("pleh0", 8, 8), ("pleo0", 8, 8),
             ("glu10", 8, 8), ("mla", 8, 8), ("cq", 3, 3), ("ckv", 2, 2)]
    order += [(f"k{h}", 2, 2) for h in range(8)]
    order += [("glu11", 8, 8), ("pleh1", 8, 8), ("pleo1", 8, 8)]
    out, sq, ap, add = {}, 0, 0, 0
    for i, (name, n, m) in enumerate(order):
        prev = order[i - 1][1] if i else 0
        m = 0 if name in DEFERRED else m
        adds = 0 if name[0] == "k" else max(0, n - 2)
        out[name] = dict(id=i, sq=sq, n=n, ap=ap, m=m, alone=prev + n > SQ_SLOTS, add=add, adds=adds)
        sq, ap, add = sq + n, ap + m, add + adds
    out["by_id"] = [out[name] for name, _, _ in order]
    return out


def make_attention():
    out, s, u, oc = {}, 0, 0, 0
    for name, heads, tiles, comps, dv in (("da", 8, TILES1, 2, 128), ("dsa", 16, TILES1, 1, 64),
                                          ("mla", 8, TILES2, 1, 128)):
        units = []
        per = P // dv
        for h in range(heads):
            for t, (q0, qn) in enumerate(tiles[:2]):
                units.append(dict(h=h, t=t, q0=q0, qn=qn, kn=q0 + qn, u=u, scores=list(range(s, s + comps)),
                                  oc=oc + h // per, first=(h % per == 0 and t == 0),
                                  last=(h % per == per - 1 and t == 1), part=dv * (h % per), dv=dv, group=None,
                                  chunk=h // per, ktiles=[(a, min(n, P)) for a, n in tiles if a < q0 + qn]))
                s += comps
                u += 1
        for g in range(heads // 8 if len(tiles) == 3 else 0):
            units.append(dict(h=0, t=2, q0=256, qn=P, kn=T1, u=u, scores=list(range(s, s + comps)), dv=dv,
                              first=False, last=False, group=g, ktiles=list(tiles)))
            s += comps
            u += 1
        out[name] = dict(units=units, tiles=tiles, heads=heads)
        oc += heads * dv // P
    unit_of_score = [x["u"] for a in ("da", "dsa", "mla") for x in out[a]["units"] for _ in x["scores"]]
    return out, unit_of_score


def make_splits():
    order = [("da", 8), ("da_mix", 8), ("conv0", 8), ("hid0", KF), ("dsa", 8), ("dsa_mix", 8), ("conv1", 8),
             ("hid1", KF), ("glu00", 8), ("hid2", KF), ("ev", 8), ("ev_mix", 8), ("glu01", 8), ("hid3", KF),
             ("pleh0", 8), ("ple0", 2), ("glu10", 8), ("hid4", KF), ("mla", 8), ("cq", 3), ("ckv", 2),
             ("mla_mix", 8), ("glu11", 8), ("hid5", KF), ("pleh1", 8), ("ple1", 2)]
    out, at = {}, 0
    for name, n in order:
        out[name] = at
        at += n
    return out


ROPE_BASE = {"da": 0, "idx": 16, "dsa": 21, "kr": 37, "mq": 38}


def build(nc, W, hT, consts, idxc, vecs, evenc, pT_in, pos, out):
    plan = make_plan(W)
    norms = make_norms()
    att, unit_of_score = make_attention()
    chunks, stages, panels = plan.chunks, plan.stages, plan.panels
    splits = make_splits()

    with ExitStack() as ctx:
        def sb(name, shape, dt=F32):
            return ctx.enter_context(nc.sbuf_tensor(name, shape, dt))

        def sem(name):
            return ctx.enter_context(nc.semaphore(name))

        bank = ctx.enter_context(nc.psum_tensor("bank", [P, 8, 512], F32))
        arena_at = -(-nc.sbuf_base // 32) * 32
        arena = sb("arena", [P, 22 * T1 + 24 * T1 + 3072 + 8 * T1])

        def over(name, floats, shape):
            return nc.alloc_sbuf_tensor_at(name, shape, F32R, offset=arena_at + 4 * floats)

        raw = sb("weights_raw", [P, RAW, SLOT])
        w_hi = sb("weights_hi", [P, SPLIT, SLOT], F32R)
        w_lo = sb("weights_lo", [P, SPLIT, SLOT], F32R)
        h = sb("h", [P, KD, T1])
        x_hi = sb("x_hi", [P, KD * T1 + 112], F32R)
        x_lo = sb("x_lo", [P, KD * T1 + 112], F32R)
        hid_hi = over("hidden_hi", 0, [P, KF, T1])
        hid_lo = over("hidden_lo", 22 * T1, [P, KF, T1])
        mix_hi = over("mix_hi", 0, [P, KD, T1])
        mix_lo = over("mix_lo", 8 * T1, [P, KD, T1])
        ple_hi = over("ple_hi", 46 * T1, [P, 2, T1])
        ple_lo = over("ple_lo", 48 * T1, [P, 2, T1])
        sq = sb("sq", [P, SQ_SLOTS, T1])
        cst = sb("cst", [P, CONST_N])
        vec = sb("vec", [P, VEC_N])
        late = sb("late", [P, 1024])
        smpr = sb("smpr", [P, 8, T1])
        pn = sb("pn", [P, 2, T1])
        pT = sb("pT", [P, 2, 3 * P])
        std = sb("std", [P, 2, T1])
        rstd = sb("rstd", [P, 2, T1])
        small = sb("small", [P, 128])
        cs_r = sq[:, 6:8, :]
        pos_sb = sb("pos_sb", [P, T2], I32)
        sm, pr = smpr[:, 0:4, :], smpr[:, 4:8, :]
        t1, t2 = pr[:, 0:2, :], pr[:, 2:4, :]

        def part(off, n, width=None):
            v = arena[:, off:off + n]
            return v.rearrange("p (c t) -> p c t", t=width) if width else v

        wide = part(0, 22 * T1, T1)
        qT = part(22 * T1, 12 * T1, T1)
        kT = part(34 * T1, 12 * T1, T1)
        v_tok = part(46 * T1, 3072, 1024)
        oT = part(46 * T1 + 3072, 8 * T1, T1)

        def con(name, rows=P):
            a, n = CONST_AT[name]
            return cst[0:rows, a:a + n]

        ident, ones, rot = con("ident"), con("ones"), con("rot")
        cos1, sin1 = con("cos"), con("sin")
        causal = con("causal")
        cs2 = cst[:, CONST_AT["cos"][0]:CONST_AT["cos"][0] + 2 * T2].rearrange("p (i t) -> p i t", i=2)

        def tile_of(mask, t):
            return mask[:, MASK_AT[t]:MASK_AT[t] + TILES1[t][0] + TILES1[t][1]]

        def col(name, i=0, p0=0, pn_=P):
            a, _ = VEC_AT[name]
            return vec[p0:p0 + pn_, a + i:a + i + 1]

        idx_const = part(46 * T1 + 3072, 2 * MASK_N)
        keep, addm = idx_const[:, 0:MASK_N], idx_const[:, MASK_N:2 * MASK_N]
        amask = late[:, 0:MASK_N]
        lmask = smpr.rearrange("p a b -> p (a b)")[:, 0:7 * P].rearrange("p (l t) -> p l t", l=7)
        wsT = smpr.rearrange("p a b -> p (a b)")[:, 4 * T1:4 * T1 + 8 * P].rearrange("p (h t) -> p h t", h=8)
        bs = late[:, 0:512].rearrange("p (c t) -> p c t", c=4)
        vn = late[:, 512:1024]

        nmx, ssum, rs = small[:, 8:16], small[:, 16:24], small[:, 24:32]
        eps_col = small[:, 0:1]
        wi_tok = small[:, 32:56].rearrange("p (t h) -> p t h", t=3)
        lam, lam_e, subln8, lam_p = small[:, 56:57], small[:, 57:59], small[:, 59:60], small[:, 60:62]
        max8 = small[:, 62:70]
        lb_t, lb, oml = small[:, 70:74], small[:, 74:78], small[:, 78:82]
        vms = small[:, 84:100]
        e_last = small[:, 100:116]
        sq_dummy = small[:, 116:117]
        rq, nrq = part(46 * T1 + 2048, 16), part(46 * T1 + 2064, 16)
        last_flat = sq.rearrange("p a b -> p (a b)")[:, T1:6 * T1]
        last_q = last_flat[:, 0:8 * P].rearrange("p (c q) -> p c q", q=P)
        ident8 = last_flat[0:16, 1200:1200 + P]
        angle_cos, angle_sin = late[:, MASK_N:MASK_N + T2], pos_sb.bitcast(F32)[:, 0:T2]
        halves = small[:, 123:125]
        rcol, rcol8 = small[:, 117:120], small[:, 120:123]

        s_const = sem("constants_loaded")
        s_vec = sem("vectors_loaded")
        s_hload = [sem(f"tokens_loaded{i}") for i in range(4)]
        s_idxc = sem("index_constants_loaded")
        s_pos = sem("positions_loaded")
        s_even = sem("even_constants_loaded")
        s_slot = [sem(f"slot{i}_loaded") for i in range(RAW)]
        s_whi = sem("weights_hi_ready")
        s_wlo = sem("weights_lo_ready")
        s_xhi = sem("activation_hi_ready")
        s_xlo = sem("activation_lo_ready")
        s_pad = sem("padding_written")
        s_ple = sem("layer_embedding_loaded")
        s_chunk = sem("chunk_ready")
        s_half = sem("half_chunk_ready")
        s_free = {"act": sem("chunk_emptied_by_act"), "dve": sem("chunk_emptied_by_dve")}
        s_sq = sem("squares_ready")
        s_col = sem("square_sum_ready")
        s_add = sem("squares_added")
        s_std = sem("standard_deviation_ready")
        s_eps = sem("epsilon_written")
        s_inv = sem("inverse_deviation_ready")
        s_app = sem("norm_applied")
        s_tab = sem("scaled_tables_ready")
        s_rcol = sem("inverse_deviation_columns_ready")
        s_silur = sem("silu_scaled")
        s_sig = sem("layer_gate_ready")
        s_evact = sem("mixer_activation_ready")
        s_rot = sem("rotated_ready")
        s_t1 = sem("cos_part_ready")
        s_rope = sem("rope_ready")
        s_clear = sem("last_queries_cleared")
        s_last = sem("last_queries_placed")
        s_amask = sem("last_mask_ready")
        s_amrep = sem("last_mask_repeated")
        s_amcopy = sem("last_mask_copied")
        s_olast = sem("last_queries_out_ready")
        s_score = sem("scores_ready")
        s_max = sem("row_max_ready")
        s_exp = sem("exp_ready")
        s_prob = sem("probs_ready")
        s_tr = sem("probs_transposed")
        s_ptc = sem("probsT_copied")
        s_pv = sem("pv_done")
        s_oev = sem("attention_out_ready")
        s_idx = sem("index_raw_ready")
        s_relu = sem("index_relu_ready")
        s_idxa = sem("index_sum_ready")
        s_top = sem("topk_mask_ready")
        s_hid = sem("hidden_ready")
        s_conv = sem("conv_first_tap_ready")
        s_free["hid"] = s_hid
        s_silu = sem("silu_ready")
        s_lam = sem("lambda_products_ready")
        s_lams = sem("lambda_sums_ready")
        s_lame = sem("lambda_exp_ready")
        s_final = sem("second_block_input_ready")
        s_ang = sem("angles_ready")
        s_sincos = sem("sincos_ready")
        s_lbd = sem("lb_difference_ready")
        s_lbe = sem("lb_exp_ready")
        s_f = sem("forget_floor_ready")
        s_ln = sem("log_forget_ready")
        s_oper = sem("operands_cleared")
        s_lvd = sem("level_exponent_ready")
        s_lve = sem("level_decay_ready")
        s_lvq = sem("level_operands_ready")
        s_lvm = sem("level_scores_ready")
        s_lva = sem("level_scores_added")
        s_ws = sem("spatial_weights_masked")
        s_gsq = sem("value_squares_ready")
        s_gnorm = sem("value_scaled")
        s_vms = sem("value_mean_square_ready")
        s_vrs = sem("value_rstd_ready")
        s_gv = sem("value_normed")
        s_mixp = sem("spatial_product_ready")
        s_mix = sem("mixed_ready")
        s_kkt = sem("key_transposed")
        s_kkc = sem("key_copied")
        s_upd = sem("state_update_ready")
        s_st = sem("state_ready")
        s_hgo = sem("hgrn_product_ready")
        s_hge = sem("hgrn_out_ready")
        s_gate = sem("hgrn_gated")
        s_qsq = sem("query_squares_ready")
        s_qsum = sem("query_square_sums_ready")
        s_qstd = sem("query_deviation_ready")
        s_kr = sem("shared_rope_key_gained")
        s_out = sem("output_stored")
        s_dve = sem("dve_step")
        s_act = sem("act_step")

        def emptied(eng, c):
            eng.wait_ge(s_free[chunks[c]["owner"]], chunks[c]["nth"] + 1)

        def chunk_of(stage, i):
            return stages[stage]["first"] + i

        def dense_bank(c):
            return bank[:, DENSE_BANKS[c % len(DENSE_BANKS)], :]

        def conv_buf(n):
            return sm[:, n % 4, :]

        def silu_buf(n):
            return pn[:, n % 2, :]

        def hid_buf(n):
            return pT[:, n % 2, 0:T1]

        block = ctx.enter_context(nc.Block())

        @block.sync
        def _(sp):
            for n, p in enumerate(panels):
                if n >= RAW:
                    sp.wait_ge(s_wlo, n - RAW + 1)
                view = raw[:, n % RAW, 0:p["k"] * p["n"]].rearrange("p (k n) -> p k n", n=p["n"])
                for a, b, src in p["loads"]:
                    sp.dma_start(view[:, :, a:b], src).then_inc(s_slot[n % RAW], 16)
            sp.wait_ge(s_free["dve"], plan.owned["dve"])
            sp.wait_ge(s_final, 8 + 16)
            sp.dma_start(out.rearrange("(c p) t -> p c t", p=P), h[:, :, 0:T2]).then_inc(s_out, 16)
            sp.wait_ge(s_out, 16)

        loaded = []
        seen = [0] * RAW
        for n, p in enumerate(panels):
            seen[n % RAW] += 16 * len(p["loads"])
            loaded.append(seen[n % RAW])

        def panel_freed(eng, n):
            kind, v = panels[n]["free"]
            eng.wait_ge(s_chunk if kind == "chunk" else s_half, v)

        def round_panel(act, n):
            size = panels[n]["k"] * panels[n]["n"]
            act.wait_ge(s_slot[n % RAW], loaded[n])
            if n >= SPLIT:
                panel_freed(act, n - SPLIT)
            nc.scalar.activation(w_hi[:, n % SPLIT, 0:size], raw[:, n % RAW, 0:size], ACT.Copy).then_inc(s_whi, 1)

        def rest_panel(dve, n):
            size = panels[n]["k"] * panels[n]["n"]
            dve.wait_ge(s_whi, n + 1)
            nc.vector.tensor_tensor(w_lo[:, n % SPLIT, 0:size], raw[:, n % RAW, 0:size],
                                    w_hi[:, n % SPLIT, 0:size].bitcast(F32), ALU.subtract).then_inc(s_wlo, 1)

        def weights_ahead(eng, split_one, c):
            for n in plan.begin[c]:
                if n + AHEAD < len(panels):
                    split_one(eng, n + AHEAD)

        @block.tensor
        def _(pe):
            def dense(stage, src, T, split, after=None):
                waited, now = set(), -1
                for s in stages[stage]["steps"]:
                    p = panels[s["panel"]]
                    if s["panel"] != now:
                        now = s["panel"]
                        pe.wait_ge(s_wlo, now + 1)
                        wh, wl = [r[:, now % SPLIT, 0:p["k"] * p["n"]].rearrange("p (k n) -> p k n", n=p["n"])
                                  for r in (w_hi, w_lo)]
                    if s["start"] and s["chunk"] >= len(DENSE_BANKS):
                        emptied(pe, s["chunk"] - len(DENSE_BANKS))
                    b = dense_bank(s["chunk"])
                    for k in range(s["k"]):
                        kk = s["k0"] + k
                        if kk not in waited:
                            pe.wait_ge(s_xlo, split + kk + 1)
                            waited.add(kk)
                        ch, cl = s["cols"](wh, k), s["cols"](wl, k)
                        if s["kind"] == "fm":
                            xh, xl = [x[:, kk * T1:kk * T1 + T] for x in src]
                            passes, o = ((ch, xh), (ch, xl), (cl, xh)), b[:, 0:T]
                        else:
                            q0 = kk * T1 + s["tile"][0]
                            xh, xl = [x[:, q0:q0 + P] for x in src]
                            passes, o = ((xh, ch), (xh, cl), (xl, ch)), b[:, 0:s["size"]]
                        for i, (lhs, rhs) in enumerate(passes):
                            mm = nc.tensor.matmul(o, lhs, rhs, start=s["start"] and k == 0 and i == 0,
                                                  stop=s["stop"] and k == s["k"] - 1 and i == 2)
                    mm.then_inc(s_chunk if s["stop"] else s_half, 1)
                    if after and s["stop"]:
                        after(s["chunk"] - stages[stage]["first"])

            def norm_sum(name, T, parts=((0, P),) * 8):
                m = norms[name]
                if m["id"]:
                    pe.wait_ge(s_std, m["id"])
                for i in range(m["adds"], m["n"]):
                    a, n = parts[i]
                    if i and i == m["adds"]:
                        pe.wait_ge(s_add, m["add"] + m["adds"])
                    else:
                        pe.wait_ge(s_sq, m["sq"] + i + 1)
                    mm = nc.tensor.matmul(bank[:, B_COL, 0:T], ones[a:a + n, :],
                                          sq[a:a + n, (m["sq"] + i) % SQ_SLOTS, 0:T],
                                          start=(i == m["adds"]), stop=(i == m["n"] - 1))
                mm.then_inc(s_col, 1)

            def rotate(r, raw, T, ready, rows=P):
                pe.wait_ge(*ready)
                if r < 2:
                    pe.wait_ge(s_lame, 1)
                if r >= 2:
                    pe.wait_ge(s_rope, r - 1)
                nc.tensor.matmul(bank[0:rows, B_S + r % 2, 0:T], rot[0:rows, 0:rows], raw,
                                 start=True, stop=True).then_inc(s_rot, 1)

            def attention(name, score_ops, stage):
                A = att[name]
                U = A["units"]
                emptied(pe, chunk_of(stage, stages[stage]["n"] - 1))
                for i in range(len(U) + 4):
                    if i < len(U):
                        x = U[i]
                        if x["group"] == 0:
                            pe.wait_ge(s_last, 1 if name == "da" else 2)
                        for c, s in enumerate(x["scores"]):
                            if s >= 4:
                                pe.wait_ge(s_max, s - 3)
                            ops = score_ops(x, c)
                            for j, (a, b) in enumerate(ops):
                                mm = nc.tensor.matmul(bank[0:x["qn"], S_BANKS[s % 4], 0:x["kn"]], a, b,
                                                      start=(j == 0), stop=(j == len(ops) - 1))
                            mm.then_inc(s_score, 1)
                    if 3 <= i < len(U) + 3:
                        x = U[i - 3]
                        pe.wait_ge(s_prob, x["u"] + 1)
                        if x["u"]:
                            pe.wait_ge(s_ptc, x["u"])
                        for kt, (a, n) in enumerate(x["ktiles"]):
                            mm = nc.tensor.transpose(bank[0:n, B_PT, kt * P:kt * P + x["qn"]],
                                                     pn[0:x["qn"], x["u"] % 2, a:a + n],
                                                     ident[0:x["qn"], 0:x["qn"]])
                        mm.then_inc(s_tr, 1)
                    if i >= 4:
                        x = U[i - 4]
                        pe.wait_ge(s_ptc, x["u"] + 1)
                        if x["group"] is not None:
                            per = P // x["dv"]
                            for hh in range(8 * x["group"], 8 * x["group"] + 8):
                                a, o, j = x["dv"] * (hh % per), hh // per * 16, hh % 8 * 16
                                for kt, (_, n) in enumerate(x["ktiles"]):
                                    mm = nc.tensor.matmul(bank[a:a + x["dv"], B_LAST, o:o + 16],
                                                          v_tok[0:n, kt, hh * x["dv"]:(hh + 1) * x["dv"]],
                                                          pT[0:n, x["u"] % 2, kt * P + j:kt * P + j + 16],
                                                          start=(kt == 0), stop=(kt == 2))
                            mm.then_inc(s_pv, 1)
                            continue
                        if x["first"] and x["oc"] >= 2:
                            pe.wait_ge(s_oev, x["oc"] - 1)
                        ob = bank[x["part"]:x["part"] + x["dv"], O_BANKS[x["oc"] % 2], x["q0"]:x["q0"] + x["qn"]]
                        for kt, (a, n) in enumerate(x["ktiles"]):
                            mm = nc.tensor.matmul(ob, v_tok[0:n, kt, x["h"] * x["dv"]:(x["h"] + 1) * x["dv"]],
                                                  pT[0:n, x["u"] % 2, kt * P:kt * P + x["qn"]],
                                                  start=(kt == 0), stop=(kt == len(x["ktiles"]) - 1))
                        mm.then_inc(s_pv, 1)

            def act_chunk(c):
                return (s_free["act"], chunks[c]["nth"] + 1)

            flat = lambda x: x.rearrange("p k t -> p (k t)")
            X = (x_hi, x_lo)
            HID = (flat(hid_hi[:, :, :]), flat(hid_lo[:, :, :]))
            MIX = (flat(mix_hi[:, :, :]), flat(mix_lo[:, :, :]))
            PLE = (flat(ple_hi[:, :, :]), flat(ple_lo[:, :, :]))


            def da_after(j):
                if j == 1:
                    pe.wait_ge(s_const, 16)
                    norm_sum("da", T1)
                    pe.wait_ge(s_lam, 1)
                    nc.tensor.matmul(bank[:, B_S, 0:2], ones[0:64, :], lam_p[0:64, :], start=True, stop=True)\
                        .then_inc(s_lams, 1)
                if 2 <= j < 18:
                    rotate(j - 2, wide[:, j - 2, :], T1, act_chunk(chunk_of("da_qkv", j - 2)))
            pe.wait_ge(s_pad, 2)
            dense("da_qkv", X, T1, splits["da"], da_after)
            pe.wait_ge(s_rope, 16)

            def da_ops(x, c):
                if x["group"] is not None:
                    return [(last_q[64 * c:64 * c + 64, j, :], kT[64 * c:64 * c + 64, j, 0:T1]) for j in range(8)]
                return [(qT[64 * c:64 * c + 64, x["h"], x["q0"]:x["q0"] + x["qn"]],
                         kT[64 * c:64 * c + 64, x["h"], 0:x["kn"]])]
            attention("da", da_ops, "da_qkv")
            for hh in range(8):
                norm_sum(f"o{hh}", T1)
            dense("da_out", MIX, T1, splits["da_mix"])
            norm_sum("conv0", T1)
            dense("conv0_up", X, T1, splits["conv0"])
            dense("conv0_down", HID, T1, splits["hid0"])

            rb = ROPE_BASE["idx"]

            def index_scores(x):
                t, hh = divmod(x, 8)
                q0, qn = TILES1[t]
                a = 64 * (hh % 2)
                if x >= 2:
                    pe.wait_ge(s_relu, x - 1)
                nc.tensor.matmul(bank[0:qn, B_S + x % 2, 0:q0 + qn], qT[a:a + 64, 8 + hh // 2, q0:q0 + qn],
                                 kT[a:a + 64, 8, 0:q0 + qn], start=True, stop=True).then_inc(s_idx, 1)

            def dsa_after(j):
                if j == 0:
                    norm_sum("dsa", T1)
                if 2 <= j < 6:
                    rotate(rb + j - 2, wide[:, j - 2, :], T1, act_chunk(chunk_of("dsa_in", j - 2)))
                if j == 5:
                    norm_sum("ki", T1, ((0, 64),))
                if j == 7:
                    rotate(rb + 4, wide[0:64, 5, :], T1, (s_app, norms["ki"]["ap"] + 1), rows=64)
                if 8 <= j < 20:
                    if j == 8:
                        pe.wait_ge(s_rope, rb + 5)
                        pe.wait_ge(s_top, 1)
                    index_scores(2 * (j - 8))
                    index_scores(2 * (j - 8) + 1)
                if j == 20:
                    pe.wait_ge(s_relu, 24)
                if j >= 22:
                    i = j - 22
                    rotate(ROPE_BASE["dsa"] + i, wide[:, 6 + i, :], T1, act_chunk(chunk_of("dsa_in", 20 + i)))
            dense("dsa_in", X, T1, splits["dsa"], dsa_after)
            for i in (14, 15):
                rotate(ROPE_BASE["dsa"] + i, wide[:, 6 + i, :], T1, act_chunk(chunk_of("dsa_in", 20 + i)))
            pe.wait_ge(s_rope, ROPE_BASE["dsa"] + 16)

            pe.wait_ge(s_amask, 1)
            pe.wait_ge(s_clear, 3)
            nc.tensor.matmul(bank[:, B_COL, 0:T1],
                             ident8,
                             tile_of(amask, 2)[0:16, :], start=True, stop=True).then_inc(s_amrep, 1)

            def dsa_ops(x, c):
                if x["group"] is not None:
                    return [(last_q[:, j, :], kT[:, j, 0:T1]) for j in range(4 * x["group"], 4 * x["group"] + 4)]
                a = 64 * (x["h"] % 2)
                return [(qT[a:a + 64, x["h"] // 2, x["q0"]:x["q0"] + x["qn"]], kT[a:a + 64, x["h"] // 2, 0:x["kn"]])]
            attention("dsa", dsa_ops, "dsa_in")
            dense("dsa_out", MIX, T1, splits["dsa_mix"])
            norm_sum("conv1", T1)
            dense("conv1_up", X, T1, splits["conv1"])
            dense("conv1_down", HID, T1, splits["hid1"])
            norm_sum("final", T1)

            def sum_first(name):
                return lambda j: norm_sum(name, T2) if j == 0 else None

            def glu(i, j):
                dense(f"glu{i}{j}_up", X, T2, splits[f"glu{i}{j}"], sum_first(f"glu{i}{j}"))
                dense(f"glu{i}{j}_down", HID, T2, splits[f"hid{2 + 2 * i + j}"])

            def ple(i):
                dense(f"ple{i}_gate", X, T2, splits[f"pleh{i}"], sum_first(f"pleh{i}"))
                dense(f"ple{i}_proj", PLE, T2, splits[f"ple{i}"])
                norm_sum(f"pleo{i}", T2)

            glu(0, 0)
            dense("ev_in", X, T2, splits["ev"], sum_first("ev"))
            slot = lambda i: part(i * 1024, 1024)
            hg_v = part(11 * 1024, 1024, 512)
            scT = part(10 * 1024, 1024, 512)
            emptied(pe, chunk_of("ev_in", 7))
            emptied(pe, chunk_of("ev_in", 11))
            for lv in range(7):
                pe.wait_ge(s_lvq, lv + 1)
                if lv == 1:
                    emptied(pe, chunk_of("ev_in", 23))
                if lv == 0:
                    qe_, ke_ = slot(0), slot(1)
                else:
                    qe_, ke_ = slot(6 + lv % 2), slot(8 + lv % 2)
                for t in range(2):
                    if lv >= 2:
                        pe.wait_ge(s_lva, 2 * (lv - 2) + t + 1)
                    for hh in range(4):
                        o = hh * T2 + t * P
                        mm = nc.tensor.matmul(bank[:, LEVEL_BANKS[lv % 2][t], hh * P:(hh + 1) * P], ke_[:, o:o + P],
                                              qe_[:, o:o + P], start=True, stop=True)
                    mm.then_inc(s_lvm, 1)
            pe.wait_ge(s_gv, 1)
            pe.wait_ge(s_ws, 1)
            gvn = part(14 * 1024, 1024, 512)
            for t in range(2):
                for hh in range(8):
                    a = 64 * (hh % 2)
                    mm = nc.tensor.matmul(bank[a:a + 64, B_COL + t, (hh // 2) * P:(hh // 2 + 1) * P],
                                          gvn[:, t, hh * 64:hh * 64 + 64], wsT[:, hh, :], start=True, stop=True)
                mm.then_inc(s_mixp, 1)
            pe.wait_ge(s_gate, 1)
            kk = slot(7)
            for t in range(2):
                if t == 1:
                    pe.wait_ge(s_kkc, 1)
                for hh in range(4):
                    mm = nc.tensor.transpose(bank[:, B_PT, hh * P:(hh + 1) * P],
                                             kk[:, hh * T2 + t * P:hh * T2 + t * P + P], ident)
                mm.then_inc(s_kkt, 1)
            kk_tok = part(14 * 1024, 1024, 512)
            pe.wait_ge(s_kkc, 2)
            pe.wait_ge(s_lva, 14)
            for n in range(3):
                a, t = 64 * (n % 2), n // 2
                if n >= 2:
                    pe.wait_ge(s_st, n - 1)
                for hh in range(4):
                    mm = nc.tensor.matmul(bank[:, B_S + n % 2, hh * P:(hh + 1) * P],
                                          kk_tok[a:a + 64, t, hh * P:(hh + 1) * P],
                                          hg_v[a:a + 64, t, hh * P:(hh + 1) * P], start=True, stop=True)
                mm.then_inc(s_upd, 1)
            states = part(8 * 1024, 1536, 512)
            qe = slot(6)
            pe.wait_ge(s_mix, 2)
            pe.wait_ge(s_st, 3)
            for hh in range(4):
                b = B_COL + hh // 2
                for t in range(2):
                    o = (hh % 2) * T2 + t * P
                    nc.tensor.matmul(bank[:, b, o:o + P], hg_v[:, t, hh * P:(hh + 1) * P],
                                     scT[:, t, hh * P:(hh + 1) * P], start=True, stop=False)
                    for n in range(max(1, 2 * t), 2 * t + 2):
                        oo = (hh % 2) * T2 + n * CHUNK
                        mm = nc.tensor.matmul(bank[:, b, oo:oo + CHUNK], states[:, n - 1, hh * P:(hh + 1) * P],
                                              qe[:, hh * T2 + n * CHUNK:hh * T2 + (n + 1) * CHUNK],
                                              start=False, stop=(n == 2 * t + 1))
                mm.then_inc(s_hgo, 1)
            pe.wait_ge(s_hge, 4)
            for hh in range(4):
                norm_sum(f"hg{hh}", T2)
            dense("ev_out", MIX, T2, splits["ev_mix"])
            glu(0, 1)
            ple(0)
            glu(1, 0)
            dense("mla_in", X, T2, splits["mla"], sum_first("mla"))
            norm_sum("cq", T2)
            norm_sum("ckv", T2)

            def query_sums(g):
                pe.wait_ge(s_qsq, 3 * g + 3)
                for t, (q0, n) in enumerate(TILES2):
                    j = t * 8 + 2 * g
                    nc.tensor.matmul(bank[:, B_S, j:j + 2], wide[:, 18 + g, q0:q0 + n], halves, start=True, stop=False)
                    for x in range(2):
                        mm = nc.tensor.matmul(bank[:, B_S, j + x:j + x + 1], wide[:, 6 + 2 * g + x, q0:q0 + n],
                                              ones[:, 0:1], start=False, stop=(x == 1))
                mm.then_inc(s_qsum, 1)
            dense("mla_q", X, T2, splits["cq"], lambda j: query_sums(j // 3 - 1) if j % 3 == 1 and j > 3 else None)
            dense("mla_kv", (x_hi[:, 3 * T1:], x_lo[:, 3 * T1:]), T2, splits["ckv"],
                  lambda j: query_sums(3) if j == 1 else None)
            rotate(ROPE_BASE["kr"], oT[:, 6, 0:T2], T2, (s_kr, 1))
            pe.wait_ge(s_qstd, 1)
            for r in range(4):
                rotate(ROPE_BASE["mq"] + r, wide[:, 6 + 8 + r, 0:T2], T2, act_chunk(chunk_of("mla_q", 3 * r + 2)))
            for hh in range(8):
                a = 64 * (hh % 2)
                norm_sum(f"k{hh}", T2, ((0, P), (a, 64)))
            pe.wait_ge(s_rope, ROPE_BASE["mq"] + 4)
            pe.wait_ge(s_app, norms["k7"]["ap"] + 2)

            def mla_ops(x, c):
                a = 64 * (x["h"] % 2)
                hh = x["h"]
                q = slice(x["q0"], x["q0"] + x["qn"])
                return [(qT[:, hh, q], kT[:, hh, 0:x["kn"]]),
                        (qT[a:a + 64, 8 + hh // 2, q], kT[a:a + 64, 8 + hh // 2, 0:x["kn"]])]
            attention("mla", mla_ops, "mla_kv")
            dense("mla_out", MIX, T2, splits["mla_mix"])
            glu(1, 1)
            ple(1)

        @block.scalar
        def _(act):
            def step(ins):
                step.n += 1
                ins.then_inc(s_act, 1)
                act.wait_ge(s_act, step.n)
            step.n = 0

            def square(name, srcs, ready, parts=((0, P),) * 8, T=T1, before=None):
                m = norms[name]
                need = m["id"] if m["alone"] else m["id"] - 1
                if need > 0:
                    act.wait_ge(s_col, need)
                for i, s in enumerate(srcs):
                    a, n = parts[i]
                    if before:
                        before(i)
                    act.wait_ge(*ready[i])
                    nc.scalar.activation(sq[a:a + n, (m["sq"] + i) % SQ_SLOTS, 0:T], s, ACT.Square).then_inc(s_sq, 1)

            def root(name, T, dim):
                m = norms[name]
                act.wait_ge(s_col, m["id"] + 1)
                if m["id"] >= 2:
                    act.wait_ge(s_inv, m["id"] - 1)
                    if norms["by_id"][m["id"] - 1]["ap"]:
                        act.wait_ge(s_app, norms["by_id"][m["id"] - 1]["ap"])
                nc.scalar.activation(std[:, m["id"] % 2, 0:T], bank[:, B_COL, 0:T], ACT.Sqrt, bias=eps_col,
                                     scale=1.0 / dim).then_inc(s_std, 1)

            def sqrt_table():
                nc.scalar.activation(sq_dummy, eps_col, ACT.Sqrt)

            def residual(stage):
                c0 = stages[stage]["first"]
                return [(s_free["dve"], chunks[c0 + i]["nth"] + 1) for i in range(8)]

            def high(at, dst, src, ready):
                for i in range(len(dst)):
                    act.wait_ge(*ready[i])
                    nc.scalar.activation(dst[i], src[i], ACT.Copy).then_inc(s_xhi, 1)

            def high_normed(name, n=KD, first=0, T=T2):
                m = norms[name]
                high(splits[name], [x_hi[:, (first + c) * T1:(first + c) * T1 + T] for c in range(n)],
                     [sq[:, (m["sq"] + c) % SQ_SLOTS, 0:T] for c in range(n)],
                     [(s_app, m["ap"] + c + 1) for c in range(n)])

            def high_mix(name, T, ready):
                high(splits[name], [mix_hi[:, c, 0:T] for c in range(KD)], [oT[:, c, 0:T] for c in range(KD)], ready)

            def norm_after(stage, name, T):
                norm_h(name, residual(stage), T, each=lambda i: ahead(chunk_of(stage, i)))

            def gained(name, c, ready, T, src=h):
                act.wait_ge(*ready)
                v, at = DEFERRED[name]
                nc.scalar.activation(x_hi[:, c * T1:c * T1 + T], src[:, c, 0:T], ACT.Copy,
                                     scale=col(v, at + c)).then_inc(s_xhi, 1)

            def norm_h(name, ready, T, each=None, src=h):
                sqrt_table()

                def before(c):
                    if each:
                        each(c)
                    if name in DEFERRED:
                        gained(name, c, ready[c], T, src)
                square(name, [src[:, c, 0:T] for c in range(KD)], ready, T=T, before=before)
                root(name, T, D)
                if name in splits and name not in DEFERRED:
                    high_normed(name, T=T)

            def ahead(c):
                weights_ahead(act, round_panel, c)

            def ahead_stage(stage):
                for i in range(stages[stage]["n"]):
                    ahead(chunk_of(stage, i))

            def evict(c, dst, func=ACT.Copy, scale=1.0, first=True):
                if first:
                    ahead(c)
                act.wait_ge(s_chunk, c + 1)
                b = dense_bank(c)
                src = b[0:dst.shape[0], 0:int(np.prod(dst.shape[1:]))]
                nc.scalar.activation(dst, src, func, scale=scale).then_inc(s_free["act"], 1)

            def attention(name):
                U = att[name]["units"]
                for i in range(len(U) + 4):
                    if i < len(U):
                        x = U[i]
                        for s in x["scores"]:
                            act.wait_ge(s_max, s + 1)
                            if s >= 4:
                                act.wait_ge(s_prob, unit_of_score[s - 4] + 1)
                            q, k = x["qn"], x["kn"]
                            j = x["t"] * 8 + x["h"]
                            nc.scalar.activation(pr[0:q, s % 4, 0:k], sm[0:q, s % 4, 0:k], ACT.Exp,
                                                 bias=nmx[0:q, s % 8:s % 8 + 1],
                                                 scale=nrq[0:q, j:j + 1] if name == "mla" else -1.0,
                                                 accum_out=ssum[0:q, s % 8:s % 8 + 1]).then_inc(s_exp, 1)
                    if 2 <= i < len(U) + 2:
                        x = U[i - 2]
                        u, q = x["u"], x["qn"]
                        act.wait_ge(s_tr, u + 1)
                        if u >= 2:
                            act.wait_ge(s_pv, u - 1)
                        full = [kt for kt in x["ktiles"] if kt[1] == P]
                        v = lambda z: z.rearrange("p (k q) -> p k q", q=P)
                        ins = nc.scalar.activation(v(pT[:, u % 2, :])[:, 0:len(full), 0:q],
                                                   v(bank[:, B_PT, 0:3 * P])[:, 0:len(full), 0:q], ACT.Copy)
                        if len(full) < len(x["ktiles"]):
                            kt, n = len(full), x["ktiles"][-1][1]
                            ins = nc.scalar.activation(pT[0:n, u % 2, kt * P:kt * P + q],
                                                       bank[0:n, B_PT, kt * P:kt * P + q], ACT.Copy)
                        ins.then_inc(s_ptc, 1)
                    if i >= 4 and U[i - 4]["last"]:
                        x = U[i - 4]
                        act.wait_ge(s_pv, x["u"] + 1)
                        nc.scalar.activation(oT[:, x["chunk"], 0:256], bank[:, O_BANKS[x["oc"] % 2], 0:256], ACT.Copy)\
                            .then_inc(s_oev, 1)
                if U[-1]["group"] is not None:
                    act.wait_ge(s_pv, U[-1]["u"] + 1)
                    nc.scalar.activation(oT[:, :, 256:T1], bank[:, B_LAST, 0:P].rearrange("p (c q) -> p c q", q=16),
                                         ACT.Copy).then_inc(s_olast, 1)

            act.dma_start(vec[:, :], vecs).then_inc(s_vec, 16)
            for c in range(0, KD, 2):
                act.dma_start(h[:, c:c + 2, :], hT.rearrange("(c p) t -> p c t", p=P)[:, c:c + 2, :])\
                    .then_inc(s_hload[c // 2], 16)
            act.dma_start(cst[:, :], consts).then_inc(s_const, 16)
            act.dma_start(pos_sb[:, :], pos).then_inc(s_pos, 16)
            act.wait_ge(s_eps, 1)
            sqrt_table()
            round_panel(act, 0)
            act.wait_ge(s_vec, 16)
            for c in range(KD):
                gained("da", c, (s_hload[c // 2], 16), T1)
            round_panel(act, 1)
            square("da", [h[:, c, :] for c in range(KD)], [(s_hload[c // 2], 16) for c in range(KD)], T=T1)
            root("da", T1, D)
            act.wait_ge(s_lbd, 1)
            nc.scalar.activation(lb, lb_t, ACT.Exp).then_inc(s_lbe, 1)
            act.wait_ge(s_lams, 1)
            nc.scalar.activation(lam_e, bank[:, B_S, 0:2], ACT.Exp).then_inc(s_lame, 1)
            for j in range(16):
                evict(chunk_of("da_qkv", j), wide[:, j, :])
            for j in range(12):
                g, t = divmod(j, 3)
                n = TILES1[t][1]
                c = chunk_of("da_qkv", 16 + j)
                act.wait_ge(s_rcol, 1)
                evict(c, v_tok[0:n, t, g * 256:(g + 1) * 256], scale=rcol[0:n, t:t + 1])
            attention("da")
            act.wait_ge(s_olast, 1)
            oc0 = att["da"]["units"][0]["oc"]
            for hh in range(9):
                if hh < 8:
                    square(f"o{hh}", [oT[:, hh, :]], [(s_oev, oc0 + hh + 1)])
                if hh >= 1:
                    root(f"o{hh - 1}", T1, P)
            high_mix("da_mix", T1, [(s_app, norms["o0"]["ap"] + i + 1) for i in range(8)])
            norm_after("da_out", "conv0", T1)
            act.wait_ge(s_xlo, splits["da_mix"] + 8)
            act.dma_start(idx_const, idxc).then_inc(s_idxc, 16)

            def conv_up(i):
                for j in range(KF + 2):
                    if j < KF:
                        for g in range(2):
                            c = chunk_of(f"conv{i}_up", 2 * j + g)
                            n = i * 2 * KF + 2 * j + g
                            ch = j + g * KF
                            ahead(c)
                            act.wait_ge(s_chunk, c + 1)
                            if n >= 4:
                                act.wait_ge(s_hid, (n - 4) // 2 + 1)
                            nc.scalar.activation(conv_buf(n), dense_bank(c)[:, 0:T1], ACT.Identity,
                                                 bias=col("conv_b", i * 44 + ch),
                                                 scale=col("conv_w", (i * 3 + 2) * 44 + ch)).then_inc(s_conv, 1)
                    if 1 <= j <= KF:
                        n = i * 2 * KF + 2 * (j - 1)
                        c = chunk_of(f"conv{i}_up", 2 * (j - 1))
                        act.wait_ge(s_free["dve"], chunks[c]["nth"] + 1)
                        nc.scalar.activation(silu_buf(n // 2), conv_buf(n), ACT.Silu).then_inc(s_silu, 1)
                    if j >= 2:
                        g = i * KF + j - 2
                        high(splits[f"hid{i}"] + j - 2, [hid_hi[:, j - 2, :]], [hid_buf(g)], [(s_hid, g + 1)])
            conv_up(0)
            norm_after("conv0_down", "dsa", T1)
            for j in range(4):
                evict(chunk_of("dsa_in", j), wide[:, j, :])
            ahead(chunk_of("dsa_in", 4))
            square("ki", [wide[0:64, 4, :]], [(s_free["dve"], chunks[chunk_of("dsa_in", 4)]["nth"] + 1)], ((0, 64),))
            root("ki", T1, 64)
            act.wait_ge(s_rcol, 2)
            for t in range(3):
                n = TILES1[t][1]
                evict(chunk_of("dsa_in", 5 + t), wi_tok[0:n, t, :], scale=rcol8[0:n, t:t + 1])
            act.wait_ge(s_rope, ROPE_BASE["idx"] + 5)
            nc.scalar.activation(kT[64:128, 8, :], kT[0:64, 8, :], ACT.Copy).then_inc(s_top, 1)

            def index_relu(x):
                t, hh = divmod(x, 8)
                q0, qn = TILES1[t]
                act.wait_ge(s_idx, x + 1)
                if x >= 2:
                    act.wait_ge(s_idxa, x - 1)
                nc.scalar.activation(pr[0:qn, x % 2, 0:q0 + qn], bank[0:qn, B_S + x % 2, 0:q0 + qn],
                                     ACT.Relu, scale=0.125).then_inc(s_relu, 1)
            for j in range(12):
                g, t = divmod(j, 3)
                n = TILES1[t][1]
                evict(chunk_of("dsa_in", 8 + j), v_tok[0:n, t, g * 256:(g + 1) * 256], scale=rcol[0:n, t:t + 1])
                index_relu(2 * j)
                index_relu(2 * j + 1)
            for j in range(16):
                evict(chunk_of("dsa_in", 20 + j), wide[:, 6 + j, :])
            act.wait_ge(s_amrep, 1)
            nc.scalar.activation(tile_of(amask, 2), bank[:, B_COL, 0:T1], ACT.Copy).then_inc(s_amcopy, 1)
            attention("dsa")
            act.wait_ge(s_olast, 2)
            high_mix("dsa_mix", T1, [(s_oev, att["dsa"]["units"][0]["oc"] + i + 1) for i in range(8)])
            act.wait_ge(s_ang, 2)
            for i, r in enumerate((angle_cos, angle_sin)):
                ins = nc.scalar.activation(cs2[:, i, :], r, ACT.Sin)
            ins.then_inc(s_sincos, 1)
            norm_after("dsa_out", "conv1", T1)
            conv_up(1)
            norm_after("conv1_down", "final", T1)
            act.wait_ge(s_xlo, splits["hid1"] + KF)
            act.wait_ge(s_sincos, 1)
            flat_smpr = smpr.rearrange("p a b -> p (a b)")
            for name, dst in (("lmask", flat_smpr[:, 0:7 * P]), ("wsT", flat_smpr[:, 4 * T1:4 * T1 + 8 * P]),
                              ("bs", late[:, 0:512]), ("vnorm", late[:, 512:1024])):
                o, n = EVEN_AT[name]
                act.dma_start(dst, evenc[:, o:o + n]).then_inc(s_even, 16)

            def glu_up(i, j):
                for n in range(KF + 1):
                    c = chunk_of(f"glu{i}{j}_up", 2 * n)
                    g = 2 * KF + (2 * i + j) * KF + n
                    if n < KF:
                        ahead(c)
                        act.wait_ge(s_free["dve"], chunks[c]["nth"] + 1)
                        nc.scalar.activation(silu_buf(g)[:, 0:T2], silu_buf(g)[:, 0:T2], ACT.Silu).then_inc(s_silu, 1)
                    if (i, j, n) == (0, 0, 1):
                        act.wait_ge(s_final, 8)
                    if n >= 1:
                        high(0, [hid_hi[:, n - 1, 0:T2]], [hid_buf(g - 1)[:, 0:T2]], [(s_hid, g)])

            def ple(i, before):
                act.dma_start(oT[:, 0:2, 0:T2], pT_in[i].rearrange("(c p) t -> p c t", p=P)).then_inc(s_ple, 16)
                norm_after(before, f"pleh{i}", T2)
                high(splits[f"ple{i}"], [ple_hi[:, c, 0:T2] for c in range(2)], [oT[:, c, 0:T2] for c in range(2)],
                     [(s_ple, 16 * (i + 1))] * 2)
                for c in range(KD):
                    cg = chunk_of(f"ple{i}_gate", c)
                    ahead(cg)
                    act.wait_ge(s_free["dve"], chunks[cg]["nth"] + 1)
                    nc.scalar.activation(wide[:, c, 0:T2], wide[:, c, 0:T2], ACT.Sigmoid).then_inc(s_sig, 1)
                sqrt_table()
                square(f"pleo{i}", [wide[:, 8 + c, 0:T2] for c in range(KD)], residual(f"ple{i}_proj"), T=T2)
                ahead_stage(f"ple{i}_proj")
                root(f"pleo{i}", T2, D)

            norm_h("glu00", [(s_app, norms["final"]["ap"] + c + 1) for c in range(8)], T2, src=wide)
            glu_up(0, 0)
            norm_after("glu00_down", "ev", T2)
            slot = lambda i: part(i * 1024, 1024)

            def activate(first, i, func):
                for c in range(4):
                    ce = chunk_of("ev_in", first + c)
                    ahead(ce)
                    act.wait_ge(s_free["dve"], chunks[ce]["nth"] + 1)
                    v = slot(i)[:, c * T2:(c + 1) * T2]
                    nc.scalar.activation(v, v, func).then_inc(s_evact, 1)
            activate(0, 1, ACT.Sigmoid)
            for c in range(4, 8):
                ahead(chunk_of("ev_in", c))
            act.wait_ge(s_rcol, 3)
            for j in range(4):
                g, t = divmod(j, 2)
                evict(chunk_of("ev_in", 8 + j), slot(11)[:, t * 512 + g * 256:t * 512 + g * 256 + 256],
                      scale=rcol[:, t:t + 1])
            act.wait_ge(s_f, 1)
            nc.scalar.activation(slot(2), slot(3), ACT.Ln).then_inc(s_ln, 1)
            for j in range(4):
                g, t = divmod(j, 2)
                evict(chunk_of("ev_in", 12 + j), slot(14)[:, t * 512 + g * 256:t * 512 + g * 256 + 256],
                      ACT.Gelu_apprx_tanh, scale=rcol[:, t:t + 1])
            activate(16, 12, ACT.Gelu_apprx_tanh)
            activate(20, 13, ACT.Silu)
            act.wait_ge(s_vms, 1)
            nc.scalar.activation(vms, vms, ACT.Sqrt).then_inc(s_vrs, 1)
            for lv in range(1, 7):
                act.wait_ge(s_lvd, lv)
                e = slot(4 + lv % 2)
                nc.scalar.activation(e, e, ACT.Exp).then_inc(s_lve, 1)
            act.wait_ge(s_lvd, 7)
            nc.scalar.activation(e_last, slot(2).rearrange("p (n c) -> p n c", c=CHUNK)[:, :, CHUNK - 1], ACT.Exp)
            nc.scalar.activation(slot(4), slot(2), ACT.Exp)
            nc.scalar.activation(slot(5), slot(5), ACT.Exp).then_inc(s_lve, 1)
            for t in range(2):
                act.wait_ge(s_kkt, t + 1)
                nc.scalar.activation(slot(14)[:, t * 512:(t + 1) * 512], bank[:, B_PT, :], ACT.Copy)\
                    .then_inc(s_kkc, 1)
            high(splits["ev_mix"], [mix_hi[:, c, 0:T2] for c in range(4)], [oT[:, c, 0:T2] for c in range(4)],
                 [(s_mix, 2)] * 4)
            for hh in range(4):
                act.wait_ge(s_hgo, 2 * (hh // 2) + 2)
                o = (hh % 2) * T2
                nc.scalar.activation(slot(3)[:, hh * T2:(hh + 1) * T2], bank[:, B_COL + hh // 2, o:o + T2], ACT.Copy)\
                    .then_inc(s_hge, 1)
            for hh in range(5):
                if hh < 4:
                    square(f"hg{hh}", [slot(3)[:, hh * T2:(hh + 1) * T2]], [(s_hge, hh + 1)], T=T2)
                if hh >= 1:
                    root(f"hg{hh - 1}", T2, P)
            high(splits["ev_mix"] + 4, [mix_hi[:, c, 0:T2] for c in range(4, 8)],
                 [oT[:, c, 0:T2] for c in range(4, 8)], [(s_gate, 5)] * 4)
            norm_after("ev_out", "glu01", T2)
            glu_up(0, 1)
            ple(0, "glu01_down")
            norm_h("glu10", [(s_final, 8 + c + 1) for c in range(8)], T2)
            glu_up(1, 0)
            norm_after("glu10_down", "mla", T2)
            ahead_stage("mla_in")
            f0 = chunks[chunk_of("mla_in", 0)]["nth"]
            square("cq", [wide[:, c, 0:T2] for c in range(3)], [(s_free["dve"], f0 + 1 + c) for c in range(3)], T=T2)
            square("ckv", [wide[:, 3 + c, 0:T2] for c in range(2)], [(s_free["dve"], f0 + 4 + c) for c in range(2)],
                   T=T2)
            root("cq", T2, 384)
            root("ckv", T2, 256)
            high_normed("cq", 3)
            high_normed("ckv", 2, first=3)
            for g in range(4):
                for x in range(3):
                    c = chunk_of("mla_q", 3 * g + x)
                    square_to = wide[:, 18 + g if x == 2 else 6 + 2 * g + x, 0:T2]
                    ahead(c)
                    act.wait_ge(s_chunk, c + 1)
                    nc.scalar.activation(square_to, dense_bank(c)[:, 0:T2], ACT.Square).then_inc(s_qsq, 1)
                    if x < 2:
                        evict(c, qT[:, 2 * g + x, 0:T2], scale=col("qn"), first=False)
                    else:
                        evict(c, wide[:, 14 + g, 0:T2], scale=col("qr"), first=False)
            for g in range(2):
                for hh in range(4):
                    evict(chunk_of("mla_kv", 6 * g + hh), kT[:, 4 * g + hh, 0:T2])
                for t in range(2):
                    evict(chunk_of("mla_kv", 6 * g + 4 + t), v_tok[:, t, g * 512:(g + 1) * 512])
            act.wait_ge(s_qsum, 4)
            nc.scalar.activation(rq, bank[:, B_S, 0:16], ACT.Sqrt, bias=eps_col, scale=1.0 / 192).then_inc(s_qstd, 1)
            fk = [chunks[chunk_of("mla_kv", j)]["nth"] + 1 for j in range(12)]
            heads = []
            for hh in range(8):
                a = 64 * (hh % 2)
                heads.append((f"k{hh}", [kT[:, hh, 0:T2], wide[a:a + 64, 5, 0:T2]],
                              [(s_free["act"], fk[6 * (hh // 4) + hh % 4]), (s_free["dve"], f0 + 6)], a))
            for i in range(9):
                if i < 8:
                    n_, src, rd, a = heads[i]
                    square(n_, src, rd, ((0, P), (a, 64)), T=T2)
                if i >= 1:
                    root(heads[i - 1][0], T2, 192)
            attention("mla")
            high_mix("mla_mix", T2, [(s_oev, att["mla"]["units"][0]["oc"] + i + 1) for i in range(8)])
            norm_after("mla_out", "glu11", T2)
            glu_up(1, 1)
            ple(1, "glu11_down")

        @block.gpsimd
        def _(pool):
            def cos_part(r, raw, table, T, ready, rows=P):
                pool.wait_ge(*ready)
                if r >= 2:
                    pool.wait_ge(s_rope, r - 1)
                nc.gpsimd.tensor_tensor(t1[0:rows, r % 2, 0:T], raw, table[0:rows, 0:T], ALU.mult).then_inc(s_t1, 1)

            def act_chunk(c):
                return (s_free["act"], chunks[c]["nth"] + 1)

            def clear_last(name):
                pool.wait_ge(s_col, norms[name]["id"] + 1)
                nc.gpsimd.memset(last_flat[:, 0:8 * P], 0.0).then_inc(s_clear, 1)

            def place(dst, first, stride, n, src):
                v = last_flat[:, first:first + n * stride].rearrange("p (c x) -> p c x", x=stride)[:, :, 0:16]
                a, b = dst
                return nc.gpsimd.tensor_copy(v[a:b], src[a:b])

            def add_squares(name, T):
                m = norms[name]
                sl = lambda i: sq[:, (m["sq"] + i) % SQ_SLOTS, 0:T]
                for i in range(1, m["adds"] + 1):
                    pool.wait_ge(s_sq, m["sq"] + i + 1)
                    if i > 1:
                        pool.wait_ge(s_add, m["add"] + i - 1)
                    nc.gpsimd.tensor_tensor(sl(i), sl(i - 1), sl(i), ALU.add).then_inc(s_add, 1)

            def glu_scale(i, j):
                r = rstd[:, norms[f"glu{i}{j}"]["id"] % 2, 0:T2]
                for n in range(KF):
                    g = 2 * KF + (2 * i + j) * KF + n
                    pool.wait_ge(s_silu, g + 1)
                    v = silu_buf(g)[:, 0:T2]
                    nc.gpsimd.tensor_tensor(v, v, r, ALU.mult).then_inc(s_silur, 1)

            nc.gpsimd.memset(x_hi[:, KD * T1:].bitcast(F32), 0.0).then_inc(s_pad, 1)
            nc.gpsimd.memset(x_lo[:, KD * T1:].bitcast(F32), 0.0).then_inc(s_pad, 1)
            add_squares("da", T1)
            pool.wait_ge(s_tab, 1)
            for j in range(16):
                cos_part(j, wide[:, j, :], cs_r[:, 0, :], T1, act_chunk(chunk_of("da_qkv", j)))
            clear_last("da")
            pool.wait_ge(s_clear, 1)
            pool.wait_ge(s_rope, 8)
            place((0, P), 0, P + 16, 8, qT[:, 0:8, 256:T1]).then_inc(s_last, 1)
            add_squares("conv0", T1)
            add_squares("dsa", T1)
            pool.wait_ge(s_tab, 2)
            for j in range(4):
                cos_part(ROPE_BASE["idx"] + j, wide[:, j, :], cs_r[:, 0, :], T1, act_chunk(chunk_of("dsa_in", j)))
            cos_part(ROPE_BASE["idx"] + 4, wide[0:64, 5, :], cos1, T1, (s_app, norms["ki"]["ap"] + 1), 64)
            pool.wait_ge(s_idxa, 24)
            for j in range(16):
                cos_part(ROPE_BASE["dsa"] + j, wide[:, 6 + j, :], cs_r[:, 0, :], T1, act_chunk(chunk_of("dsa_in", 20 + j)))
            clear_last("ki")
            nc.gpsimd.tensor_copy(ident8.rearrange("p (h c) -> p h c", c=16),
                                  ident[0:16, 0:16].rearrange("p (o c) -> p o c", o=1).to_broadcast([16, 8, 16]))\
                .then_inc(s_clear, 1)
            pool.wait_ge(s_clear, 3)
            pool.wait_ge(s_rope, ROPE_BASE["dsa"] + 8)
            for g in range(2):
                for a in (0, 64):
                    ins = place((a, a + 64), 4 * P * g + a // 4, P + 32, 4, qT[:, 4 * g:4 * g + 4, 256:T1])
            ins.then_inc(s_last, 1)
            add_squares("conv1", T1)
            add_squares("final", T1)
            add_squares("glu00", T2)
            for c in range(KD):
                pool.wait_ge(s_app, norms["final"]["ap"] + c + 1)
                nc.gpsimd.tensor_copy(h[:, c, 0:T2], wide[:, c, 0:T2]).then_inc(s_final, 1)
            glu_scale(0, 0)
            pool.wait_ge(s_even, 64)
            nc.gpsimd.affine_select(out=wsT, in_=wsT, compare_op=ALU.is_ge, fill=0.0, base=0,
                                    pattern=[[0, 8], [1, P]], channel_multiplier=-1).then_inc(s_ws, 1)
            for name in ("ev", "glu01", "pleh0", "pleo0", "glu10", "mla", "cq", "ckv"):
                add_squares(name, T2)
                if name == "ev":
                    pool.wait_ge(s_chunk, chunk_of("ev_in", 0) + 1)
                    nc.gpsimd.memset(part(6 * 1024, 4 * 1024), 0.0).then_inc(s_oper, 1)
                    gv, squares = part(14 * 1024, 1024), part(10 * 1024, 1024)
                    g64 = lambda z: z.rearrange("p (g d) -> p g d", d=64)
                    pool.wait_ge(*act_chunk(chunk_of("ev_in", 15)))
                    nc.gpsimd.tensor_tensor(squares, gv, gv, ALU.mult).then_inc(s_gsq, 1)
                    pool.wait_ge(s_vrs, 1)
                    nc.gpsimd.tensor_tensor(g64(gv), g64(gv),
                                            vms.rearrange("p (g o) -> p g o", o=1).to_broadcast([P, 16, 64]),
                                            ALU.mult).then_inc(s_gnorm, 1)
                    pool.wait_ge(s_gnorm, 1)
                    for t in range(2):
                        v = gv[:, t * 512:(t + 1) * 512]
                        ins = nc.gpsimd.tensor_tensor(v, v, vn, ALU.mult)
                    ins.then_inc(s_gv, 1)
                if name[:3] == "glu":
                    glu_scale(int(name[3]), int(name[4]))
            pool.wait_ge(s_sincos, 1)
            cos_part(ROPE_BASE["kr"], oT[:, 6, 0:T2], cs2[:, 0, :], T2, (s_kr, 1))
            for r in range(4):
                cos_part(ROPE_BASE["mq"] + r, wide[:, 14 + r, 0:T2], cs2[:, 0, :], T2,
                         act_chunk(chunk_of("mla_q", 3 * r + 2)))
            for name in ("glu11", "pleh1", "pleo1"):
                add_squares(name, T2)
                if name == "glu11":
                    glu_scale(1, 1)

        @block.vector
        def _(dve):
            V = nc.vector

            def step(ins):
                step.n += 1
                ins.then_inc(s_dve, 1)
                dve.wait_ge(s_dve, step.n)
            step.n = 0

            def norm_inv(name, T):
                m = norms[name]
                dve.wait_ge(s_std, m["id"] + 1)
                V.reciprocal(rstd[:, m["id"] % 2, 0:T], std[:, m["id"] % 2, 0:T]).then_inc(s_inv, 1)
                dve.wait_ge(s_inv, m["id"] + 1)

            def inverse(name, T):
                return rstd[:, norms[name]["id"] % 2, 0:T]

            def inverse_columns(name, tiles):
                m = norms[name]
                for t, (q0, n) in enumerate(tiles):
                    d = rstd[0:n, (m["id"] + 1) % 2, q0:q0 + n]
                    step(V.tensor_tensor(d, rstd[0:n, m["id"] % 2, q0:q0 + n], ident[0:n, 0:n], ALU.mult))
                    step(V.tensor_reduce(rcol[0:n, t:t + 1], d, AX.X, ALU.add))
                for t, (q0, n) in enumerate(tiles):
                    ins = V.tensor_scalar(rcol8[0:n, t:t + 1], rcol[0:n, t:t + 1], IDX_HEADS ** -0.5, None, ALU.mult)
                ins.then_inc(s_rcol, 1)

            def scaled_tables(name):
                V.tensor_tensor(cs_r[:, 0, :], cos1, inverse(name, T1), ALU.mult)
                V.tensor_tensor(cs_r[:, 1, :], sin1, inverse(name, T1), ALU.mult).then_inc(s_tab, 1)

            def scaled(name, c, dst, rows=P, last=True, ahead_too=True):
                if ahead_too:
                    ahead(c)
                dve.wait_ge(s_chunk, c + 1)
                m = norms[name]
                ins = V.tensor_tensor(dst, dense_bank(c)[0:rows, 0:dst.shape[-1]],
                                      rstd[0:rows, m["id"] % 2, 0:dst.shape[-1]], ALU.mult)
                if last:
                    ins.then_inc(s_free["dve"], 1)

            def low_gained(name, c, T, src=h):
                v, at = DEFERRED[name]
                dve.wait_ge(s_xhi, splits[name] + c + 1)
                o = slice(c * T1, c * T1 + T)
                V.scalar_tensor_tensor(out=x_lo[:, o], in0=src[:, c, 0:T], scalar=col(v, at + c),
                                       in1=x_hi[:, o].bitcast(F32), op0=ALU.mult, op1=ALU.subtract).then_inc(s_xlo, 1)

            def norm_apply(name, T, ops, shift=0):
                m = norms[name]
                for o, s, g, a, n in ops:
                    V.scalar_tensor_tensor(out=o, in0=s, scalar=g, in1=rstd[a:a + n, m["id"] % 2, shift:shift + T],
                                           op0=ALU.mult, op1=ALU.mult).then_inc(s_app, 1)

            def low(at, hi, lo, src):
                for i in range(len(src)):
                    dve.wait_ge(s_xhi, at + i + 1)
                    V.tensor_tensor(lo[i], src[i], hi[i].bitcast(F32), ALU.subtract).then_inc(s_xlo, 1)

            def norm_split(name, T, n, src, gain, at, first=0):
                m = norms[name]
                for c in range(n + 2):
                    if c < n:
                        norm_apply(name, T, [(sq[:, (m["sq"] + c) % SQ_SLOTS, 0:T], src[c], col(gain, at + c), 0, P)])
                    if c >= 2:
                        i = c - 2
                        o = slice((first + i) * T1, (first + i) * T1 + T)
                        low(splits[name] + i, [x_hi[:, o]], [x_lo[:, o]], [sq[:, (m["sq"] + i) % SQ_SLOTS, 0:T]])

            def norm_h(name, T, gain, at):
                norm_inv(name, T)
                norm_split(name, T, KD, [h[:, c, 0:T] for c in range(KD)], gain, at)

            def low_mix(name, T, a=0, b=KD):
                low(splits[name] + a, [mix_hi[:, c, 0:T] for c in range(a, b)], [mix_lo[:, c, 0:T] for c in range(a, b)],
                    [oT[:, c, 0:T] for c in range(a, b)])

            def ahead(c):
                weights_ahead(dve, rest_panel, c)

            def residual(stage, T, scale=None, then=None):
                for i in range(8):
                    c = chunk_of(stage, i)
                    ahead(c)
                    dve.wait_ge(s_chunk, c + 1)
                    src, dst = dense_bank(c)[:, 0:T], h[:, i, 0:T]
                    if scale is None:
                        ins = V.tensor_tensor(dst, src, dst, ALU.add)
                    else:
                        ins = V.scalar_tensor_tensor(out=dst, in0=src, scalar=scale, in1=dst, op0=ALU.mult,
                                                     op1=ALU.add)
                    ins.then_inc(s_free["dve"], 1)
                    if then and i:
                        low_gained(then, i - 1, T)
                if then:
                    low_gained(then, 7, T)

            def rope(r, out_, table, T, rows=P):
                dve.wait_ge(s_rot, r + 1)
                step(V.tensor_tensor(t2[0:rows, r % 2, 0:T], bank[0:rows, B_S + r % 2, 0:T], table[0:rows, 0:T],
                                     ALU.mult))
                dve.wait_ge(s_t1, r + 1)
                V.tensor_tensor(out_, t1[0:rows, r % 2, 0:T], t2[0:rows, r % 2, 0:T], ALU.add).then_inc(s_rope, 1)

            def attention(name, scale, mask):
                U = att[name]["units"]
                lag = 3 - len(U[0]["scores"])
                for i in range(len(U) + lag):
                    if i < len(U):
                        x = U[i]
                        q, k = x["qn"], x["kn"]
                        if name == "dsa" and x["group"] == 0:
                            dve.wait_ge(s_amcopy, 1)
                        for s in x["scores"]:
                            dve.wait_ge(s_score, s + 1)
                            if s >= 4:
                                dve.wait_ge(s_exp, s - 3)
                            V.tensor_tensor_reduce(sm[0:q, s % 4, 0:k], bank[0:q, S_BANKS[s % 4], 0:k],
                                                   tile_of(mask, x["t"])[0:q, :], -scale, 3e38, ALU.add, ALU.min,
                                                   nmx[0:q, s % 8:s % 8 + 1]).then_inc(s_dve if name == "mla" else
                                                                                       s_max, 1)
                            if name == "mla":
                                step.n += 1
                                dve.wait_ge(s_dve, step.n)
                                j, n = x["t"] * 8 + x["h"], nmx[0:q, s % 8:s % 8 + 1]
                                V.tensor_tensor(n, n, rq[0:q, j:j + 1], ALU.mult).then_inc(s_max, 1)
                    if i >= lag:
                        x = U[i - lag]
                        q, k, u = x["qn"], x["kn"], x["u"]
                        s = x["scores"]
                        dve.wait_ge(s_exp, s[-1] + 1)
                        if u >= 2:
                            dve.wait_ge(s_tr, u - 1)
                        a = s[0] % 8
                        step(V.reciprocal(rs[0:q, a:a + len(s)], ssum[0:q, a:a + len(s)]))
                        if len(s) == 1:
                            V.tensor_scalar(pn[0:q, u % 2, 0:k], pr[0:q, s[0] % 4, 0:k], rs[0:q, a:a + 1], None,
                                            ALU.mult).then_inc(s_prob, 1)
                        else:
                            p1 = pr[0:q, s[1] % 4, 0:k]
                            step(V.tensor_scalar(p1, p1, rs[0:q, a + 1:a + 2], lam[0:q], ALU.mult, ALU.mult))
                            V.scalar_tensor_tensor(out=pn[0:q, u % 2, 0:k], in0=pr[0:q, s[0] % 4, 0:k],
                                                   scalar=rs[0:q, a:a + 1], in1=p1, op0=ALU.mult,
                                                   op1=ALU.subtract).then_inc(s_prob, 1)

            V.memset(eps_col, EPS).then_inc(s_eps, 1)
            for i in range(2):
                for a in (0, 64):
                    V.memset(halves[a:a + 64, i:i + 1], float(a == 64 * i))
            dve.wait_ge(s_vec, 16)
            la = VEC_AT["lam"][0]
            V.tensor_tensor(lam_p[0:64, :], vec[0:64, la:la + 2], vec[0:64, la + 2:la + 4], ALU.mult)\
                .then_inc(s_lam, 1)
            V.tensor_scalar(subln8, col("subln"), 1.0 - LAMBDA_INIT, None, ALU.mult)
            lr = vec[:, VEC_AT["lb_raw"][0]:VEC_AT["lb_raw"][0] + 4]
            V.tensor_tensor(lb_t, lr, lr, ALU.subtract).then_inc(s_lbd, 1)
            rest_panel(dve, 0)
            for c in range(KD):
                low_gained("da", c, T1)
            rest_panel(dve, 1)

            def angles():
                dve.wait_ge(s_pos, 16)
                ang, kf = std[:, 1, 0:T2], rstd[:, 1, 0:T2]
                step(V.tensor_copy(ang, pos_sb[:, :]))
                step(V.tensor_scalar(ang, ang, con("inv"), None, ALU.mult))
                magic = float(1.5 * 2 ** 23)
                for r, shift in ((angle_cos, 0.25), (angle_sin, 0.0)):
                    step(V.tensor_scalar(kf, ang, 1.0 / TWO_PI, shift, ALU.mult, ALU.add))
                    step(V.tensor_scalar(kf, kf, magic, None, ALU.add))
                    step(V.tensor_scalar(kf, kf, -magic, -shift, ALU.add, ALU.add))
                    c1 = 6.28125
                    c2 = float(np.float32(np.round((TWO_PI - c1) * 2 ** 19) / 2 ** 19))
                    c3 = float(np.float32(TWO_PI - c1 - c2))
                    src = ang
                    for cc in (c1, c2, c3):
                        step(V.scalar_tensor_tensor(out=r, in0=kf, scalar=-cc, in1=src, op0=ALU.mult, op1=ALU.add))
                        src = r
                    V.tensor_scalar(r, r, float(np.float32(3.1415925)), -float(np.float32(3.1415925)),
                                    ALU.min, ALU.max).then_inc(s_ang, 1)

            for j in range(28):
                ahead(chunk_of("da_qkv", j))
                if j == 20:
                    angles()
                if j == 2:
                    norm_inv("da", T1)
                    dve.wait_ge(s_const, 16)
                    scaled_tables("da")
                    inverse_columns("da", TILES1)
                if j == 18:
                    dve.wait_ge(s_lbe, 1)
                    step(V.reciprocal(oml, lb))
                    step(V.tensor_tensor(lb_t, lb, oml, ALU.mult))
                    step(V.tensor_tensor(lb, lb_t, lb_t, ALU.subtract))
                    step(V.tensor_scalar(lb, lb, 0.0, 0.999, ALU.max, ALU.min))
                    step(V.tensor_scalar(oml, lb, -1.0, 1.0, ALU.mult, ALU.add))
                    dve.wait_ge(s_lame, 1)
                    step(V.tensor_tensor(lam, lam_e[:, 0:1], lam_e[:, 1:2], ALU.subtract))
                    step(V.tensor_scalar(lam, lam, LAMBDA_INIT, None, ALU.add))
                if 2 <= j < 18:
                    rope(j - 2, (qT if j < 10 else kT)[:, (j - 2) % 8, :], cs_r[:, 1, :], T1)
            attention("da", 64 ** -0.5, causal)
            for hh in range(9):
                if hh < 8:
                    norm_inv(f"o{hh}", T1)
                if hh >= 1:
                    o = oT[:, hh - 1, :]
                    norm_apply(f"o{hh - 1}", T1, [(o, o, subln8, 0, P)])
            low_mix("da_mix", T1)
            residual("da_out", T1)
            norm_h("conv0", T1, "ffn_norm", 0)

            def hid_split(g):
                return splits[f"hid{g // KF}"] + g % KF

            def low_hidden(g, T):
                j = g % KF
                low(hid_split(g), [hid_hi[:, j, 0:T]], [hid_lo[:, j, 0:T]], [hid_buf(g)[:, 0:T]])

            def conv_up(i):
                for j in range(KF + 1):
                    if j < KF:
                        for g in range(2):
                            c = chunk_of(f"conv{i}_up", 2 * j + g)
                            n = i * 2 * KF + 2 * j + g
                            ch = j + g * KF
                            cb, b = conv_buf(n), dense_bank(c)
                            ahead(c)
                            dve.wait_ge(s_conv, n + 1)
                            step(V.scalar_tensor_tensor(out=cb[:, 1:T1], in0=b[:, 0:T1 - 1],
                                                        scalar=col("conv_w", (i * 3 + 1) * 44 + ch),
                                                        in1=cb[:, 1:T1], op0=ALU.mult, op1=ALU.add))
                            V.scalar_tensor_tensor(out=cb[:, 2:T1], in0=b[:, 0:T1 - 2],
                                                   scalar=col("conv_w", (i * 3) * 44 + ch), in1=cb[:, 2:T1],
                                                   op0=ALU.mult, op1=ALU.add).then_inc(s_free["dve"], 1)
                    if j >= 1:
                        n = i * 2 * KF + 2 * (j - 1)
                        dve.wait_ge(s_silu, n // 2 + 1)
                        c = chunk_of(f"conv{i}_up", 2 * (j - 1) + 1)
                        dve.wait_ge(s_free["dve"], chunks[c]["nth"] + 1)
                        g = i * KF + j - 1
                        if g >= 2:
                            dve.wait_ge(s_xlo, hid_split(g - 2) + 1)
                        V.tensor_tensor(hid_buf(g), silu_buf(n // 2), conv_buf(n + 1), ALU.mult).then_inc(s_hid, 1)
                    if j >= 2:
                        low_hidden(i * KF + j - 2, T1)
                low_hidden(i * KF + KF - 1, T1)
            conv_up(0)
            residual("conv0_down", T1, then="dsa")
            work = sm

            def index_add(x):
                t, hh = divmod(x, 8)
                q0, q = TILES1[t]
                dve.wait_ge(s_relu, x + 1)
                rx, w = pr[0:q, x % 2, 0:q0 + q], wi_tok[0:q, t, hh:hh + 1]
                acc = work[0:q, t, 0:q0 + q]
                if hh == 0:
                    ins = V.tensor_scalar(acc, rx, w, None, ALU.mult)
                else:
                    ins = V.scalar_tensor_tensor(out=acc, in0=rx, scalar=w, in1=acc, op0=ALU.mult, op1=ALU.add)
                ins.then_inc(s_idxa, 1)
                dve.wait_ge(s_idxa, x + 1)

            def top_eight(r):
                t, i = divmod(r, TOPK // 8)
                q0, q = TILES1[t]
                a, b = [work[0:q, y, 0:q0 + q] for y in ((t, 3) if i % 2 == 0 else (3, t))]
                if i == 0:
                    step(V.tensor_tensor(a, a, tile_of(keep, t)[0:q, :], ALU.mult))
                    step(V.tensor_tensor(a, a, tile_of(addm, t)[0:q, :], ALU.add))
                step(V.max(max8[0:q], a))
                step(V.match_replace(b, max8[0:q], a, -3e38))
                if i == TOPK // 8 - 1:
                    step(V.tensor_scalar(a, b, -2e38, NEG, ALU.is_gt, ALU.mult))
                    ins = V.tensor_tensor(tile_of(amask, t)[0:q, :], a, tile_of(causal, t)[0:q, :], ALU.add)
                    if t == 2:
                        ins.then_inc(s_amask, 1)
                    else:
                        step(ins)

            for j in range(36):
                if j != 4:
                    ahead(chunk_of("dsa_in", j))
                if j == 0:
                    norm_inv("dsa", T1)
                    scaled_tables("dsa")
                    inverse_columns("dsa", TILES1)
                if j == 4:
                    scaled("dsa", chunk_of("dsa_in", 4), wide[0:64, 4, :], 64)
                if 2 <= j < 6:
                    rope(ROPE_BASE["idx"] + j - 2, qT[:, 8 + j - 2, :], cs_r[:, 1, :], T1)
                if j == 6:
                    norm_inv("ki", T1)
                    norm_apply("ki", T1, [(wide[0:64, 5, :], wide[0:64, 4, :], col("idxk", 0, 0, 64), 0, 64)])
                if j == 7:
                    rope(ROPE_BASE["idx"] + 4, kT[0:64, 8, :], sin1, T1, 64)
                    dve.wait_ge(s_free["act"], chunks[chunk_of("dsa_in", 7)]["nth"] + 1)
                if 8 <= j < 20:
                    index_add(2 * (j - 8))
                    index_add(2 * (j - 8) + 1)
                if j == 20:
                    dve.wait_ge(s_idxc, 16)
                if j >= 20:
                    for r in range(3 * (j - 20) // 2, 3 * (j - 19) // 2):
                        top_eight(r)
                if j >= 22:
                    rope(ROPE_BASE["dsa"] + j - 22, (qT if j < 30 else kT)[:, (j - 22) % 8, :], cs_r[:, 1, :], T1)
            for i in (14, 15):
                rope(ROPE_BASE["dsa"] + i, kT[:, i % 8, :], cs_r[:, 1, :], T1)
            attention("dsa", 64 ** -0.5, amask)
            low_mix("dsa_mix", T1)
            residual("dsa_out", T1)
            norm_h("conv1", T1, "ffn_norm", 8)
            conv_up(1)
            residual("conv1_down", T1)
            norm_inv("final", T1)
            norm_apply("final", T2, [(wide[:, c, 0:T2], h[:, c, META:T1], col("final", c), 0, P) for c in range(KD)],
                       shift=META)

            def glu(i, j, then):
                name = f"glu{i}{j}"
                g0 = 2 * KF + (2 * i + j) * KF
                for n in range(KF + 2):
                    if n < KF:
                        c = chunk_of(f"{name}_up", 2 * n)
                        if n == 0:
                            ahead(c)
                            norm_inv(name, T2)
                            scaled(name, c, silu_buf(g0)[:, 0:T2], ahead_too=False)
                        else:
                            scaled(name, c, silu_buf(g0 + n)[:, 0:T2])
                    if 1 <= n <= KF:
                        g = g0 + n - 1
                        c = chunk_of(f"{name}_up", 2 * n - 1)
                        dve.wait_ge(s_silur, g - 2 * KF + 1)
                        dve.wait_ge(s_chunk, c + 1)
                        dve.wait_ge(s_xlo, hid_split(g - 2) + 1)
                        V.tensor_tensor(hid_buf(g)[:, 0:T2], dense_bank(c)[:, 0:T2], silu_buf(g)[:, 0:T2], ALU.mult)\
                            .then_inc(s_hid, 1)
                    if n >= 2:
                        low_hidden(g0 + n - 2, T2)
                if (i, j) == (0, 0):
                    dve.wait_ge(s_final, 8)
                residual(f"{name}_down", T2, 0.5, then)

            def ple(i):
                dve.wait_ge(s_ple, 16 * (i + 1))
                low(splits[f"ple{i}"], [ple_hi[:, c, 0:T2] for c in range(2)], [ple_lo[:, c, 0:T2] for c in range(2)],
                    [oT[:, c, 0:T2] for c in range(2)])
                ahead(chunk_of(f"ple{i}_gate", 0))
                norm_inv(f"pleh{i}", T2)
                for c in range(KD):
                    scaled(f"pleh{i}", chunk_of(f"ple{i}_gate", c), wide[:, c, 0:T2], ahead_too=c > 0)
                for c in range(KD):
                    cc = chunk_of(f"ple{i}_proj", c)
                    dve.wait_ge(s_chunk, cc + 1)
                    dve.wait_ge(s_sig, 8 * i + c + 1)
                    V.tensor_tensor(wide[:, 8 + c, 0:T2], dense_bank(cc)[:, 0:T2], wide[:, c, 0:T2], ALU.mult)\
                        .then_inc(s_free["dve"], 1)
                for c in range(KD):
                    ahead(chunk_of(f"ple{i}_proj", c))
                norm_inv(f"pleo{i}", T2)
                for c in range(KD + 1):
                    if c < KD:
                        norm_apply(f"pleo{i}", T2, [(wide[:, c, 0:T2], wide[:, 8 + c, 0:T2],
                                                     col("gains", 8 * (5 * i + 4) + c), 0, P)])
                    if c >= 1:
                        dve.wait_ge(s_app, norms[f"pleo{i}"]["ap"] + c)
                        V.tensor_tensor(h[:, c - 1, 0:T2], wide[:, c - 1, 0:T2], h[:, c - 1, 0:T2], ALU.add)\
                            .then_inc(s_final, 1)
                    if c >= 2 and i == 0:
                        low_gained("glu10", c - 2, T2)
                if i == 0:
                    low_gained("glu10", 7, T2)

            for c in range(KD):
                low_gained("glu00", c, T2, wide)
            glu(0, 0, "ev")
            slot = lambda i: part(i * 1024, 1024)
            place = {0: 1, 4: 0, 16: 12, 20: 13}

            def ev_ahead(a, b):
                for c in range(a, b):
                    ahead(chunk_of("ev_in", c))
                    if c == 0:
                        norm_inv("ev", T2)
                    if c == 5:
                        inverse_columns("ev", TILES2)
                    if c - c % 4 in place:
                        scaled("ev", chunk_of("ev_in", c), slot(place[c - c % 4])[:, c % 4 * T2:(c % 4 + 1) * T2],
                               ahead_too=False)
            ev_ahead(0, 6)
            dve.wait_ge(s_evact, 4)
            sig, kf_ = slot(1), slot(3)
            for hh in range(4):
                ps_ = slice(hh * T2, (hh + 1) * T2)
                ins = V.tensor_scalar(sig[:, ps_], sig[:, ps_], oml[:, hh:hh + 1], lb[:, hh:hh + 1], ALU.mult, ALU.add)
            step(ins)
            V.tensor_scalar(kf_, sig, 1e-6, None, ALU.max).then_inc(s_f, 1)
            dve.wait_ge(s_f, 1)
            V.tensor_scalar(sig, sig, -1.0, 1.0, ALU.mult, ALU.add).then_inc(s_lvq, 1)
            dve.wait_ge(s_lvq, 1)
            ev_ahead(6, 12)
            dve.wait_ge(s_ln, 1)
            a, b = 2, 3
            c64 = lambda i: slot(i).rearrange("p (n c) -> p n c", c=CHUNK)
            for s in (1, 2, 4, 8, 16, 32):
                V.tensor_copy(c64(b)[:, :, 0:s], c64(a)[:, :, 0:s])
                step(V.tensor_tensor(c64(b)[:, :, s:CHUNK], c64(a)[:, :, s:CHUNK], c64(a)[:, :, 0:CHUNK - s],
                                     ALU.add))
                a, b = b, a
            assert a == 2
            ev_ahead(12, 16)
            scT = part(10 * 1024, 1024, 512)
            tmp = pT[:, :, :].rearrange("p a b -> p (a b)")[:, 0:512]
            dve.wait_ge(s_even, 64)

            def add_level(lv):
                for t in range(2):
                    dve.wait_ge(s_lvm, 2 * lv + t + 1)
                    v3 = lambda z: z.rearrange("p (h t) -> p h t", h=4)
                    mk = lmask[:, lv:lv + 1, :].to_broadcast([P, 4, P])
                    b = bank[:, LEVEL_BANKS[lv % 2][t], :]
                    if lv == 0:
                        V.tensor_tensor(v3(scT[:, t, :]), v3(b), mk, ALU.mult).then_inc(s_lva, 1)
                    else:
                        V.copy_predicated(v3(scT[:, t, :]), mk.bitcast(U32), v3(b))\
                            .then_inc(s_lva, 1)
                    dve.wait_ge(s_lva, 2 * lv + t + 1)

            def exponents(lv):
                m = LEVELS[lv - 1]
                v = lambda i: slot(i).rearrange("p (n s m) -> p n s m", s=2, m=m)
                e, bb = v(4 + lv % 2), v(2)
                nb = 512 // m
                ref = bb[:, :, 0, m - 1:m].to_broadcast([P, nb, m])
                V.tensor_tensor(e[:, :, 0, :], ref, bb[:, :, 0, :], ALU.subtract)
                V.tensor_tensor(e[:, :, 1, :], bb[:, :, 1, :], ref, ALU.subtract).then_inc(s_lvd, 1)

            def operands(lv):
                dve.wait_ge(s_lve, lv)
                if lv >= 3:
                    dve.wait_ge(s_lvm, 2 * (lv - 2) + 2)
                m = LEVELS[lv - 1]
                v = lambda i: slot(i).rearrange("p (n s m) -> p n s m", s=2, m=m)
                e = v(4 + lv % 2)
                V.tensor_tensor(v(6 + lv % 2)[:, :, 1, :], v(0)[:, :, 1, :], e[:, :, 1, :], ALU.mult)
                V.tensor_tensor(v(8 + lv % 2)[:, :, 0, :], v(1)[:, :, 0, :], e[:, :, 0, :], ALU.mult)\
                    .then_inc(s_lvq, 1)

            exponents(1)
            ev_ahead(16, 20)
            dve.wait_ge(s_gsq, 1)
            step(V.tensor_reduce(vms, slot(10).rearrange("p (g d) -> p g d", d=64), AX.X, ALU.add))
            step(V.tensor_scalar(vms, vms, 1.0 / 64, EPS, ALU.mult, ALU.add))
            V.reciprocal(vms, vms).then_inc(s_vms, 1)
            dve.wait_ge(s_vms, 1)
            ev_ahead(20, 24)
            dve.wait_ge(s_oper, 1)
            for lv in range(1, 7):
                if lv < 6:
                    exponents(lv + 1)
                operands(lv)
                add_level(lv - 1)
            c5_, b5 = c64(5), c64(2)
            V.tensor_tensor(c5_, b5[:, :, CHUNK - 1:CHUNK].to_broadcast([P, 16, CHUNK]), b5, ALU.subtract)\
                .then_inc(s_lvd, 1)
            add_level(6)
            dve.wait_ge(s_lve, 7)
            V.tensor_tensor(slot(6), slot(0), slot(4), ALU.mult)
            V.tensor_tensor(slot(7), slot(1), slot(5), ALU.mult).then_inc(s_gate, 1)
            gu = slot(12).rearrange("p (c t) -> p c t", c=4)
            dve.wait_ge(s_evact, 8)
            for t in range(2):
                dve.wait_ge(s_mixp, t + 1)
                v3 = lambda z: z.rearrange("p (h t) -> p h t", h=4)
                step(V.tensor_tensor(v3(tmp), v3(bank[:, B_COL + t, :]), bs, ALU.add))
                V.tensor_tensor(oT[:, 0:4, t * P:(t + 1) * P], v3(tmp), gu[:, :, t * P:(t + 1) * P], ALU.mult)\
                    .then_inc(s_mix, 1)
                dve.wait_ge(s_mix, t + 1)
            states = part(8 * 1024, 1536, 512)
            el = e_last.rearrange("p (h n) -> p h n", h=4)
            for n in range(3):
                dve.wait_ge(s_upd, n + 1)
                v3 = lambda z: z.rearrange("p (h t) -> p h t", h=4)
                if n == 0:
                    V.tensor_copy(states[:, 0, :], bank[:, B_S, :]).then_inc(s_st, 1)
                else:
                    step(V.tensor_tensor(v3(tmp), v3(states[:, n - 1, :]), el[:, :, n:n + 1].to_broadcast([P, 4, P]),
                                         ALU.mult))
                    V.tensor_tensor(states[:, n, :], bank[:, B_S + n % 2, :], tmp, ALU.add).then_inc(s_st, 1)
                dve.wait_ge(s_st, n + 1)
            dve.wait_ge(s_evact, 12)
            low_mix("ev_mix", T2, 0, 3)
            for hh in range(5):
                if hh < 4:
                    norm_inv(f"hg{hh}", T2)
                if hh >= 1:
                    i = hh - 1
                    o = slot(3)[:, i * T2:(i + 1) * T2]
                    norm_apply(f"hg{i}", T2, [(o, o, col("hg_out"), 0, P)])
                    dve.wait_ge(s_app, norms[f"hg{i}"]["ap"] + 1)
                    V.tensor_tensor(oT[:, 4 + i, 0:T2], o, slot(13)[:, i * T2:(i + 1) * T2], ALU.mult)\
                        .then_inc(s_gate, 1)
            low_mix("ev_mix", T2, 3, 8)
            residual("ev_out", T2, then="glu01")
            glu(0, 1, "pleh0")
            ple(0)
            glu(1, 0, "mla")
            ahead(chunk_of("mla_in", 0))
            norm_inv("mla", T2)
            for c in range(5):
                scaled("mla", chunk_of("mla_in", c), wide[:, c, 0:T2], ahead_too=c > 0)
            scaled("mla", chunk_of("mla_in", 5), wide[64:128, 5, 0:T2], 64, last=False)
            scaled("mla", chunk_of("mla_in", 5), wide[0:64, 5, 0:T2], 64, ahead_too=False)
            norm_inv("cq", T2)
            norm_inv("ckv", T2)
            norm_split("cq", T2, 3, [wide[:, c, 0:T2] for c in range(3)], "qa", 0)
            norm_split("ckv", T2, 2, [wide[:, 3 + c, 0:T2] for c in range(2)], "kva", 0, first=3)
            for c in range(12):
                ahead(chunk_of("mla_q", c))
            for c in range(12):
                ahead(chunk_of("mla_kv", c))
            f0 = chunks[chunk_of("mla_in", 0)]["nth"]
            dve.wait_ge(s_free["dve"], f0 + 6)
            V.tensor_scalar(oT[:, 6, 0:T2], wide[:, 5, 0:T2], col("kr"), None, ALU.mult).then_inc(s_kr, 1)
            dve.wait_ge(s_sincos, 1)
            rope(ROPE_BASE["kr"], oT[:, 7, 0:T2], cs2[:, 1, :], T2)
            dve.wait_ge(s_rope, ROPE_BASE["kr"] + 1)
            heads = []
            for hh in range(8):
                a = 64 * (hh % 2)
                heads.append((f"k{hh}", [(kT[:, hh, 0:T2], kT[:, hh, 0:T2], col("kn"), 0, P),
                                         (kT[a:a + 64, 8 + hh // 2, 0:T2], oT[a:a + 64, 7, 0:T2],
                                          1.0, a, 64)]))
            dve.wait_ge(s_qstd, 1)
            step(V.reciprocal(rq, rq))
            step(V.tensor_scalar(nrq, rq, -1.0, None, ALU.mult))
            for r in range(4):
                rope(ROPE_BASE["mq"] + r, qT[:, 8 + r, 0:T2], cs2[:, 1, :], T2)
            for i in range(9):
                if i < 8:
                    norm_inv(heads[i][0], T2)
                if i >= 1:
                    norm_apply(heads[i - 1][0], T2, heads[i - 1][1])
            attention("mla", 192 ** -0.5, causal)
            low_mix("mla_mix", T2)
            residual("mla_out", T2, then="glu11")
            glu(1, 1, "pleh1")
            ple(1)


WEIGHTS = [("da_w_qkv", "da_w_qkv"), ("da_w_o", "da_w_o"), ("dsa_w_in", "dsa_w_in"), ("dsa_w_o", "dsa_w_o"),
           ("ffn_w_up", "ffn_w_up"), ("ffn_w_down", "ffn_w_down"), ("ffn_w_gate", "ffn_w_gate_2"),
           ("ffn_w_up_2", "ffn_w_up_2"), ("ffn_w_down_2", "ffn_w_down_2"), ("ple_w_gate", "ple_w_gate_2"),
           ("ple_w_proj", "ple_w_proj_2"), ("even_w_in", "even_w_in_2"), ("even_w_out", "even_w_out_2"),
           ("mla_w_in", "mla_w_in_2"), ("mla_w_q_b", "mla_w_q_b_2"), ("mla_w_kv_b", "mla_w_kv_b_2"),
           ("mla_w_out", "mla_w_out_2")]


def kernel(**inputs):
    import concourse.bacc as bacc
    from concourse.bass_utils import run_bass_kernel_spmd

    a = {k: np.asarray(v) for k, v in inputs.items()}

    def cols(v):
        return v.reshape(-1, P).T

    def twice(v):
        return np.concatenate([v, v]).reshape(P, 1)

    sc = shape_constants()
    z = np.zeros((64,), np.float32)
    pad = lambda v: np.concatenate([v.reshape(-1), z]).reshape(P, 1)
    v = {
        "da_norm": cols(a["da_norm"]), "subln": cols(a["da_subln"]), "dsa_norm": cols(a["dsa_norm"]),
        "idxk": pad(a["dsa_idx_k_norm"]), "ffn_norm": cols(a["ffn_norm"]), "conv_w": cols(a["ffn_conv_w"]),
        "conv_b": cols(a["ffn_conv_b"]), "final": cols(a["final_norm"]), "gains": cols(a["norm_gains_2"]),
        "lb_raw": cols(a["hgrn_lb_raw_2"]), "hg_out": cols(a["hgrn_out_norm_2"]), "qa": cols(a["mla_q_a_norm_2"]),
        "kva": cols(a["mla_kv_a_norm_2"]), "qn": cols(a["mla_q_norm_2"][0, 0:P]), "qr": twice(a["mla_q_norm_2"][0, P:]),
        "kn": cols(a["mla_k_norm_2"][0, 0:P]), "kr": twice(a["mla_k_norm_2"][0, P:]),
        "lam": np.concatenate([pad(a[f"da_lambda_{n}"][0]) for n in ("q1", "q2", "k1", "k2")], 1),
    }
    bs = a["gmlp_b_s_2"][0].reshape(4, 2, 1, P)
    e = {
        "lmask": level_masks(),
        "wsT": a["gmlp_w_s_2"][0].transpose(2, 0, 1).reshape(P, -1),
        "bs": np.broadcast_to(bs, (4, 2, 64, P)).transpose(1, 2, 0, 3).reshape(P, -1),
        "vnorm": np.broadcast_to(a["gmlp_v_norm_2"][0].reshape(1, -1), (P, 512)),
    }
    arrays = {
        "hT": np.concatenate([a["meta_tokens"], a["x"][0]], 0).T,
        "consts": np.concatenate([sc[n] for n, _ in CONST_PARTS], 1),
        "idxc": index_constants(),
        "vecs": np.concatenate([v[n] for n, _ in VEC_PARTS], 1),
        "evenc": np.concatenate([e[n] for n, _ in EVEN_PARTS], 1),
        "pleT": a["p_2"][:, 0].transpose(0, 2, 1),
        "pos": np.broadcast_to(a["positions_2"].reshape(1, -1), (P, T2)),
    }
    for name, src in WEIGHTS:
        arrays["w_" + name] = a[src]
    arrays = {k: np.ascontiguousarray(x) for k, x in arrays.items()}

    nc = bacc.Bacc("TRN2", target_bir_lowering=False, num_devices=1)
    ap = {k: nc.dram_tensor(k, x.shape, mybir.dt.from_np(x.dtype), kind="ExternalInput").ap()
          for k, x in arrays.items()}
    out = nc.dram_tensor("outT", (D, T2), F32, kind="ExternalOutput").ap()
    build(nc, {n: ap["w_" + n] for n, _ in WEIGHTS}, ap["hT"], ap["consts"], ap["idxc"], ap["vecs"], ap["evenc"],
          ap["pleT"], ap["pos"], out)
    r = run_bass_kernel_spmd(nc, [arrays], core_ids=[0])
    return r.results[0]["outT"].T[None].copy()
```
